# Optimizing a Trainium2 kernel written in Bass

```python
import jax, jax.numpy as jnp
from jax import lax
import numpy as np

D_MODEL = 1024
BATCH = 1
SEQ = 512
DEPTH = 1

HEAD_DIM = 64
FOX_HEADS = 8
SB_HEADS = 4
POOL_GROUPS = 4
POOL_WINDOWS = (2, 4, 8, 16)
POOL_GROUP_DIM = 64
FOX_W = FOX_HEADS * HEAD_DIM
SB_W = SB_HEADS * HEAD_DIM
POOL_W = POOL_GROUPS * POOL_GROUP_DIM
D_MIX = FOX_W + POOL_W + SB_W
Q_BLOCK = 128
EPS = 1e-6
NEG = -1e30

IN_SPLITS = (
    FOX_W, FOX_W, FOX_W, FOX_W,
    FOX_HEADS,
    POOL_W, POOL_W,
    SB_W, SB_W, SB_W, SB_W,
)
D_IN = sum(IN_SPLITS)


def rms_norm(x, g):
    xf = x.astype(jnp.float32)
    y = xf * lax.rsqrt(jnp.mean(xf * xf, axis=-1, keepdims=True) + EPS)
    return (y * g.astype(jnp.float32)).astype(x.dtype)

def to_heads(t, n_heads):
    b, s, _ = t.shape
    return t.reshape(b, s, n_heads, HEAD_DIM).transpose(0, 2, 1, 3)

def from_heads(t):
    b, h, s, d = t.shape
    return t.transpose(0, 2, 1, 3).reshape(b, s, h * d)

def split_blocks(t):
    b, h, s = t.shape[:3]
    nb = s // Q_BLOCK
    t = t.reshape((b, h, nb, Q_BLOCK) + t.shape[3:])
    return jnp.moveaxis(t, 2, 0)

def merge_blocks(o):
    nb, b, h, qb, d = o.shape
    return jnp.moveaxis(o, 0, 2).reshape(b, h, nb * qb, d)

def forgetting_attention(q, k, v, log_f):
    s_len, d = q.shape[2], q.shape[3]
    c = jnp.cumsum(log_f, axis=-1)
    kpos = jnp.arange(s_len)
    scale = d ** -0.5

    def one_block(args):
        qi, ci, i = args
        qpos = i * Q_BLOCK + jnp.arange(Q_BLOCK)
        sc = jnp.einsum('bhqd,bhkd->bhqk', qi, k).astype(jnp.float32) * scale
        sc = sc + (ci[..., :, None] - c[..., None, :])
        sc = jnp.where(kpos[None, :] <= qpos[:, None], sc, NEG)
        p = jax.nn.softmax(sc, axis=-1)
        return jnp.einsum('bhqk,bhkd->bhqd', p.astype(v.dtype), v)

    nb = s_len // Q_BLOCK
    o = lax.map(one_block, (split_blocks(q), split_blocks(c), jnp.arange(nb)))
    return merge_blocks(o)

def stick_breaking_attention(q, k, v):
    s_len, d = q.shape[2], q.shape[3]
    kpos = jnp.arange(s_len)
    scale = d ** -0.5

    def one_block(args):
        qi, i = args
        qpos = i * Q_BLOCK + jnp.arange(Q_BLOCK)
        z = jnp.einsum('bhqd,bhkd->bhqk', qi, k).astype(jnp.float32) * scale
        causal = kpos[None, :] < qpos[:, None]
        log_1m_beta = jnp.where(causal, -jax.nn.softplus(z), 0.0)
        rest = lax.cumsum(log_1m_beta, axis=3, reverse=True) - log_1m_beta
        a = jnp.where(causal, jnp.exp(jax.nn.log_sigmoid(z) + rest), 0.0)
        return jnp.einsum('bhqk,bhkd->bhqd', a.astype(v.dtype), v)

    nb = s_len // Q_BLOCK
    o = lax.map(one_block, (split_blocks(q), jnp.arange(nb)))
    return merge_blocks(o)

def causal_window_mean(x, w):
    s_len = x.shape[1]
    xf = x.astype(jnp.float32)
    cs = jnp.cumsum(xf, axis=1)
    cs_prev = jnp.pad(cs, ((0, 0), (w, 0), (0, 0)))[:, :s_len]
    count = jnp.minimum(jnp.arange(s_len) + 1, w).astype(jnp.float32)
    return ((cs - cs_prev) / count[None, :, None]).astype(x.dtype)

def multiscale_pool(x, w_pool, scale):
    b, s_len, _ = x.shape
    groups = jnp.split(x, POOL_GROUPS, axis=-1)
    pooled = jnp.stack([causal_window_mean(g, w) - g for g, w in zip(groups, POOL_WINDOWS)], axis=2)
    y = jnp.einsum('bsgc,gcd->bsgd', pooled, w_pool).reshape(b, s_len, POOL_W)
    return y * scale

def hybrid_layer(x, norm_g, w_in, b_f, q_norm_g, k_norm_g, w_pool, pool_scale, w_out):
    h = rms_norm(x, norm_g)
    proj = jnp.einsum('bsd,de->bse', h, w_in)
    idx = np.cumsum(IN_SPLITS)[:-1].tolist()
    (fq, fk, fv, fg, ff, px, pg, sq, sk, sv, sg) = jnp.split(proj, idx, axis=-1)

    fq = rms_norm(to_heads(fq, FOX_HEADS), q_norm_g)
    fk = rms_norm(to_heads(fk, FOX_HEADS), k_norm_g)
    fv = to_heads(fv, FOX_HEADS)
    log_f = jax.nn.log_sigmoid((ff + b_f).astype(jnp.float32)).transpose(0, 2, 1)
    fox_out = from_heads(forgetting_attention(fq, fk, fv, log_f)) * jax.nn.silu(fg)

    pool_out = multiscale_pool(px, w_pool, pool_scale) * jax.nn.silu(pg)

    sb = stick_breaking_attention(to_heads(sq, SB_HEADS), to_heads(sk, SB_HEADS), to_heads(sv, SB_HEADS))
    sb_out = from_heads(sb) * jax.nn.silu(sg)

    mixed = jnp.concatenate([fox_out, pool_out, sb_out], axis=-1)
    return x + jnp.einsum('bse,ed->bsd', mixed, w_out)

def first_inputs(seed: int = 0) -> dict:
    key = jax.random.key(seed)
    ks = jax.random.split(key, 10)
    x = jax.random.normal(ks[0], (BATCH, SEQ, D_MODEL), jnp.float32)
    norm_g = 1.0 + 0.02 * jax.random.normal(ks[1], (DEPTH, D_MODEL), jnp.float32)
    w_in = jax.random.normal(ks[2], (DEPTH, D_MODEL, D_IN), jnp.float32) * D_MODEL ** -0.5
    b_f = jax.random.uniform(ks[3], (DEPTH, FOX_HEADS), jnp.float32, 1.0, 4.0)
    q_norm_g = 1.0 + 0.02 * jax.random.normal(ks[4], (DEPTH, HEAD_DIM), jnp.float32)
    k_norm_g = 1.0 + 0.02 * jax.random.normal(ks[5], (DEPTH, HEAD_DIM), jnp.float32)
    w_pool = jax.random.normal(ks[6], (DEPTH, POOL_GROUPS, POOL_GROUP_DIM, POOL_GROUP_DIM), jnp.float32) * POOL_GROUP_DIM ** -0.5
    pool_scale = 1.0 + 0.02 * jax.random.normal(ks[7], (DEPTH, POOL_W), jnp.float32)
    w_out = jax.random.normal(ks[8], (DEPTH, D_MIX, D_MODEL), jnp.float32) * D_MIX ** -0.5
    return {"x": x, "norm_g": norm_g, "w_in": w_in, "b_f": b_f, "q_norm_g": q_norm_g,
            "k_norm_g": k_norm_g, "w_pool": w_pool, "pool_scale": pool_scale, "w_out": w_out}

def first_block(x, norm_g, w_in, b_f, q_norm_g, k_norm_g, w_pool, pool_scale, w_out):
    for l in range(DEPTH):
        x = hybrid_layer(x, norm_g[l], w_in[l], b_f[l], q_norm_g[l], k_norm_g[l],
                         w_pool[l], pool_scale[l], w_out[l])
    return x


DEPTH_2 = 2

N_A_LAYERS = DEPTH_2 // 2
N_B_LAYERS = DEPTH_2 - N_A_LAYERS
M_HEADS = 4
M_DV = D_MODEL // M_HEADS
M_DK = M_DV // 2
M_CHUNK = 64
GATE_CAP = 15.0
M_QK_W = M_HEADS * M_DK
M_V_W = M_HEADS * M_DV
M_IN_COLS = 2 * M_QK_W + 2 * M_V_W + 2 * M_HEADS
M_SPLITS = [M_QK_W, 2 * M_QK_W, 2 * M_QK_W + M_V_W, 2 * M_QK_W + 2 * M_V_W, 2 * M_QK_W + 2 * M_V_W + M_HEADS]
A_HEAD_DIM = 64
A_Q_HEADS = D_MODEL // A_HEAD_DIM
A_KV_HEADS = 4
A_GROUP = A_Q_HEADS // A_KV_HEADS
WINDOW = 128
ROPE_DIM = A_HEAD_DIM // 4
ROPE_THETA = 500000.0
D_FF = 4 * D_MODEL
PLE_DIM = 256
LN_EPS = 1e-5
DEEPNORM_ALPHA = (2 * DEPTH_2) ** 0.25
DEEPNORM_BETA = (8 * DEPTH_2) ** -0.25


def layer_norm(x, g, b):
    xf = x.astype(jnp.float32)
    mu = jnp.mean(xf, axis=-1, keepdims=True)
    var = jnp.mean(jnp.square(xf - mu), axis=-1, keepdims=True)
    return ((xf - mu) * lax.rsqrt(var + LN_EPS) * g + b).astype(x.dtype)

def partial_rope(t, pos):
    half = ROPE_DIM // 2
    inv_freq = jnp.power(ROPE_THETA, -jnp.arange(half, dtype=jnp.float32) * (2.0 / ROPE_DIM))
    ang = pos.astype(jnp.float32)[..., None] * inv_freq
    cos = jnp.cos(ang)[:, :, None, :]
    sin = jnp.sin(ang)[:, :, None, :]
    tr = t[..., :ROPE_DIM].astype(jnp.float32)
    t1, t2 = tr[..., :half], tr[..., half:]
    rot = jnp.concatenate([t1 * cos - t2 * sin, t2 * cos + t1 * sin], axis=-1).astype(t.dtype)
    return jnp.concatenate([rot, t[..., ROPE_DIM:]], axis=-1)

def soft_cap(g):
    return GATE_CAP * jnp.tanh(g / GATE_CAP)

def to_chunks(t, nc):
    t = t.reshape(t.shape[0], nc, M_CHUNK, *t.shape[2:])
    return jnp.moveaxis(t, (1, 3), (0, 2))

def mlstm_chunkwise(q, k, v, ig, lf):
    B, S, H, DK = q.shape
    DV = v.shape[-1]
    nc = S // M_CHUNK
    xs = tuple(to_chunks(t, nc) for t in (q, k, v, ig, lf))
    causal = jnp.tril(jnp.ones((M_CHUNK, M_CHUNK), dtype=bool))
    init = (jnp.zeros((B, H, DK, DV), jnp.float32),
            jnp.zeros((B, H, DK), jnp.float32),
            jnp.zeros((B, H), jnp.float32))

    def step(carry, chunk):
        C, n, m = carry
        qc, kc, vc, igc, lfc = chunk
        b = jnp.cumsum(lfc, axis=-1)
        log_d = b[..., :, None] - b[..., None, :] + igc[..., None, :]
        log_d = jnp.where(causal, log_d, -jnp.inf)
        log_inter = b + m[..., None]
        m_t = jnp.maximum(jnp.max(log_d, axis=-1), log_inter)
        d = jnp.exp(log_d - m_t[..., None])
        inter = jnp.exp(log_inter - m_t)
        s = jnp.einsum('bhtk,bhsk->bhts', qc, kc) * d
        num = jnp.einsum('bhts,bhsv->bhtv', s, vc) + inter[..., None] * jnp.einsum('bhtk,bhkv->bhtv', qc, C)
        den = jnp.sum(s, axis=-1) + inter * jnp.einsum('bhtk,bhk->bht', qc, n)
        h = num / jnp.maximum(jnp.abs(den), jnp.exp(-m_t))[..., None]
        b_last = b[..., -1]
        a = b_last[..., None] - b + igc
        m_new = jnp.maximum(b_last + m, jnp.max(a, axis=-1))
        w = jnp.exp(a - m_new[..., None])
        decay = jnp.exp(b_last + m - m_new)
        C_new = decay[..., None, None] * C + jnp.einsum('bhs,bhsk,bhsv->bhkv', w, kc, vc)
        n_new = decay[..., None] * n + jnp.einsum('bhs,bhsk->bhk', w, kc)
        return (C_new, n_new, m_new), h

    _, h = lax.scan(step, init, xs)
    return jnp.moveaxis(h, (0, 2), (1, 3)).reshape(B, S, H, DV)

def mlstm_mixer(x, w_in, b_ig, b_fg, head_g, w_out):
    B, S, _ = x.shape
    proj = x @ w_in
    q, k, v, o, ig, fg = jnp.split(proj, M_SPLITS, axis=-1)
    q = q.reshape(B, S, M_HEADS, M_DK).astype(jnp.float32) * (M_DK ** -0.5)
    k = k.reshape(B, S, M_HEADS, M_DK).astype(jnp.float32)
    v = v.reshape(B, S, M_HEADS, M_DV).astype(jnp.float32)
    log_i = soft_cap(ig.astype(jnp.float32) + b_ig)
    log_f = jax.nn.log_sigmoid(soft_cap(fg.astype(jnp.float32) + b_fg))
    h = mlstm_chunkwise(q, k, v, log_i, log_f)
    mu = jnp.mean(h, axis=-1, keepdims=True)
    var = jnp.mean(jnp.square(h - mu), axis=-1, keepdims=True)
    h = (h - mu) * lax.rsqrt(var + LN_EPS) * head_g.reshape(M_HEADS, M_DV)
    h = h.reshape(B, S, D_MODEL).astype(x.dtype)
    return (jax.nn.sigmoid(o) * h) @ w_out

def shared_kv(x, pos, kv_w, kv_b):
    B, S, _ = x.shape
    kv = x @ kv_w + kv_b
    k, v = jnp.split(kv, 2, axis=-1)
    k = partial_rope(k.reshape(B, S, A_KV_HEADS, A_HEAD_DIM), pos)
    v = v.reshape(B, S, A_KV_HEADS, A_HEAD_DIM)
    return k, v

def banded(t, nb):
    t = t.reshape(t.shape[0], nb, WINDOW, A_KV_HEADS, A_HEAD_DIM)
    prev = jnp.pad(t, ((0, 0), (1, 0), (0, 0), (0, 0), (0, 0)))[:, :-1]
    return jnp.concatenate([prev, t], axis=2)

def swa_sink_attention(x, pos, k_sh, v_sh, w_q, b_q, sinks, w_o, b_o):
    B, S, _ = x.shape
    nb = S // WINDOW
    q = partial_rope((x @ w_q + b_q).reshape(B, S, A_Q_HEADS, A_HEAD_DIM), pos)
    q = q.reshape(B, nb, WINDOW, A_KV_HEADS, A_GROUP, A_HEAD_DIM)
    kb, vb = banded(k_sh, nb), banded(v_sh, nb)
    scores = jnp.einsum('bnqkgd,bnskd->bnkgqs', q, kb).astype(jnp.float32) * (A_HEAD_DIM ** -0.5)
    qi = jnp.arange(WINDOW)[:, None]
    si = jnp.arange(2 * WINDOW)[None, :]
    diff = qi + WINDOW - si
    band = (diff >= 0) & (diff < WINDOW)
    blk = jnp.arange(nb)[:, None, None]
    valid = band[None] & (blk * WINDOW - WINDOW + si[None] >= 0)
    scores = jnp.where(valid[None, :, None, None], scores, -jnp.inf)
    sink = sinks.astype(jnp.float32).reshape(A_KV_HEADS, A_GROUP)[None, None, :, :, None]
    m = jnp.maximum(jnp.max(scores, axis=-1), sink)
    e = jnp.exp(scores - m[..., None])
    probs = e / (jnp.sum(e, axis=-1) + jnp.exp(sink - m))[..., None]
    out = jnp.einsum('bnkgqs,bnskd->bnqkgd', probs.astype(x.dtype), vb).reshape(B, S, D_MODEL)
    return out @ w_o + b_o

def squared_relu_mlp(x, w_up, w_down):
    return jnp.square(jax.nn.relu(x @ w_up)) @ w_down

def second_inputs(seed: int = 0) -> dict:
    key = jax.random.key(seed)
    ks = jax.random.split(key, 24)
    f32 = jnp.float32
    nrm = lambda k, shape, scale: jax.random.normal(k, shape, f32) * scale
    x = jax.random.normal(ks[0], (BATCH, SEQ, D_MODEL), f32)
    p = jax.random.normal(ks[1], (DEPTH_2, BATCH, SEQ, PLE_DIM), f32)
    start = jax.random.randint(ks[2], (BATCH, 1), 0, 1024, dtype=jnp.int32)
    positions = (start + jnp.arange(SEQ, dtype=jnp.int32)[None, :]).astype(jnp.int32)
    a_w_in = nrm(ks[3], (N_A_LAYERS, D_MODEL, M_IN_COLS), D_MODEL ** -0.5)
    a_b_igate = nrm(ks[4], (N_A_LAYERS, M_HEADS), 0.1)
    a_b_fgate = jnp.linspace(3.0, 6.0, M_HEADS, dtype=f32)[None, :] + nrm(ks[5], (N_A_LAYERS, M_HEADS), 0.1)
    a_head_norm_g = 1.0 + nrm(ks[6], (N_A_LAYERS, D_MODEL), 0.02)
    a_w_out = nrm(ks[7], (N_A_LAYERS, D_MODEL, D_MODEL), D_MODEL ** -0.5 * DEEPNORM_BETA)
    kv_w = nrm(ks[8], (D_MODEL, 2 * A_KV_HEADS * A_HEAD_DIM), D_MODEL ** -0.5)
    kv_b = nrm(ks[9], (2 * A_KV_HEADS * A_HEAD_DIM,), 0.02)
    b_w_q = nrm(ks[10], (N_B_LAYERS, D_MODEL, A_Q_HEADS * A_HEAD_DIM), D_MODEL ** -0.5)
    b_b_q = nrm(ks[11], (N_B_LAYERS, A_Q_HEADS * A_HEAD_DIM), 0.02)
    b_sinks = nrm(ks[12], (N_B_LAYERS, A_Q_HEADS), 0.5)
    b_w_o = nrm(ks[13], (N_B_LAYERS, A_Q_HEADS * A_HEAD_DIM, D_MODEL), D_MODEL ** -0.5 * DEEPNORM_BETA)
    b_b_o = nrm(ks[14], (N_B_LAYERS, D_MODEL), 0.02)
    mix_ln_g = 1.0 + nrm(ks[15], (DEPTH_2, D_MODEL), 0.02)
    mix_ln_b = nrm(ks[16], (DEPTH_2, D_MODEL), 0.02)
    mlp_w_up = nrm(ks[17], (DEPTH_2, D_MODEL, D_FF), D_MODEL ** -0.5)
    mlp_w_down = nrm(ks[18], (DEPTH_2, D_FF, D_MODEL), D_FF ** -0.5 * DEEPNORM_BETA)
    mlp_ln_g = 1.0 + nrm(ks[19], (DEPTH_2, D_MODEL), 0.02)
    mlp_ln_b = nrm(ks[20], (DEPTH_2, D_MODEL), 0.02)
    ple_w_gate = nrm(ks[21], (DEPTH_2, D_MODEL, D_MODEL), D_MODEL ** -0.5)
    ple_b_gate = nrm(ks[22], (DEPTH_2, D_MODEL), 0.02)
    ple_w_proj = nrm(ks[23], (DEPTH_2, PLE_DIM, D_MODEL), PLE_DIM ** -0.5 * DEEPNORM_BETA)
    return {"x": x, "p": p, "positions": positions,
            "a_w_in": a_w_in, "a_b_igate": a_b_igate, "a_b_fgate": a_b_fgate,
            "a_head_norm_g": a_head_norm_g, "a_w_out": a_w_out,
            "kv_w": kv_w, "kv_b": kv_b,
            "b_w_q": b_w_q, "b_b_q": b_b_q, "b_sinks": b_sinks, "b_w_o": b_w_o, "b_b_o": b_b_o,
            "mix_ln_g": mix_ln_g, "mix_ln_b": mix_ln_b,
            "mlp_w_up": mlp_w_up, "mlp_w_down": mlp_w_down, "mlp_ln_g": mlp_ln_g, "mlp_ln_b": mlp_ln_b,
            "ple_w_gate": ple_w_gate, "ple_b_gate": ple_b_gate, "ple_w_proj": ple_w_proj}

def second_block(x, p, positions, a_w_in, a_b_igate, a_b_fgate, a_head_norm_g, a_w_out,
              kv_w, kv_b, b_w_q, b_b_q, b_sinks, b_w_o, b_b_o,
              mix_ln_g, mix_ln_b, mlp_w_up, mlp_w_down, mlp_ln_g, mlp_ln_b,
              ple_w_gate, ple_b_gate, ple_w_proj):
    k_sh, v_sh = None, None
    for i in range(DEPTH_2):
        if i < N_A_LAYERS:
            mix = mlstm_mixer(x, a_w_in[i], a_b_igate[i], a_b_fgate[i], a_head_norm_g[i], a_w_out[i])
        else:
            if i == N_A_LAYERS:
                k_sh, v_sh = shared_kv(x, positions, kv_w, kv_b)
            j = i - N_A_LAYERS
            mix = swa_sink_attention(x, positions, k_sh, v_sh, b_w_q[j], b_b_q[j], b_sinks[j], b_w_o[j], b_b_o[j])
        x = layer_norm(DEEPNORM_ALPHA * x + mix, mix_ln_g[i], mix_ln_b[i])
        x = layer_norm(DEEPNORM_ALPHA * x + squared_relu_mlp(x, mlp_w_up[i], mlp_w_down[i]), mlp_ln_g[i], mlp_ln_b[i])
        x = x + jax.nn.sigmoid(x @ ple_w_gate[i] + ple_b_gate[i]) * (p[i] @ ple_w_proj[i])
    return x


def setup_inputs(seed=0):
    out = dict(first_inputs(seed))
    for name, value in second_inputs(seed + 1).items():
        if name != "x":
            out[name + "_2"] = value
    return out


def reference(
    x, norm_g, w_in, b_f, q_norm_g, k_norm_g, w_pool, pool_scale, w_out, p_2, positions_2,
    a_w_in_2, a_b_igate_2, a_b_fgate_2, a_head_norm_g_2, a_w_out_2, kv_w_2, kv_b_2, b_w_q_2,
    b_b_q_2, b_sinks_2, b_w_o_2, b_b_o_2, mix_ln_g_2, mix_ln_b_2, mlp_w_up_2, mlp_w_down_2,
    mlp_ln_g_2, mlp_ln_b_2, ple_w_gate_2, ple_b_gate_2, ple_w_proj_2,
):
    x = first_block(
        x, norm_g, w_in, b_f, q_norm_g, k_norm_g, w_pool, pool_scale, w_out,
    )
    return second_block(
        x, p_2, positions_2, a_w_in_2, a_b_igate_2, a_b_fgate_2, a_head_norm_g_2, a_w_out_2,
        kv_w_2, kv_b_2, b_w_q_2, b_b_q_2, b_sinks_2, b_w_o_2, b_b_o_2, mix_ln_g_2, mix_ln_b_2,
        mlp_w_up_2, mlp_w_down_2, mlp_ln_g_2, mlp_ln_b_2, ple_w_gate_2, ple_b_gate_2,
        ple_w_proj_2,
    )


_drawn_inputs = setup_inputs


def setup_inputs(seed=0):
    import zlib

    import numpy as np

    out = dict(_drawn_inputs(seed))
    spreads = {}
    factors = {'norm_g': 4.388,
     'q_norm_g': 31.036,
     'k_norm_g': 26.308,
     'pool_scale': 22.882,
     'a_b_igate_2': 200.0,
     'a_head_norm_g_2': 200.0,
     'kv_b_2': 8.0,
     'b_b_q_2': 47.857,
     'b_sinks_2': 8.0,
     'b_b_o_2': 4.247,
     'ple_b_gate_2': 8.0,
     'a_b_fgate_2': 8.0}
    for name, (base, spread) in spreads.items():
        noise = np.random.default_rng([zlib.crc32(name.encode()), seed]).standard_normal(out[name].shape)
        drawn = base * np.exp(spread * noise) if base else spread * noise
        out[name] = __import__('jax').numpy.asarray(drawn.astype(out[name].dtype))
    for name, factor in factors.items():
        out[name] = (out[name] * factor).astype(out[name].dtype)
    return out
```

```python
from contextlib import ExitStack

import numpy as np

import concourse.bass as bass
from concourse import mybir

F32 = mybir.dt.float32
F32R = mybir.dt.float32r
I32 = mybir.dt.int32
BF16 = mybir.dt.bfloat16
ACT = mybir.ActivationFunctionType
ALU = mybir.AluOpType

P = 128
T = 512
NT = T // P
D = 1024
KD = D // P
D_FF = 4 * D
HALF_FF = D_FF // 2 // P
HD = 64
FOX_HEADS, SB_HEADS, POOL_GROUPS = 8, 4, 4
M_HEADS, M_DK, M_DV = 4, 128, 256
Q_HEADS, KV_HEADS = 16, 4
PLE = 256
POOL_WINDOWS = (2, 4, 8, 16)
PAD = POOL_WINDOWS[-1]
ROPE_DIM, ROPE_THETA = 16, 500000.0
ALPHA = float((2 * 2) ** 0.25)
EPS, LN_EPS, CAP = 1e-6, 1e-5, 15.0
QK_SCALE = HD ** -0.5
NEG = -1e30
RAW_SLOTS, W_SLOTS = 2, 4
ACC = 4

_MLP = [("up{0}a", 16, 1, "act"), ("down{0}a", 8, 2, "dve"), ("up{0}b", 16, 1, "act"), ("down{0}b", 8, 2, "dve"),
        ("gate{0}", 8, 1, "act"), ("proj{0}", 8, 0.25, "dve")]
PHASES = [("gates1", 1, 1, "act"), ("qk1", 8, 1, "act"), ("sbpool1", 6, 1, "act"), ("v1", 6, 1, "act"),
          ("silu1", 8, 1, "act"), ("out1", 8, 1, "dve"),
          ("gates2", 1, 1, "act"), ("qk2", 8, 1, "act"), ("v2", 8, 1, "act"), ("o2", 8, 1, "act"),
          ("out2", 8, 1, "dve")]
PHASES += [(n.format(0), t, b, e) for n, t, b, e in _MLP]
PHASES += [("rope3", 10, 1, "act"), ("v3", 2, 1, "act"), ("out3", 8, 1, "dve")]
PHASES += [(n.format(1), t, b, e) for n, t, b, e in _MLP]


class Phase:

    def __init__(self, first, tiles, per_tile, act_before, dve_before, reader):
        self.first, self.tiles, self.per_tile, self.reader = first, tiles, per_tile, reader
        self.blocks = int(tiles * per_tile)
        self.last = first + self.blocks
        self.act_before, self.dve_before = act_before, dve_before
        self.before = act_before if reader == "act" else dve_before


def plan():
    out, block, act, dve = {}, 0, 0, 0
    for name, tiles, per_tile, reader in PHASES:
        out[name] = Phase(block, tiles, per_tile, act, dve, reader)
        block += out[name].blocks
        act += tiles * (reader == "act")
        dve += tiles * (reader == "dve")
    return out, block


PLAN, N_BLOCKS = plan()

def constant_columns():
    r, c = np.arange(P)[:, None], np.arange(P)[None, :]
    rope = np.zeros((P, P), np.float32)
    half = ROPE_DIM // 2
    for head in (0, HD):
        for m in range(half):
            rope[head + m + half, head + m] = -1.0
            rope[head + m, head + m + half] = 1.0
    select = np.zeros((P, FOX_HEADS, P), np.float32)
    for h in range(FOX_HEADS):
        select[h, h] = 1.0
    inv_freq = np.zeros((P, 1), np.float32)
    freq = np.power(np.float32(ROPE_THETA), -np.arange(half, dtype=np.float32) * np.float32(2.0 / ROPE_DIM))
    for head in (0, HD):
        inv_freq[head:head + half, 0] = freq
        inv_freq[head + half:head + ROPE_DIM, 0] = freq
    window = np.repeat(np.array(POOL_WINDOWS, np.float32).reshape(2, 2).T, HD, axis=0)
    count = np.minimum(np.arange(PAD)[None, None, :] + 1.0, window[:, :, None])
    parts = {
        "ident": np.eye(P), "head_mean": (r // HD == c // HD) / HD, "rope": rope,
        "fox_mask": np.where(c <= r, 0.0, NEG),
        "band_mask": np.concatenate([np.where(c > r, 0.0, NEG), np.where(c <= r, 0.0, NEG)], 1),
        "past_add": np.where(r <= c, 0.0, NEG),
        "before_add": np.where(r < c, 0.0, NEG),
        "before_mul": r < c,
        "minus_later": -1.0 * (r >= c),
        "minus_one": -np.ones((P, P)), "mean": np.ones((P, P)) / D, "one": np.ones((P, P)),
        "select": select.reshape(P, -1), "inv_freq": inv_freq, "inv_window": 1.0 / window,
        "count_fix": (window[:, :, None] / count).reshape(P, -1),
    }
    at, cols = {}, []
    for name, a in parts.items():
        a = np.asarray(a, np.float32)
        at[name] = (sum(x.shape[1] for x in cols), a.shape[1])
        cols.append(a)
    return at, np.ascontiguousarray(np.concatenate(cols, 1))


CONST_AT, CONSTANTS = constant_columns()

PARAM_WIDTHS = [("norm_g", 8), ("b_f", 1), ("q_norm_g", 1), ("k_norm_g", 1), ("pool_scale", 2), ("b_gates", 2),
                ("head_g", 8), ("b_rope", 10), ("b_v", 2), ("sinks", Q_HEADS), ("b_o", 8),
                ("mix_g0", 8), ("mix_b0", 8), ("mlp_g0", 8), ("mlp_b0", 8), ("ple_b0", 8),
                ("mix_g1", 8), ("mix_b1", 8), ("mlp_g1", 8), ("mlp_b1", 8), ("ple_b1", 8), ("w_pool", 2 * P)]
PARAM_AT = {}
for _name, _width in PARAM_WIDTHS:
    PARAM_AT[_name] = (sum(w for _, w in PARAM_AT.values()), _width)
N_PARAMS = sum(w for _, w in PARAM_WIDTHS)

Q_ORDER = [(2 * g + half) * 4 + j for g in range(2) for j in range(4) for half in range(2)]


def grouped(eng, n, step, group=4):
    full = n // group
    for i in range(min(n, group)):
        step(i, i)
    if full > 2:
        with eng.Fori(1, full) as g:
            for j in range(group):
                step(g * group + j, j)
    elif full == 2:
        for j in range(group):
            step(group + j, j)
    if full:
        for j in range(n - full * group):
            step(full * group + j, j)


def early(i, n):
    return isinstance(i, int) and i < n


def build(nc, x, weights, constants, params, positions, ple_in, out, stop=None, probe=None):
    with ExitStack() as ctx:
        def sb(name, shape, dt=F32, where=ctx):
            return where.enter_context(nc.sbuf_tensor(name, shape, dt))

        def sem(name):
            return ctx.enter_context(nc.semaphore(name))

        X = sb("X", [P, KD, T])
        A_hi = sb("A_hi", [P, KD, T], F32R)
        A_lo = sb("A_lo", [P, KD, T], F32R)
        W_raw = sb("W_raw", [P, RAW_SLOTS, KD * P])
        W_hi = sb("W_hi", [P, W_SLOTS, KD * P], F32R)
        W_lo = sb("W_lo", [P, W_SLOTS, KD * P], F32R)
        CONST = sb("CONST", [P, CONSTANTS.shape[1]])
        PARAM = sb("PARAM", [P, N_PARAMS])
        SUM, SQSUM = sb("SUM", [P, T]), sb("SQSUM", [P, T])
        SQ = sb("SQ", [P, 2, T])
        MEAN, RSTD = sb("MEAN", [P, T]), sb("RSTD", [P, T])
        COS, SIN = sb("COS", [P, T]), sb("SIN", [P, T])
        MIX = sb("MIX", [P, 2, T])
        SMALL = sb("SMALL", [P, 64])
        GK = sb("GK", [P, 2])
        EPS_COL = sb("EPS_COL", [P, 2])
        HOLD, HOLD_ACT = sb("HOLD", [1, 1 + W_SLOTS]), sb("HOLD_ACT", [1, 9])
        IDENT_B, FOX_MASK_B = sb("IDENT_B", [P, P], BF16), sb("FOX_MASK_B", [P, P], BF16)
        BAND_MASK_B, ONE_B = sb("BAND_MASK_B", [P, 2 * P], BF16), sb("ONE_B", [3, P], BF16)

        with ExitStack() as part:
            POS_I = sb("POS_I", [1, T], I32, part)
            POS_F = sb("POS_F", [1, T], F32, part)
            ANG, TURN = sb("ANG", [P, T], F32, part), sb("TURN", [P, T], F32, part)
            ROT_TMP = sb("ROT_TMP", [P, T], F32, part)
        with ExitStack() as part:
            QK = sb("QK", [P, 8, T], F32, part)
            SBQK = sb("SBQK", [P, 4, T], F32, part)
            PX = sb("PX", [P, 2, PAD + T], F32, part)
            V1 = sb("V1", [P, NT, 6, P], F32, part)
            G1 = sb("G1", [P, 8, T], F32, part)
            with ExitStack() as sub:
                NEG_C = sb("NEG_C", [3, FOX_HEADS, T], BF16, sub)
                with ExitStack() as prelude:
                    FF = sb("FF", [FOX_HEADS, 3, T], F32, prelude)
                    FF_PART = sb("FF_PART", [FOX_HEADS, 3, T], BF16, prelude)
                STAGE_Q, STAGE_K = sb("STAGE_Q", [P, T], F32, sub), sb("STAGE_K", [P, T], F32, sub)
                PR, PT = sb("PR", [P, 2, T], F32, sub), sb("PT", [P, 2, T], F32, sub)
                O_T = sb("O_T", [P, NT, P], F32, sub)
            with ExitStack() as sub:
                WIN = sb("WIN", [P, 2, PAD + T], F32, sub)
                POOLED = sb("POOLED", [P, T], F32, sub)
            with ExitStack() as sub:
                SP_T = sb("SP_T", [P, NT, T], F32, sub)
                SB_TMP = sb("SB_TMP", [P, 2, T], F32, sub)
                ATT = sb("ATT", [P, NT, T], F32, sub)
        with ExitStack() as part:
            MQK = sb("MQK", [P, 8, T], F32, part)
            V2 = sb("V2", [P, NT, M_HEADS, M_DV + 1], F32, part)
            O2 = sb("O2", [P, 8, T], F32, part)
            MCOL = sb("MCOL", [P, NT, 2, M_HEADS], F32, part)
            NEG_M = sb("NEG_M", [P, M_HEADS, T], F32, part)
            STATS = sb("STATS", [P, M_HEADS, NT, 6], F32, part)
            AGGR = sb("AGGR", [P, M_HEADS, NT, 2], F32, part)
            with ExitStack() as sub:
                MG = sb("MG", [36, 3, T], F32, sub)
                ROWS = sb("ROWS", [M_HEADS, 4, T], F32, sub)
            with ExitStack() as sub:
                MK = sb("MK", [P, T], F32, sub)
                DEC = sb("DEC", [P, NT, T], F32, sub)
                DIAG = sb("DIAG", [P, NT, P], F32, sub)
        with ExitStack() as part:
            QK3 = sb("QK3", [P, 10, T], F32, part)
            V3 = sb("V3", [P, NT, 2, P], F32, part)
            RAWQ, ROT = sb("RAWQ", [P, 2, T], F32, part), sb("ROT", [P, T], F32, part)
            STAGE_Q3 = sb("STAGE_Q3", [P, T], F32, part)
            PR3, PT3 = sb("PR3", [P, 2, T], F32, part), sb("PT3", [P, 2, T], F32, part)
            O_T3 = sb("O_T3", [P, NT, P], F32, part)
        with ExitStack() as part:
            H_hi = sb("H_hi", [P, HALF_FF, T], F32R, part)
            H_lo = sb("H_lo", [P, HALF_FF, T], F32R, part)
            RELU, SQR = sb("RELU", [P, 2, T], F32, part), sb("SQR", [P, 2, T], F32, part)
        with ExitStack() as part:
            GATE = sb("GATE", [P, KD, T], F32, part)
            P_hi, P_lo = sb("P_hi", [P, 2, T], F32R, part), sb("P_lo", [P, 2, T], F32R, part)

        PS = ctx.enter_context(nc.psum_tensor("PS", [P, 8, T], F32))

        def const(name, width=None, row=slice(None), skip=0):
            at, full = CONST_AT[name]
            return CONST[row, at + skip:at + skip + (width or full)]

        def param(name, i=0, rows=slice(None)):
            at = PARAM_AT[name][0]
            return PARAM[rows, at + i:at + i + 1]

        x_in, c_in, pos_in, ple_got, out_done = (sem(n) for n in ("x_in", "c_in", "pos_in", "ple_got", "out_done"))
        w_in = [sem(f"w_in{s}") for s in range(RAW_SLOTS)]
        w_hi, w_lo = sem("w_hi"), sem("w_lo")
        block_done = sem("block_done")
        sums_read = {"act": sem("sums_read_act"), "dve": sem("sums_read_dve")}
        by_act, by_dve = sums_read["act"], sums_read["dve"]
        a_hi, a_lo = sem("a_hi"), sem("a_lo")
        h_sq, h_hi, h_lo = sem("h_sq"), sem("h_hi"), sem("h_lo")
        p_hi, p_lo = sem("p_hi"), sem("p_lo")
        sq_ready, sum_added, sq_added = sem("sq_ready"), sem("sum_added"), sem("sq_added")
        stats_done, var_ready, sd_ready = sem("stats_done"), sem("var_ready"), sem("sd_ready")
        rstd_ready, normed, x_ready = sem("rstd_ready"), sem("normed"), sem("x_ready")
        act_own, dve_own = sem("act_own"), sem("dve_own")
        turned = sem("turned")
        v_ready = sem("v_ready")
        zeroed, hold_set = sem("zeroed"), sem("hold_set")
        mix_ready = sem("mix_ready")
        embedded = sem("embedded")
        proj_part = sem("proj_part")
        pos_float, pos_wide = sem("pos_float"), sem("pos_wide")
        angle_ready, angle_done = sem("angle_ready"), sem("angle_done")
        qk_sq, qk_ms, qk_sd, qk_normed = sem("qk_sq"), sem("qk_ms"), sem("qk_sd"), sem("qk_normed")
        fox_soft, fox_rows, fox_gates_in = sem("fox_soft"), sem("fox_rows"), sem("fox_gates_in")
        pooled, pool_done = sem("pooled"), sem("pool_done")
        sb_scored, sb_soft, sb_sp1, sb_sp, sb_summed, sb_att, sb_weighed = (
            sem("sb_" + n) for n in ("scored", "soft", "sp1", "sp", "summed", "att", "weighed"))
        m_tanh, m_capped, m_soft, m_log_f, m_shifted, m_rows, m_cols_turned, m_cols, m_spread, m_spread_read = (
            sem("m_" + n) for n in ("tanh", "capped", "soft", "log_f", "shifted", "rows", "cols_turned", "cols", "spread",
                                    "spread_read"))
        m_staged, m_scored, m_diag, m_dec, m_w, m_weighed, m_h, m_aggr, m_sd, m_normed, m_turned = (
            sem("m_" + n) for n in ("staged", "scored", "diag", "dec", "w", "weighed", "h", "aggr", "sd", "normed", "turned"))
        rope_swapped, roped = sem("rope_swapped"), sem("roped")

        class Attention:

            def __init__(self, name):
                self.staged = sem(name + "_staged")
                self.scored = sem(name + "_scored")
                self.scores_read = sem(name + "_scores_read")
                self.maxed = sem(name + "_maxed")
                self.exped = sem(name + "_exped")
                self.turned = sem(name + "_turned")
                self.turned_read = sem(name + "_turned_read")
                self.weighed = sem(name + "_weighed")
                self.o_read = sem(name + "_o_read")
                self.pair_turned = sem(name + "_pair_turned")

        FOX, SWA = Attention("fox"), Attention("swa")

        def fox_keys(i):
            return 0, (i + 1) * P

        def swa_keys(i):
            return (0, P) if i == 0 else ((i - 1) * P, 2 * P)

        def sink_at(p, h, g):
            at = PARAM_AT["sinks"][0]
            if isinstance(p, int):
                return slice(at + 2 * p + h, at + 2 * p + h + 1)
            return bass.ds(p * 2 + (at + h), 1)

        H2F = MQK[:].rearrange("p a t -> p (a t)").rearrange("p (h i c) -> p h i c", h=M_HEADS, i=NT)

        class Own:

            def __init__(self, eng, s):
                self.eng, self.s, self.n = eng, s, 0
                self.loop, self.start, self.per = None, 0, 0

            def __call__(self, ins):
                ins.then_inc(self.s, 1)
                self.n += 1

            def wait(self):
                n = self.n
                if self.loop is not None:
                    n = self.start + (self.n - self.start) + self.loop * self.per
                self.eng.wait_ge(self.s, n)

            def enter(self, loop, per):
                self.loop, self.start, self.per = loop, self.n, per

            def leave(self, rounds):
                assert self.n - self.start == self.per, (self.n - self.start, self.per)
                self.n = self.start + rounds * self.per
                self.loop = None

        A_STAGE = {n: i for i, n in enumerate(["norm", "mixed1", "x1", "mixed2", "ln0", "ln1", "ple0", "mixed3",
                                               "ln2", "ln3"])}

        block = ctx.enter_context(nc.Block())

        @block.sync
        def _(sp):
            sp.dma_start(X[:], x).then_inc(x_in, 16)
            sp.dma_start(CONST[:], constants).then_inc(c_in, 16)
            sp.dma_start(PARAM[:], params).then_inc(c_in, 16)
            sp.dma_start(POS_I[:], positions).then_inc(pos_in, 16)

            def fetch(n, s):
                if not early(n, RAW_SLOTS):
                    sp.wait_ge(w_lo, n - RAW_SLOTS + 1)
                sp.dma_start(W_raw[:, s, :], weights[n]).then_inc(w_in[s], 16)

            grouped(sp, N_BLOCKS, fetch, RAW_SLOTS)

        @block.gpsimd
        def _(pool):
            def split(n, s, use):
                r = s % RAW_SLOTS
                pool.wait_ge(w_in[r], 16 * (use + 1))
                if not early(n, W_SLOTS):
                    pool.wait_ge(block_done, n - W_SLOTS + 1)
                pool.tensor_tensor(HOLD[:, 1 + s:2 + s], HOLD[:, 0:1], HOLD[:, 0:1], ALU.add)
                pool.tensor_scalar(W_hi[:, s, :], W_raw[:, r, :], 1.0, 1.0, ALU.mult, ALU.mult).then_inc(w_hi, 1)
                pool.wait_ge(w_hi, n + 1)
                pool.tensor_tensor(W_lo[:, s, :], W_raw[:, r, :], W_hi[:, s, :].bitcast(F32),
                                   ALU.subtract).then_inc(w_lo, 1)

            pool.memset(HOLD[:], 0.0).then_inc(hold_set, 1)
            pool.wait_ge(hold_set, 1)
            uses = W_SLOTS // RAW_SLOTS
            for n in range(W_SLOTS):
                split(n, n, n // RAW_SLOTS)
            with pool.Fori(1, N_BLOCKS // W_SLOTS) as g:
                for s in range(W_SLOTS):
                    split(g * W_SLOTS + s, s, g * uses + s // RAW_SLOTS)
            for n in range(N_BLOCKS // W_SLOTS * W_SLOTS, N_BLOCKS):
                split(n, n % W_SLOTS, n // RAW_SLOTS)

        @block.tensor
        def _(pe):
            def product(phase, hi, lo, ready, ready_at, tiles_k=KD, beside=None):
                ph = PLAN[phase]
                per = max(1, int(ph.per_tile))
                pe.wait_ge(by_act, ph.act_before)
                if ph.dve_before:
                    pe.wait_ge(by_dve, ph.dve_before)

                def tile(i, j):
                    bank = j % ACC
                    if not early(i, ACC):
                        pe.wait_ge(sums_read[ph.reader], ph.before + i - ACC + 1)
                    for b in range(per):
                        slot = (ph.first + j * per + b) % W_SLOTS
                        pe.wait_ge(w_lo, i * per + (ph.first + b + 1))
                        for k in range(KD):
                            kk = b * KD + k
                            if early(i, 1):
                                pe.wait_ge(ready, ready_at + kk + 1)
                            w = slice(k * P, k * P + P)
                            first, last = kk == 0, kk == per * KD - 1
                            pe.matmul(PS[:, bank, :], W_hi[:, slot, w], hi[:, kk, :], start=first, stop=False)
                            pe.matmul(PS[:, bank, :], W_lo[:, slot, w], hi[:, kk, :], start=False, stop=False)
                            done = pe.matmul(PS[:, bank, :], W_hi[:, slot, w], lo[:, kk, :], start=False, stop=last)
                        done.then_inc(block_done, 1)
                    if beside and not early(i, 1):
                        beside(i - 1)

                grouped(pe, ph.tiles, tile, ACC)
                if beside:
                    beside(ph.tiles - 1)

            def beside_bank(i):
                return 4 + i % 2

            def turn_values(phase, at):
                ph = PLAN[phase]

                def turn(i):
                    pe.wait_ge(by_act, ph.before + i + 1)
                    if i >= 2:
                        pe.wait_ge(v_ready, at + i - 1)
                    for t in range(NT):
                        mm = pe.transpose(PS[:, beside_bank(i), t * P:t * P + P], SQ[:, i % 2, t * P:t * P + P],
                                          const("ident"))
                    mm.then_inc(turned, 1)
                return turn

            def angles():
                pe.wait_ge(c_in, 32)
                pe.wait_ge(pos_float, 1)
                pe.matmul(PS[:, 6, :], const("one", row=slice(0, 1)), POS_F[:], start=True, stop=True).then_inc(pos_wide, 1)

            def first_norm():
                pe.wait_ge(sq_added, KD)
                pe.matmul(PS[:, 5, :], const("mean"), SQSUM[:], start=True, stop=True).then_inc(stats_done, 1)

            def head_norm(i):
                pe.wait_ge(qk_sq, i + 1)
                if i >= 2:
                    pe.wait_ge(qk_sd, i - 1)
                pe.matmul(PS[:, beside_bank(i), :], const("head_mean"), SQ[:, i % 2, :], start=True,
                          stop=True).then_inc(qk_ms, 1)

            def spread_rows(rows, n, ready, ready_at, spread, used, banks):
                pe.wait_ge(ready, ready_at)
                for h in range(n):
                    if h >= len(banks):
                        pe.wait_ge(used, h - len(banks) + 1)
                    pe.matmul(PS[:, banks[h % len(banks)], :], const("select", P, slice(0, rows.shape[0]), h * P), rows,
                              start=True, stop=True).then_inc(spread, 1)

            def softmax_attention(S, keys, stage, values, mask, log_gates=None):
                PR_, PT_, O_, Q_, K_ = stage

                def pair(p, k_tile, stages):
                    def u(n):
                        return p * 8 + n

                    def scores(n):
                        h, i = n // NT, n % NT
                        first, width = keys(i)
                        bank = 4 + n % 2
                        if not early(u(n), 2):
                            pe.wait_ge(S.exped, u(n) - 1)
                        half = slice(h * HD, h * HD + HD)
                        pe.matmul(PS[:, bank, 0:width], Q_[half, i * P:i * P + P], k_tile[half, first:first + width],
                                  start=True, stop=False)
                        if log_gates is not None:
                            pe.matmul(PS[:, bank, 0:width], ONE_B[:], log_gates(p, h)[:, 0:width], start=False, stop=False)
                        mw = mask.shape[1] if width >= mask.shape[1] else width
                        mm = pe.matmul(PS[:, bank, width - mw:width], IDENT_B[:], mask[:, mask.shape[1] - mw:], start=False,
                                       stop=True)
                        mm.then_inc(S.scored, 1)

                    def transposes(n):
                        first, width = keys(n % NT)
                        pe.wait_ge(S.exped, u(n) + 1)
                        if not early(u(n), 2):
                            pe.wait_ge(S.turned_read, u(n) - 1)
                        for j in range(width // P):
                            mm = pe.transpose(PS[:, 6 + n % 2, j * P:j * P + P], PR_[:, n % 2, j * P:j * P + P],
                                              const("ident"))
                        mm.then_inc(S.turned, 1)

                    def weigh(n):
                        h, i = n // NT, n % NT
                        first, width = keys(i)
                        pe.wait_ge(S.turned_read, u(n) + 1)
                        if not early(u(n), 2):
                            pe.wait_ge(S.o_read, u(n) - 1)
                        for j in range(width // P):
                            mm = pe.matmul(PS[:, n % 2, 0:HD], PT_[:, n % 2, j * P:j * P + P],
                                           values(p, first // P + j, h), start=j == 0, stop=(j + 1) * P == width)
                        mm.then_inc(S.weighed, 1)

                    pe.wait_ge(S.staged, stages)
                    scores(0)
                    for n in range(8):
                        if n + 1 < 8:
                            scores(n + 1)
                        transposes(n)
                        if n:
                            weigh(n - 1)
                    weigh(7)
                    pe.wait_ge(S.o_read, u(8))
                    for t in range(NT):
                        mm = pe.transpose(PS[:, 2, t * P:t * P + P], O_[:, t, :], const("ident"))
                    mm.then_inc(S.pair_turned, 1)

                return pair

            def pool_product():
                for c in range(2):
                    pe.wait_ge(pooled, c + 1)
                    at = PARAM_AT["w_pool"][0] + c * P
                    pe.matmul(PS[:, 3, :], PARAM[:, at:at + P], POOLED[:], start=True, stop=True).then_inc(pool_done, 1)

            def stick_breaking():
                for h in range(SB_HEADS):
                    c, half = h // 2, slice(h % 2 * HD, h % 2 * HD + HD)
                    for j in range(NT):
                        if h:
                            pe.wait_ge(sb_att, NT * (h - 1) + j + 1)
                        pe.matmul(PS[:, j, 0:T - j * P], SBQK[half, 2 + c, j * P:j * P + P], SBQK[half, c, j * P:T],
                                  start=True, stop=True).then_inc(sb_scored, 1)
                    pe.wait_ge(sb_sp, NT * (h + 1))
                    for j in range(NT):
                        width = T - j * P
                        pe.matmul(PS[:, j, 0:width], const("minus_later"), SP_T[:, j, 0:width], start=False,
                                  stop=True, skip_group_check=True)
                        for i in range(j + 1, NT):
                            pe.matmul(PS[:, j, (i - j) * P:width], const("minus_one"), SP_T[:, i, 0:T - i * P],
                                      start=False, stop=True, skip_group_check=True)
                        pe.matmul(PS[:, j, 0:P], const("ident"), const("before_add"), start=False, stop=True,
                                  skip_group_check=True).then_inc(sb_summed, 1)
                    for j in range(NT):
                        pe.wait_ge(sb_att, NT * h + j + 1)
                        mm = pe.matmul(PS[half, 4 + c, j * P:T], V1[:, j, 4 + c, half], ATT[:, j, 0:T - j * P],
                                       start=j == 0, stop=j == NT - 1, skip_group_check=True)
                    mm.then_inc(sb_weighed, 1)

            def matrix_memory():
                pe.wait_ge(m_rows, 1)
                for t in range(NT):
                    for r in range(2):
                        mm = pe.transpose(PS[:, 6, (t * 2 + r) * M_HEADS:(t * 2 + r + 1) * M_HEADS],
                                          ROWS[:, r * 3, t * P:t * P + P], const("ident", M_HEADS, slice(0, M_HEADS)))
                mm.then_inc(m_cols_turned, 1)
                spread_rows(ROWS[:, 2, :], M_HEADS, m_rows, 1, m_spread, m_spread_read, (4, 5))

                def head(h, round_, first=False):
                    pe.wait_ge(m_staged, round_ + 1)
                    for j in range(NT):
                        if not first:
                            pe.wait_ge(m_w, round_ * NT - NT + j + 1)
                        pe.matmul(PS[:, j, 0:T - j * P], MK[:, j * P:j * P + P], MQK[:, 2 * h, j * P:T], start=True,
                                  stop=True).then_inc(m_scored, 1)
                    for i in range(NT):
                        pe.wait_ge(m_w, round_ * NT + NT)
                        if not first:
                            pe.wait_ge(m_h, round_ * NT - NT + i + 1)
                        for j in range(i + 1):
                            mm = pe.matmul(PS[:, 4 + i, 0:M_DV + 1], DEC[:, j, (i - j) * P:(i - j + 1) * P],
                                           V2[:, j, h, :], start=j == 0, stop=j == i)
                        mm.then_inc(m_weighed, 1)

                pe.wait_ge(m_spread_read, M_HEADS)
                head(0, 0, True)
                with pe.Fori(1, M_HEADS) as h:
                    head(h, h)
                pe.wait_ge(m_normed, M_HEADS * NT)
                for f in range(KD):
                    if f >= 2:
                        pe.wait_ge(mix_ready, 2 * KD + f - 1)
                    for t in range(NT):
                        h, c = f // 2, f % 2
                        mm = pe.transpose(PS[:, 4 + f % 2, t * P:t * P + P],
                                          H2F[:, h, t, c * P:c * P + P], const("ident"))
                    mm.then_inc(m_turned, 1)

            def layer_stats(n):
                pe.wait_ge(sum_added, KD * (n + 1))
                pe.wait_ge(sq_added, KD * (n + 2))
                pe.matmul(PS[:, 4, :], const("mean"), SUM[:], start=True, stop=True).then_inc(stats_done, 1)
                pe.matmul(PS[:, 5, :], const("mean"), SQSUM[:], start=True, stop=True).then_inc(stats_done, 1)

            def from_a(phase, stage, beside=None):
                product(phase, A_hi, A_lo, a_lo, KD * A_STAGE[stage], beside=beside)

            def mlp(l):
                for half, letter in enumerate("ab"):
                    from_a(f"up{l}{letter}", f"ln{2 * l}")
                    product(f"down{l}{letter}", H_hi, H_lo, h_lo, HALF_FF * (2 * l + half), HALF_FF)
                layer_stats(2 * l + 1)

            def embed(l):
                from_a(f"gate{l}", f"ln{2 * l + 1}")
                ph = PLAN[f"proj{l}"]
                pe.wait_ge(by_act, ph.act_before)
                pe.wait_ge(p_lo, l + 1)
                for i in range(KD):
                    n, quarter = ph.first + i // 4, i % 4
                    if quarter == 0:
                        pe.wait_ge(w_lo, n + 1)
                    if i >= ACC:
                        pe.wait_ge(by_dve, ph.before + i - ACC + 1)
                    for k in range(2):
                        w = slice((quarter * 2 + k) * P, (quarter * 2 + k + 1) * P)
                        slot = n % W_SLOTS
                        pe.matmul(PS[:, i % ACC, :], W_hi[:, slot, w], P_hi[:, k, :], start=k == 0, stop=False)
                        pe.matmul(PS[:, i % ACC, :], W_lo[:, slot, w], P_hi[:, k, :], start=False, stop=False)
                        mm = pe.matmul(PS[:, i % ACC, :], W_hi[:, slot, w], P_lo[:, k, :], start=False, stop=k == 1)
                    if quarter == 3:
                        mm.then_inc(block_done, 1)
                    else:
                        mm.then_inc(proj_part, 1)

            def rope_swap(i):
                ph = PLAN["rope3"]
                pe.wait_ge(by_act, ph.before + i + 1)
                if i >= 2:
                    pe.wait_ge(roped, i - 1)
                pe.matmul(PS[:, beside_bank(i), :], const("rope"), RAWQ[:, i % 2, :], start=True,
                          stop=True).then_inc(rope_swapped, 1)

            angles()
            first_norm()
            from_a("gates1", "norm")
            from_a("qk1", "norm", head_norm)
            from_a("sbpool1", "norm")
            from_a("v1", "norm", turn_values("v1", 0))
            from_a("silu1", "norm")
            pair = softmax_attention(FOX, fox_keys, (PR, PT, O_T, STAGE_Q, STAGE_K),
                                     lambda p, j, h: V1[:, j, p, h * HD:h * HD + HD], FOX_MASK_B,
                                     lambda p, h: NEG_C[:, p * 2 + h, :])
            pe.wait_ge(fox_gates_in, 48)
            pe.wait_ge(v_ready, 6)
            pe.wait_ge(by_act, PLAN["silu1"].act_before + 8)
            pair(0, STAGE_K, 2)
            with pe.Fori(1, 4) as p:
                pair(p, STAGE_K, p * 2 + 2)
            pool_product()
            pe.wait_ge(a_lo, KD * 1 + 6)
            stick_breaking()
            from_a("out1", "mixed1")
            from_a("gates2", "x1")
            from_a("qk2", "x1")
            from_a("v2", "x1", turn_values("v2", 6))
            from_a("o2", "x1")
            pe.wait_ge(v_ready, 14)
            pe.wait_ge(by_act, PLAN["out2"].act_before)
            matrix_memory()
            from_a("out2", "mixed2")
            layer_stats(0)
            mlp(0)
            embed(0)
            from_a("rope3", "ple0", rope_swap)
            pe.wait_ge(roped, 10)
            from_a("v3", "ple0", turn_values("v3", 14))
            pe.wait_ge(v_ready, 16)
            for g in range(2):
                pair = softmax_attention(SWA, swa_keys, (PR3, PT3, O_T3, STAGE_Q3, None),
                                         lambda p, j, h: V3[:, j, g, h * HD:h * HD + HD], BAND_MASK_B)
                pair(4 * g, QK3[:, g, :], 4 * g + 1)
                with pe.Fori(4 * g + 1, 4 * g + 4) as p:
                    pair(p, QK3[:, g, :], p + 1)
            from_a("out3", "mixed3")
            layer_stats(2)
            mlp(1)
            embed(1)

        @block.scalar
        def _(act):
            own = Own(act, act_own)
            held = [0]

            def sums(phase, step):
                ph = PLAN[phase]

                def tile(i, j):
                    act.wait_ge(block_done, (i + 1) * int(ph.per_tile) + ph.first)
                    step(i, PS[:, j % ACC, :], ph.before + i)

                grouped(act, ph.tiles, tile, ACC)

            def split(source, k, stage, ready, at):
                act.wait_ge(ready, at)
                act.activation(A_hi[:, k, :], source, ACT.Copy).then_inc(a_hi, 1)

            def hold():
                at = held[0] = held[0] % 8 + 1
                act.activation(HOLD_ACT[:, at:at + 1], HOLD_ACT[:, 0:1], ACT.Copy)

            def log_one_plus_exp(dst, src):
                own(act.activation(dst, src, ACT.Abs))
                own.wait()
                own(act.activation(dst, dst, ACT.Exp, scale=-1.0))
                own.wait()
                return act.activation(dst, dst, ACT.Ln, bias=1.0)

            def angles():
                act.wait_ge(angle_ready, 2)
                act.activation(SIN[:], ANG[:], ACT.Sin)
                act.activation(COS[:], TURN[:], ACT.Sin).then_inc(angle_done, 1)

            def first_norm():
                act.wait_ge(x_in, 16)
                for k in range(KD):
                    if k >= 2:
                        act.wait_ge(sq_added, k - 1)
                    act.activation(SQ[:, k % 2, :], X[:, k, :], ACT.Square).then_inc(sq_ready, 1)
                act.wait_ge(stats_done, 1)
                act.wait_ge(zeroed, 1)
                act.activation(RSTD[:], PS[:, 5, :], ACT.Sqrt, bias=EPS_COL[:, 0:1]).then_inc(sd_ready, 1)
                for k in range(KD):
                    split(MIX[:, k % 2, :], k, 0, mix_ready, k + 1)

            def fox_gates(i, bank, at):
                act.activation(FF[:, 0, :], bank[0:FOX_HEADS], ACT.Identity, bias=param("b_f", 0, slice(0, FOX_HEADS))).then_inc(by_act, 1)
                act.wait_ge(by_act, at + 1)
                log_one_plus_exp(FF[:, 1, :], FF[:, 0, :]).then_inc(fox_soft, 1)

            def head_sd(i):
                act.wait_ge(qk_ms, i + 1)
                if i >= 2:
                    act.wait_ge(qk_normed, i - 1)
                act.activation(MIX[:, i % 2, :], PS[:, 4 + i % 2, :], ACT.Sqrt, bias=EPS_COL[:, 0:1]).then_inc(qk_sd, 1)

            def fox_qk(i, bank, at):
                act.activation(QK[:, i, :], bank, ACT.Copy).then_inc(by_act, 1)
                act.wait_ge(by_act, at + 1)
                if i >= 2:
                    act.wait_ge(qk_ms, i - 1)
                act.activation(SQ[:, i % 2, :], QK[:, i, :], ACT.Square).then_inc(qk_sq, 1)
                if i:
                    head_sd(i - 1)

            def read_spread(dst, n, spread, used, banks):
                for h in range(n):
                    act.wait_ge(spread, h + 1)
                    act.activation(dst[:, h, :], PS[:, banks[h % len(banks)], :], ACT.Copy).then_inc(used, 1)

            def sb_pool(i, bank, at):
                if i < 2:
                    act.activation(SBQK[:, i, :], bank, ACT.Copy, scale=QK_SCALE).then_inc(by_act, 1)
                elif i < 4:
                    act.activation(SBQK[:, i, :], bank, ACT.Copy).then_inc(by_act, 1)
                else:
                    act.activation(PX[:, i - 4, PAD:], bank, ACT.Copy).then_inc(by_act, 1)

            def values(at_v, bias=False):
                def step(i, bank, at):
                    if i >= 2:
                        act.wait_ge(turned, at_v + i - 1)
                    if bias:
                        act.activation(SQ[:, i % 2, :], bank, ACT.Identity, bias=param("b_v", i)).then_inc(by_act, 1)
                    else:
                        act.activation(SQ[:, i % 2, :], bank, ACT.Copy).then_inc(by_act, 1)
                return step

            def into(dst, func, bias=None):
                def step(i, bank, at):
                    b = {} if bias is None else {"bias": param(bias, i)}
                    act.activation(dst(i), bank, func, **b).then_inc(by_act, 1)
                return step

            def softmax_attention(S, keys, stage, tiles, mixed_at, a_at, sinks):
                PR_, PT_, Q_, K_ = stage

                def pair(p, stage_key=None, first=False):
                    def u(n):
                        return p * 8 + n

                    def copy(n):
                        _, width = keys(n % NT)
                        act.wait_ge(S.turned, u(n) + 1)
                        if not early(u(n), 2):
                            act.wait_ge(S.weighed, u(n) - 1)
                        act.activation(PT_[:, n % 2, 0:width], PS[:, 6 + n % 2, 0:width], ACT.Copy).then_inc(S.turned_read, 1)

                    if not first:
                        act.wait_ge(S.scored, u(0))
                        hold()
                    act.activation(Q_[:], tiles(p), ACT.Copy).then_inc(S.staged, 1)
                    if stage_key is not None:
                        act.activation(K_[:], stage_key, ACT.Copy).then_inc(S.staged, 1)
                    for n in range(8):
                        _, width = keys(n % NT)
                        act.wait_ge(S.maxed, u(n) + 1)
                        neg_max = SMALL[:, n % 4:n % 4 + 1]
                        if sinks:
                            hold()
                            act.activation(SMALL[:, 8 + n % 4:9 + n % 4], sinks(p, n // NT), ACT.Exp, bias=neg_max)
                        act.activation(PR_[:, n % 2, 0:width], PS[:, 4 + n % 2, 0:width], ACT.Exp, bias=neg_max,
                                       accum_out=SMALL[:, 4 + n % 4:5 + n % 4]).then_inc(S.exped, 1)
                        if n:
                            copy(n - 1)
                    copy(7)
                    act.wait_ge(mix_ready, p + (mixed_at + 1))
                    hold()
                    act.activation(A_hi[:, p, :], MIX[:, 0, :], ACT.Copy).then_inc(a_hi, 1)

                return pair

            def stick_breaking():
                for h in range(SB_HEADS):
                    for j in range(NT):
                        width = T - j * P
                        act.wait_ge(sb_scored, NT * h + j + 1)
                        if NT * h + j >= 2:
                            act.wait_ge(sb_sp1, NT * h + j - 1)
                        tmp = SB_TMP[:, j % 2, 0:width]
                        log_one_plus_exp(tmp, PS[:, j, 0:width]).then_inc(sb_soft, 1)
                    for j in range(NT):
                        width = T - j * P
                        act.wait_ge(sb_summed, NT * h + j + 1)
                        if h and j == 0:
                            act.wait_ge(sb_weighed, h)
                        act.activation(ATT[:, j, 0:width], PS[:, j, 0:width], ACT.Exp).then_inc(sb_att, 1)
                    if h % 2:
                        c = h // 2
                        split(MIX[:, c, :], 6 + c, 1, mix_ready, 8 + 6 + c + 1)

            def memory_gates(i, bank, at):
                act.activation(MG[:, 0, :], bank[0:36], ACT.Identity, bias=param("b_gates", 0, slice(0, 36))).then_inc(by_act, 1)
                act.wait_ge(by_act, at + 1)
                act.activation(MG[:, 1, :], MG[:, 0, :], ACT.Tanh, scale=1.0 / CAP).then_inc(m_tanh, 1)
                act.wait_ge(m_capped, 1)
                fg = slice(32, 32 + M_HEADS)
                log_one_plus_exp(MG[fg, 0, :], MG[fg, 2, :]).then_inc(m_soft, 1)
                act.wait_ge(m_log_f, 1)
                act.activation(ROWS[:, 3, :], MG[fg, 1, :], ACT.Copy).then_inc(m_shifted, 1)

            def matrix_memory():
                act.wait_ge(m_cols_turned, 1)
                cols = PS[:, 6, 0:NT * 2 * M_HEADS].rearrange("p (t r h) -> p t r h", t=NT, r=2)
                act.activation(MCOL[:, :, 0, :], cols[:, :, 0, :], ACT.Copy)
                act.activation(MCOL[:, :, 1, :], cols[:, :, 1, :], ACT.Exp, scale=-1.0).then_inc(m_cols, 1)
                act.wait_ge(m_cols, 1)
                read_spread(NEG_M, M_HEADS, m_spread, m_spread_read, (4, 5))

                def head(h, first=False):
                    if not first:
                        act.wait_ge(m_scored, h * NT)
                        hold()
                    act.activation(MK[:], MQK[:, 2 * h + 1, :], ACT.Copy).then_inc(m_staged, 1)
                    if not first:
                        act.wait_ge(m_weighed, h * NT)
                    for j in range(NT):
                        u = MCOL[:, j, 0, h:h + 1] if first else MCOL[:, j, 0, bass.ds(h, 1)]
                        act.wait_ge(m_diag, h * NT + j + 1)
                        hold()
                        act.activation(DEC[:, j, 0:P], DIAG[:, j, :], ACT.Exp, bias=u).then_inc(m_dec, 1)
                        if j + 1 < NT:
                            act.activation(DEC[:, j, P:T - j * P], NEG_M[:, h, (j + 1) * P:T], ACT.Exp,
                                           bias=u).then_inc(m_dec, 1)

                head(0, True)
                with act.Fori(1, M_HEADS) as h:
                    head(h)
                act.wait_ge(m_aggr, 1)
                act.activation(SMALL[:, 16:32].rearrange("p (h i) -> p h i", h=M_HEADS), AGGR[:, :, :, 1], ACT.Sqrt,
                               bias=EPS_COL[:, 1:2]).then_inc(m_sd, 1)
                for f in range(KD):
                    split(MIX[:, f % 2, :], f, 3, mix_ready, 16 + f + 1)

            def squares(phase, n):
                ph = PLAN[phase]
                for i in range(KD):
                    act.wait_ge(by_dve, ph.before + i + 1)
                    if i >= 2:
                        act.wait_ge(sq_added, KD * (n + 1) + i - 1)
                    act.activation(SQ[:, i % 2, :], X[:, i, :], ACT.Square).then_inc(sq_ready, 1)

            def layer_norm(n, g, b, stage):
                act.wait_ge(var_ready, n + 1)
                act.activation(RSTD[:], RSTD[:], ACT.Sqrt, bias=EPS_COL[:, 1:2]).then_inc(sd_ready, 1)
                for k in range(KD):
                    act.wait_ge(normed, 2 * KD * n + 2 * k + 2)
                    act.activation(X[:, k, :], X[:, k, :], ACT.Identity, scale=param(g, k), bias=param(b, k)).then_inc(x_ready, 1)
                    split(X[:, k, :], k, stage, x_ready, KD * n + k + 1)

            def mlp(l):
                for half, letter in enumerate("ab"):
                    base = HALF_FF * (2 * l + half)

                    def hidden(i, bank, at):
                        slot = (i if isinstance(i, int) else at_j[0]) % 2
                        if not early(i, 2):
                            act.wait_ge(h_sq, i + (base - 1))
                        act.activation(RELU[:, slot, :], bank, ACT.Relu).then_inc(by_act, 1)
                        act.wait_ge(h_sq, i + (base + 1))
                        hold()
                        act.activation(H_hi[:, i, :], SQR[:, slot, :], ACT.Copy).then_inc(h_hi, 1)

                    ph = PLAN[f"up{l}{letter}"]
                    at_j = [0]

                    def tile(i, j):
                        at_j[0] = j
                        act.wait_ge(block_done, i + (ph.first + 1))
                        hidden(i, PS[:, j, :], None)

                    grouped(act, ph.tiles, tile, ACC)
                squares(f"down{l}b", 2 * l + 1)

            def embed(l):
                act.wait_ge(sq_added, KD * (2 * l + 3))
                act.dma_start(SQ[:], ple_in[l]).then_inc(ple_got, 16)
                layer_norm(2 * l + 1, f"mlp_g{l}", f"mlp_b{l}", f"ln{2 * l + 1}")
                act.wait_ge(ple_got, 16 * (l + 1))
                act.activation(P_hi[:], SQ[:], ACT.Copy).then_inc(p_hi, 1)
                sums(f"gate{l}", into(lambda i: GATE[:, i, :], ACT.Sigmoid, f"ple_b{l}"))
                for i in range(KD):
                    if l == 0:
                        split(X[:, i, :], i, "ple0", embedded, i + 1)
                    else:
                        act.wait_ge(embedded, KD + i + 1)
                        act.dma_start(out[i], X[:, i, :]).then_inc(out_done, 16)

            def rope(i, bank, at):
                if i >= 2:
                    act.wait_ge(roped, i - 1)
                act.activation(RAWQ[:, i % 2, :], bank, ACT.Identity, bias=param("b_rope", i)).then_inc(by_act, 1)

            angles()
            first_norm()
            sums("gates1", fox_gates)
            sums("qk1", fox_qk)
            head_sd(7)
            act.wait_ge(fox_rows, 3)
            for part in range(3):
                act.dma_start(NEG_C[part:part + 1, :, :], FF_PART[:, part, :]).then_inc(fox_gates_in, 16)
            sums("sbpool1", sb_pool)
            sums("v1", values(0))
            sums("silu1", into(lambda i: G1[:, i, :], ACT.Silu))
            pair = softmax_attention(FOX, fox_keys, (PR, PT, STAGE_Q, STAGE_K), lambda p: QK[:, p, :], 8, 8, None)
            act.wait_ge(qk_normed, 8)
            act.wait_ge(fox_gates_in, 48)
            pair(0, QK[:, 4, :], True)
            with act.Fori(1, 4) as p:
                pair(p, QK[:, p + 4, :])
            for c in range(2):
                split(MIX[:, c, :], 4 + c, 1, mix_ready, 8 + 4 + c + 1)
            stick_breaking()
            act.wait_ge(block_done, PLAN["out1"].last)
            for k in range(KD):
                split(X[:, k, :], k, 2, by_dve, PLAN["out1"].before + k + 1)
            sums("gates2", memory_gates)
            sums("qk2", into(lambda i: MQK[:, 2 * i if i < M_HEADS else 2 * (i - M_HEADS) + 1, :], ACT.Copy))
            sums("v2", values(6))
            sums("o2", into(lambda i: O2[:, i, :], ACT.Sigmoid))
            matrix_memory()
            squares("out2", 0)
            layer_norm(0, "mix_g0", "mix_b0", "ln0")
            mlp(0)
            embed(0)
            sums("rope3", rope)
            sums("v3", values(14, True))
            act.wait_ge(roped, 10)
            for g in range(2):
                pair = softmax_attention(SWA, swa_keys, (PR3, PT3, STAGE_Q3, None), lambda p: QK3[:, p + 2, :], 24, 24,
                                         lambda p, h: PARAM[:, sink_at(p, h, g)])
                pair(4 * g, None, g == 0)
                with act.Fori(4 * g + 1, 4 * g + 4) as p:
                    pair(p)
            squares("out3", 2)
            layer_norm(2, "mix_g1", "mix_b1", "ln2")
            mlp(1)
            embed(1)
            act.wait_ge(out_done, 16 * KD)

        @block.vector
        def _(dve):
            own = Own(dve, dve_own)

            def low_part(k, stage_at, source):
                dve.wait_ge(a_hi, k + (stage_at + 1))
                dve.tensor_tensor(A_lo[:, k, :], source, A_hi[:, k, :].bitcast(F32), ALU.subtract).then_inc(a_lo, 1)

            def prepare():
                dve.memset(MEAN[:], 1.0)
                dve.memset(SQSUM[:], 0.0)
                dve.memset(PX[:, :, 0:PAD], 0.0)
                dve.memset(HOLD_ACT[:], 0.0)
                dve.memset(EPS_COL[:, 1:2], LN_EPS)
                dve.memset(EPS_COL[:, 0:1], EPS).then_inc(zeroed, 1)
                dve.wait_ge(zeroed, 1)

            def angles():
                two_pi, magic = 2 * np.pi, 1.5 * 2.0 ** 23
                c1 = 6.28125
                c2 = float(np.float32(round((two_pi - c1) * 2 ** 24) / 2 ** 24))
                c2 = float(np.floor((two_pi - c1) * 2 ** 21) / 2 ** 21)
                c3 = float(two_pi - c1 - c2)
                dve.wait_ge(pos_in, 16)
                dve.tensor_copy(POS_F[:], POS_I[:]).then_inc(pos_float, 1)
                dve.wait_ge(pos_wide, 1)
                own(dve.tensor_scalar(ANG[:], PS[:, 6, :], const("inv_freq"), None, ALU.mult))
                own.wait()
                own(dve.tensor_scalar(TURN[:], ANG[:], 1.0 / two_pi, magic, ALU.mult, ALU.add))
                own.wait()
                own(dve.tensor_scalar(TURN[:], TURN[:], magic, None, ALU.subtract))
                own.wait()
                for c in (c1, c2, c3):
                    own(dve.scalar_tensor_tensor(out=ANG[:], in0=TURN[:], scalar=-c, in1=ANG[:], op0=ALU.mult, op1=ALU.add))
                    own.wait()
                top = float(np.nextafter(np.float32(np.pi), np.float32(0)))
                own(dve.tensor_scalar(ANG[:], ANG[:], top, -top, ALU.min, ALU.max))
                own.wait()
                own(dve.tensor_scalar(ROT_TMP[:], ANG[:], float(np.pi / 2), -two_pi, ALU.is_gt, ALU.mult))
                own.wait()
                dve.scalar_tensor_tensor(out=TURN[:], in0=ANG[:], scalar=float(np.pi / 2), in1=ROT_TMP[:], op0=ALU.add,
                                         op1=ALU.add).then_inc(angle_ready, 1)
                dve.wait_ge(angle_ready, 1)
                dve.tensor_scalar(TURN[:], TURN[:], top, -top, ALU.min, ALU.max).then_inc(angle_ready, 1)

            def add_square(i, n_before):
                dve.wait_ge(sq_ready, n_before + i + 1)
                if i:
                    dve.wait_ge(sq_added, n_before + i)
                dve.tensor_tensor(SQSUM[:], SQSUM[:], SQ[:, i % 2, :], ALU.add).then_inc(sq_added, 1)

            def mix_slot(k, stage_at):
                if k >= 2:
                    dve.wait_ge(a_lo, stage_at + k - 1)

            def first_norm():
                for k in range(KD):
                    add_square(k, 0)
                dve.wait_ge(sd_ready, 1)
                own(dve.reciprocal(RSTD[:], RSTD[:]))
                own.wait()
                for k in range(KD):
                    mix_slot(k, 0)
                    dve.scalar_tensor_tensor(out=MIX[:, k % 2, :], in0=X[:, k, :], scalar=param("norm_g", k), in1=RSTD[:],
                                             op0=ALU.mult, op1=ALU.mult).then_inc(mix_ready, 1)
                    if k:
                        low_part(k - 1, 0, MIX[:, (k - 1) % 2, :])
                low_part(KD - 1, 0, MIX[:, (KD - 1) % 2, :])

            def running_sum(out, rows_in):
                n = out.shape[0]
                return dve.tensor_tensor_scan(out, MEAN[0:n, :], rows_in, 0.0, ALU.mult, ALU.add)

            def fox_gates():
                dve.wait_ge(fox_soft, 1)
                own(dve.scalar_tensor_tensor(out=FF[:, 2, :], in0=FF[:, 0, :], scalar=0.0, in1=FF[:, 1, :], op0=ALU.min,
                                             op1=ALU.subtract))
                own.wait()
                own(running_sum(FF[:, 1, :], FF[:, 2, :]))
                own.wait()
                own(dve.tensor_scalar(FF[:, 0, :], FF[:, 1, :], -1.0, None, ALU.mult))
                own.wait()
                for part in range(3):
                    dve.tensor_copy(FF_PART[:, part, :], FF[:, 0, :]).then_inc(fox_rows, 1)
                    if part < 2:
                        dve.wait_ge(fox_rows, part + 1)
                        own(dve.tensor_tensor(FF[:, 0, :], FF[:, 0, :], FF_PART[:, part, :], ALU.subtract))
                        own.wait()

            def fox_qk():
                for i in range(8):
                    dve.wait_ge(qk_sd, i + 1)
                    own(dve.reciprocal(MIX[:, i % 2, :], MIX[:, i % 2, :]))
                    own.wait()
                    g = GK[:, 0:1] if i < 4 else param("k_norm_g")
                    dve.scalar_tensor_tensor(out=QK[:, i, :], in0=QK[:, i, :], scalar=g, in1=MIX[:, i % 2, :],
                                             op0=ALU.mult, op1=ALU.mult).then_inc(qk_normed, 1)

            def store_values(at_v, n, dst):
                for i in range(n):
                    dve.wait_ge(turned, at_v + i + 1)
                    dve.tensor_copy(dst(i), PS[:, 4 + i % 2, :].rearrange("p (t f) -> p t f", t=NT)).then_inc(v_ready, 1)

            def softmax_attention(S, keys, O_, a_at, sinks, gate):

                def pair(p):
                    def u(n):
                        return p * 8 + n

                    def finish(n):
                        h, i = n // NT, n % NT
                        dve.wait_ge(S.weighed, u(n) + 1)
                        total = SMALL[:, 4 + n % 4:5 + n % 4]
                        if sinks:
                            own(dve.tensor_tensor(total, total, SMALL[:, 8 + n % 4:9 + n % 4], ALU.add))
                            own.wait()
                        own(dve.reciprocal(SMALL[:, 14 + n % 2:15 + n % 2], total))
                        own.wait()
                        dve.tensor_scalar(O_[:, i, h * HD:h * HD + HD], PS[:, n % 2, 0:HD], SMALL[:, 14 + n % 2:15 + n % 2],
                                          None, ALU.mult).then_inc(S.o_read, 1)

                    for n in range(8):
                        first, width = keys(n % NT)
                        dve.wait_ge(S.scored, u(n) + 1)
                        dve.tensor_reduce(SMALL[:, 12 + n % 2:13 + n % 2], PS[:, 4 + n % 2, 0:width],
                                          mybir.AxisListType.X, ALU.max).then_inc(S.scores_read, 1)
                        dve.wait_ge(S.scores_read, u(n) + 1)
                        if sinks:
                            dve.tensor_scalar(SMALL[:, n % 4:n % 4 + 1], SMALL[:, 12 + n % 2:13 + n % 2],
                                              sinks(p, n // NT), -1.0, ALU.max, ALU.mult).then_inc(S.maxed, 1)
                        else:
                            dve.tensor_scalar(SMALL[:, n % 4:n % 4 + 1], SMALL[:, 12 + n % 2:13 + n % 2],
                                              -1.0, None, ALU.mult).then_inc(S.maxed, 1)
                        if n >= 2:
                            finish(n - 2)
                    finish(6)
                    finish(7)
                    dve.wait_ge(a_lo, p + a_at)
                    dve.wait_ge(S.pair_turned, p + 1)
                    if gate:
                        dve.tensor_tensor(MIX[:, 0, :], PS[:, 2, :], gate(p), ALU.mult).then_inc(mix_ready, 1)
                    else:
                        dve.tensor_copy(MIX[:, 0, :], PS[:, 2, :]).then_inc(mix_ready, 1)
                    low_part(p, a_at, MIX[:, 0, :])

                return pair

            def pool():
                own(dve.memset(WIN[:, :, 0:PAD], 0.0))
                for c in range(2):
                    src, dst = PX[:, c, :], 0
                    steps = POOL_WINDOWS[2 * c + 1].bit_length() - 1
                    for s in range(steps):
                        rows = slice(HD, P) if s == steps - 1 else slice(0, P)
                        own.wait()
                        own(dve.tensor_tensor(WIN[rows, dst, PAD:], src[rows, PAD:], src[rows, PAD - 2 ** s:PAD + T - 2 ** s],
                                              ALU.add))
                        src, dst = WIN[:, dst, :], 1 - dst
                    own.wait()
                    wide, narrow = 1 - dst, dst
                    if c:
                        dve.wait_ge(pool_done, c)
                    own(dve.tensor_scalar(POOLED[0:HD, :], WIN[0:HD, narrow, PAD:], const("inv_window", 1, slice(0, HD), c),
                                          None, ALU.mult))
                    own(dve.tensor_scalar(POOLED[HD:P, :], WIN[HD:P, wide, PAD:], const("inv_window", 1, slice(HD, P), c),
                                          None, ALU.mult))
                    own.wait()
                    own(dve.tensor_tensor(POOLED[:, 0:PAD], POOLED[:, 0:PAD], const("count_fix", PAD, skip=c * PAD), ALU.mult))
                    own.wait()
                    dve.tensor_tensor(POOLED[:], POOLED[:], PX[:, c, PAD:], ALU.subtract).then_inc(pooled, 1)
                    dve.wait_ge(pool_done, c + 1)
                    dve.wait_ge(a_lo, 8 + 4 + c)
                    dve.scalar_tensor_tensor(out=MIX[:, c, :], in0=PS[:, 3, :], scalar=param("pool_scale", c),
                                             in1=G1[:, 4 + c, :], op0=ALU.mult, op1=ALU.mult).then_inc(mix_ready, 1)
                    low_part(4 + c, 8, MIX[:, c, :])

            def stick_breaking():
                for h in range(SB_HEADS):
                    for j in range(NT):
                        width = T - j * P
                        dve.wait_ge(sb_soft, NT * h + j + 1)
                        dve.scalar_tensor_tensor(out=SP_T[:, j, 0:width], in0=PS[:, j, 0:width], scalar=0.0,
                                                 in1=SB_TMP[:, j % 2, 0:width], op0=ALU.max, op1=ALU.add).then_inc(sb_sp1, 1)
                        dve.wait_ge(sb_sp1, NT * h + j + 1)
                        dve.tensor_tensor(SP_T[:, j, 0:P], SP_T[:, j, 0:P], const("before_mul"), ALU.mult).then_inc(sb_sp, 1)
                    if h % 2:
                        c = h // 2
                        dve.wait_ge(sb_weighed, h + 1)
                        dve.wait_ge(a_lo, 8 + 6 + c)
                        dve.tensor_tensor(MIX[:, c, :], PS[:, 4 + c, :], G1[:, 6 + c, :], ALU.mult).then_inc(mix_ready, 1)
                        low_part(6 + c, 8, MIX[:, c, :])

            def residual(phase, n=None, scale=None, bias=None):
                ph = PLAN[phase]
                if n is not None:
                    own(dve.memset(SUM[:], 0.0))
                    own(dve.memset(SQSUM[:], 0.0))
                    own.wait()
                for i in range(KD):
                    if bias:
                        own(dve.tensor_scalar(X[:, i, :], X[:, i, :], scale, param(bias, i), ALU.mult, ALU.add))
                        own.wait()
                    dve.wait_ge(block_done, ph.first + (i + 1) * ph.per_tile)
                    if scale and not bias:
                        dve.scalar_tensor_tensor(out=X[:, i, :], in0=X[:, i, :], scalar=scale, in1=PS[:, i % ACC, :],
                                                 op0=ALU.mult, op1=ALU.add).then_inc(by_dve, 1)
                    else:
                        dve.tensor_tensor(X[:, i, :], X[:, i, :], PS[:, i % ACC, :], ALU.add).then_inc(by_dve, 1)
                    if n is not None:
                        dve.wait_ge(by_dve, ph.before + i + 1)
                        if i:
                            dve.wait_ge(sum_added, KD * n + i)
                        dve.tensor_tensor(SUM[:], SUM[:], X[:, i, :], ALU.add).then_inc(sum_added, 1)
                        if i:
                            add_square(i - 1, KD * (n + 1))
                if n is not None:
                    add_square(KD - 1, KD * (n + 1))

            def layer_norm(n, stage_at):
                dve.wait_ge(stats_done, 2 * n + 2)
                own(dve.tensor_copy(MEAN[:], PS[:, 4, :]))
                own.wait()
                own(dve.tensor_tensor(RSTD[:], MEAN[:], MEAN[:], ALU.mult))
                own.wait()
                dve.wait_ge(stats_done, 2 * n + 3)
                own(dve.tensor_tensor(RSTD[:], PS[:, 5, :], RSTD[:], ALU.subtract))
                own.wait()
                dve.tensor_scalar(RSTD[:], RSTD[:], 0.0, None, ALU.max).then_inc(var_ready, 1)
                dve.wait_ge(sd_ready, n + 2)
                own(dve.reciprocal(RSTD[:], RSTD[:]))
                own.wait()
                for k in range(KD):
                    dve.tensor_tensor(X[:, k, :], X[:, k, :], MEAN[:], ALU.subtract).then_inc(normed, 1)
                    dve.wait_ge(normed, 2 * KD * n + 2 * k + 1)
                    dve.tensor_tensor(X[:, k, :], X[:, k, :], RSTD[:], ALU.mult).then_inc(normed, 1)
                    if k:
                        low_part(k - 1, stage_at, X[:, k - 1, :])
                low_part(KD - 1, stage_at, X[:, KD - 1, :])

            def mlp(l):
                for half, letter in enumerate("ab"):
                    base, ph = HALF_FF * (2 * l + half), PLAN[f"up{l}{letter}"]

                    def tile(i, j):
                        slot = j % 2
                        dve.wait_ge(by_act, i + (ph.before + 1))
                        if not early(i, 2):
                            dve.wait_ge(h_lo, i + (base - 1))
                        dve.tensor_tensor(SQR[:, slot, :], RELU[:, slot, :], RELU[:, slot, :], ALU.mult).then_inc(h_sq, 1)
                        dve.wait_ge(h_hi, i + (base + 1))
                        dve.tensor_tensor(H_lo[:, i, :], SQR[:, slot, :], H_hi[:, i, :].bitcast(F32),
                                          ALU.subtract).then_inc(h_lo, 1)

                    grouped(dve, ph.tiles, tile, ACC)
                    if half == 0:
                        residual(f"down{l}a", None, ALPHA)
                    else:
                        residual(f"down{l}b", 2 * l + 1)

            def embed(l):
                dve.wait_ge(p_hi, l + 1)
                dve.tensor_tensor(P_lo[:], SQ[:], P_hi[:].bitcast(F32), ALU.subtract).then_inc(p_lo, 1)
                ph = PLAN[f"proj{l}"]
                for i in range(KD):
                    if i % 4 == 3:
                        dve.wait_ge(block_done, ph.first + i // 4 + 1)
                    else:
                        dve.wait_ge(proj_part, 6 * l + i // 4 * 3 + i % 4 + 1)
                    dve.tensor_tensor(GATE[:, i, :], GATE[:, i, :], PS[:, i % ACC, :], ALU.mult).then_inc(by_dve, 1)
                    dve.wait_ge(by_dve, ph.before + i + 1)
                    dve.tensor_tensor(X[:, i, :], X[:, i, :], GATE[:, i, :], ALU.add).then_inc(embedded, 1)
                    if l == 0 and i:
                        low_part(i - 1, KD * A_STAGE["ple0"], X[:, i - 1, :])
                if l == 0:
                    low_part(KD - 1, KD * A_STAGE["ple0"], X[:, KD - 1, :])

            def memory_gates():
                fg = slice(32, 32 + M_HEADS)
                dve.wait_ge(m_tanh, 1)
                dve.tensor_scalar(MG[:, 2, :], MG[:, 1, :], CAP, None, ALU.mult).then_inc(m_capped, 1)
                dve.wait_ge(m_soft, 1)
                dve.scalar_tensor_tensor(out=MG[fg, 1, :], in0=MG[fg, 2, :], scalar=0.0, in1=MG[fg, 0, :], op0=ALU.min,
                                         op1=ALU.subtract).then_inc(m_log_f, 1)
                dve.wait_ge(m_shifted, 1)
                own(running_sum(ROWS[:, 1, :], ROWS[:, 3, :]))
                own.wait()
                own(dve.tensor_tensor(ROWS[:, 0, :], MG[0:M_HEADS, 2, :], ROWS[:, 1, :], ALU.subtract))
                own.wait()
                own(dve.tensor_tensor_scan(ROWS[:, 2, :], ROWS[:, 0, :], ROWS[:, 0, :], 0.0, ALU.max, ALU.max))
                own.wait()
                own(dve.tensor_tensor(ROWS[:, 3, :], ROWS[:, 1, :], ROWS[:, 2, :], ALU.add))
                own(dve.memset(V2[:, :, :, M_DV:M_DV + 1], 1.0))
                dve.tensor_scalar(ROWS[:, 2, :], ROWS[:, 2, :], -1.0, None, ALU.mult).then_inc(m_rows, 1)

            def matrix_memory():
                dve.wait_ge(m_cols, 1)
                dve.wait_ge(m_spread_read, M_HEADS)

                def head(h, first=False):
                    for j in range(NT):
                        dve.tensor_tensor(DIAG[:, j, :], NEG_M[:, h, j * P:j * P + P], const("past_add"),
                                          ALU.add).then_inc(m_diag, 1)
                    for j in range(NT):
                        dve.wait_ge(m_scored, h * NT + j + 1)
                        dve.wait_ge(m_dec, h * (2 * NT - 1) + min(2 * j + 2, 2 * NT - 1))
                        dve.scalar_tensor_tensor(out=DEC[:, j, 0:T - j * P], in0=PS[:, j, 0:T - j * P],
                                                 scalar=float(M_DK ** -0.5), in1=DEC[:, j, 0:T - j * P], op0=ALU.mult,
                                                 op1=ALU.mult).then_inc(m_w, 1)
                    for i in range(NT):
                        e = MCOL[:, i, 1, h:h + 1] if first else MCOL[:, i, 1, bass.ds(h, 1)]
                        den, mag = SMALL[:, 32 + i:33 + i], SMALL[:, 36 + i:37 + i]
                        dve.wait_ge(m_weighed, h * NT + i + 1)
                        own(dve.tensor_copy(den, PS[:, 4 + i, M_DV:M_DV + 1]))
                        own.wait()
                        own(dve.scalar_tensor_tensor(out=mag, in0=den, scalar=-1.0, in1=den, op0=ALU.mult, op1=ALU.max))
                        own.wait()
                        own(dve.tensor_tensor(mag, mag, e, ALU.max))
                        own.wait()
                        own(dve.reciprocal(mag, mag))
                        own.wait()
                        row = H2F[:, h, i, :]
                        dve.tensor_scalar(row, PS[:, 4 + i, 0:M_DV], mag, None, ALU.mult).then_inc(m_h, 1)
                        dve.wait_ge(m_h, h * NT + i + 1)
                        own(dve.bn_stats(STATS[:, h, i, :], row))

                head(0, True)
                with dve.Fori(1, M_HEADS) as h:
                    own.enter(h - 1, 5 * NT)
                    head(h)
                    own.leave(M_HEADS - 1)
                own.wait()
                for h in range(M_HEADS):
                    for i in range(NT):
                        ins = dve.bn_aggr(AGGR[:, h, i, :], STATS[:, h, i, :])
                ins.then_inc(m_aggr, 1)
                dve.wait_ge(m_sd, 1)
                own(dve.reciprocal(SMALL[:, 16:32], SMALL[:, 16:32]))
                own.wait()
                for h in range(M_HEADS):
                    for i in range(NT):
                        r = 16 + h * NT + i
                        dve.tensor_scalar(H2F[:, h, i, :], H2F[:, h, i, :], AGGR[:, h, i, 0:1], SMALL[:, r:r + 1],
                                          ALU.subtract, ALU.mult).then_inc(m_normed, 1)
                for f in range(KD):
                    dve.wait_ge(m_turned, f + 1)
                    mix_slot(f, 24)
                    dve.scalar_tensor_tensor(out=MIX[:, f % 2, :], in0=PS[:, 4 + f % 2, :], scalar=param("head_g", f),
                                             in1=O2[:, f, :], op0=ALU.mult, op1=ALU.mult).then_inc(mix_ready, 1)
                    if f:
                        low_part(f - 1, 24, MIX[:, (f - 1) % 2, :])
                low_part(KD - 1, 24, MIX[:, (KD - 1) % 2, :])

            def rope():
                ph = PLAN["rope3"]
                for i in range(10):
                    s = 1.0 if i < 2 else QK_SCALE
                    dve.wait_ge(rope_swapped, i + 1)
                    own(dve.scalar_tensor_tensor(out=QK3[:, i, :], in0=RAWQ[:, i % 2, :], scalar=s, in1=COS[:],
                                                 op0=ALU.mult, op1=ALU.mult))
                    if i:
                        dve.wait_ge(roped, i)
                    own(dve.scalar_tensor_tensor(out=ROT[:], in0=PS[:, 4 + i % 2, :], scalar=s, in1=SIN[:],
                                                 op0=ALU.mult, op1=ALU.mult))
                    own.wait()
                    dve.tensor_tensor(QK3[:, i, :], QK3[:, i, :], ROT[:], ALU.add).then_inc(roped, 1)

            prepare()
            dve.wait_ge(c_in, 32)
            dve.tensor_copy(IDENT_B[:], const("ident"))
            dve.tensor_copy(FOX_MASK_B[:], const("fox_mask"))
            dve.tensor_copy(BAND_MASK_B[:], const("band_mask"))
            dve.tensor_copy(ONE_B[:], const("one", P, slice(0, 3)))
            own(dve.tensor_scalar(GK[:, 0:1], param("q_norm_g"), QK_SCALE, None, ALU.mult))
            angles()
            first_norm()
            fox_gates()
            fox_qk()
            store_values(0, 6, lambda i: V1[:, :, i, :])
            pair = softmax_attention(FOX, fox_keys, O_T, 8, None, lambda p: G1[:, p, :])
            dve.wait_ge(by_act, PLAN["silu1"].act_before + 8)
            pair(0)
            with dve.Fori(1, 4) as p:
                own.enter(p - 1, 8)
                pair(p)
                own.leave(3)
            pool()
            stick_breaking()
            residual("out1")
            for k in range(KD):
                low_part(k, KD * A_STAGE["x1"], X[:, k, :])
            memory_gates()
            store_values(6, 8, lambda i: V2[:, :, i // 2, i % 2 * P:i % 2 * P + P])
            matrix_memory()
            residual("out2", 0, ALPHA)
            layer_norm(0, KD * A_STAGE["ln0"])
            mlp(0)
            layer_norm(1, KD * A_STAGE["ln1"])
            embed(0)
            dve.wait_ge(angle_done, 1)
            rope()
            store_values(14, 2, lambda i: V3[:, :, i, :])

            for g in range(2):
                pair = softmax_attention(SWA, swa_keys, O_T3, KD * A_STAGE["mixed3"],
                                         lambda p, h: PARAM[:, sink_at(p, h, g)], None)
                pair(4 * g)
                with dve.Fori(4 * g + 1, 4 * g + 4) as p:
                    own.enter(p - (4 * g + 1), 16)
                    pair(p)
                    own.leave(3)
            residual("out3", 2, ALPHA, "b_o")
            layer_norm(2, KD * A_STAGE["ln2"])
            mlp(1)
            layer_norm(3, KD * A_STAGE["ln3"])
            embed(1)


def _blocks(w):
    k, m = w.shape
    if m % P:
        w = np.concatenate([w, np.zeros((k, P - m % P), w.dtype)], 1)
        m = w.shape[1]
    return w.reshape(k // D, KD, P, m // P, P).transpose(3, 0, 2, 1, 4).reshape(-1, P, D)


def _columns(v):
    return np.asarray(v).reshape(-1, P).T


def lay_out(a):
    a = {k: np.asarray(v) for k, v in a.items()}
    wi = a["w_in"][0]
    edges = np.cumsum([0, 512, 512, 512, 512, 8, 256, 256, 256, 256, 256, 256])
    fq, fk, fv, fg, ff, px, pg, sq, sk, sv, sg = (wi[:, s:e] for s, e in zip(edges[:-1], edges[1:]))
    wm = a["a_w_in_2"][0]
    gates2 = np.zeros((D, P), wm.dtype)
    gates2[:, 0:4] = wm[:, 3072:3076]
    gates2[:, 32:36] = wm[:, 3076:3080]
    q_cols = np.concatenate([np.arange(h * HD, h * HD + HD) for h in Q_ORDER])
    stream = [_blocks(w) for w in (ff, fq, fk, sq, sk, px, fv, sv, fg, pg, sg, a["w_out"][0], gates2,
                                   wm[:, 0:3072], a["a_w_out_2"][0])]

    def mlp(l):
        up, down = a["mlp_w_up_2"][l], a["mlp_w_down_2"][l]
        half = D_FF // 2
        for s in (0, half):
            yield _blocks(up[:, s:s + half])
            yield _blocks(down[s:s + half])
        yield _blocks(a["ple_w_gate_2"][l])
        w = a["ple_w_proj_2"][l].reshape(2, P, 2, 4, P)
        yield w.transpose(2, 1, 3, 0, 4).reshape(2, P, D)

    stream += list(mlp(0))
    stream += [_blocks(w) for w in (a["kv_w_2"][:, 0:256], a["b_w_q_2"][0][:, q_cols], a["kv_w_2"][:, 256:512],
                                    a["b_w_o_2"][0][q_cols])]
    stream += list(mlp(1))

    def col(v, at=0):
        c = np.zeros((P, 1), np.float32)
        c[at:at + v.size, 0] = v
        return c

    b_gates = col(a["a_b_igate_2"][0])
    b_gates[32:36, 0] = a["a_b_fgate_2"][0]
    pool = np.zeros((P, 2, P), np.float32)
    for g in range(POOL_GROUPS):
        r = slice(g % 2 * HD, g % 2 * HD + HD)
        pool[r, g // 2, r] = a["w_pool"][0, g]
    sinks = np.broadcast_to(a["b_sinks_2"][0][np.array(Q_ORDER)][None, :], (P, Q_HEADS))
    parts = {
        "norm_g": _columns(a["norm_g"]), "b_f": col(a["b_f"][0]),
        "q_norm_g": np.concatenate([a["q_norm_g"][0]] * 2)[:, None],
        "k_norm_g": np.concatenate([a["k_norm_g"][0]] * 2)[:, None],
        "pool_scale": _columns(a["pool_scale"]), "b_gates": np.concatenate([b_gates, b_gates], 1),
        "head_g": _columns(a["a_head_norm_g_2"]),
        "b_rope": _columns(np.concatenate([a["kv_b_2"][0:256], a["b_b_q_2"][0][q_cols]])),
        "b_v": _columns(a["kv_b_2"][256:512]), "sinks": sinks, "b_o": _columns(a["b_b_o_2"]),
        "w_pool": pool.reshape(P, -1),
    }
    for l in range(2):
        parts[f"mix_g{l}"] = _columns(a["mix_ln_g_2"][l])
        parts[f"mix_b{l}"] = _columns(a["mix_ln_b_2"][l])
        parts[f"mlp_g{l}"] = _columns(a["mlp_ln_g_2"][l])
        parts[f"mlp_b{l}"] = _columns(a["mlp_ln_b_2"][l])
        parts[f"ple_b{l}"] = _columns(a["ple_b_gate_2"][l])
    return {
        "x": np.ascontiguousarray(a["x"][0].T.reshape(KD, P, T).transpose(1, 0, 2)),
        "weights": np.concatenate(stream, 0),
        "constants": CONSTANTS,
        "params": np.ascontiguousarray(np.concatenate([parts[n] for n, _ in PARAM_WIDTHS], 1)),
        "positions": np.ascontiguousarray(a["positions_2"]),
        "ple_in": np.ascontiguousarray(a["p_2"][:, 0].transpose(0, 2, 1).reshape(2, 2, P, T).transpose(0, 2, 1, 3)),
    }


def kernel(**inputs):
    import concourse.bacc as bacc
    from concourse.bass_utils import run_bass_kernel_spmd

    nc = bacc.Bacc("TRN2", target_bir_lowering=False, num_devices=1)
    arrays, aps = {}, []
    for name, a in lay_out(inputs).items():
        arrays[f"in_{name}"] = a
        aps.append(nc.dram_tensor(f"in_{name}", a.shape, mybir.dt.from_np(a.dtype), kind="ExternalInput").ap())
    out = nc.dram_tensor("out", (KD, P, T), F32, kind="ExternalOutput").ap()
    build(nc, *aps, out)
    got = run_bass_kernel_spmd(nc, [arrays], core_ids=[0]).results[0]["out"]
    return np.ascontiguousarray(np.asarray(got).reshape(D, T).T)[None]
```

```python
from contextlib import ExitStack

import numpy as np

import concourse.bass as bass
from concourse import mybir

F32 = mybir.dt.float32
F32R = mybir.dt.float32r
I32 = mybir.dt.int32
BF16 = mybir.dt.bfloat16
ACT = mybir.ActivationFunctionType
ALU = mybir.AluOpType

P = 128
T = 512
NT = T // P
D = 1024
KD = D // P
D_FF = 4 * D
HALF_FF = D_FF // 2 // P
HD = 64
FOX_HEADS, SB_HEADS, POOL_GROUPS = 8, 4, 4
M_HEADS, M_DK, M_DV = 4, 128, 256
Q_HEADS, KV_HEADS = 16, 4
PLE = 256
POOL_WINDOWS = (2, 4, 8, 16)
PAD = POOL_WINDOWS[-1]
ROPE_DIM, ROPE_THETA = 16, 500000.0
ALPHA = float((2 * 2) ** 0.25)
EPS, LN_EPS, CAP = 1e-6, 1e-5, 15.0
QK_SCALE = HD ** -0.5
NEG = -1e30
RAW_SLOTS, W_SLOTS = 2, 4
WOVEN = 3
ACC = 4

SB_AT = {0: 0, 1: T, 3: T + 3 * P, 2: 2 * T}
SB_COLS = 2 * T + 2 * P

_MLP = [("up{0}a", 16, 1, "act"), ("down{0}a", 8, 2, "dve"), ("up{0}b", 16, 1, "act"), ("down{0}b", 8, 2, "dve"),
        ("gate{0}", 8, 1, "act"), ("proj{0}", 8, 0.25, "dve")]
PHASES = [("gates1", 1, 1, "act"), ("qk1", 8, 1, "act"), ("sbpool1", 6, 1, "act"), ("v1", 6, 1, "act"),
          ("silu1", 6, 1, "act"), ("late1", 2, 1, "act"), ("out1", 8, 1, "dve"),
          ("gates2", 1, 1, "act"), ("qk2", 8, 1, "act"), ("v2", 8, 1, "act"), ("o2", 8, 1, "act"),
          ("out2", 8, 1, "dve")]
PHASES += [(n.format(0), t, b, e) for n, t, b, e in _MLP]
PHASES += [("rope3", 10, 1, "act"), ("v3", 2, 1, "act"), ("out3", 8, 1, "dve")]
PHASES += [(n.format(1), t, b, e) for n, t, b, e in _MLP]


class Phase:

    def __init__(self, first, tiles, per_tile, act_before, dve_before, reader):
        self.first, self.tiles, self.per_tile, self.reader = first, tiles, per_tile, reader
        self.blocks = int(tiles * per_tile)
        self.last = first + self.blocks
        self.act_before, self.dve_before = act_before, dve_before
        self.before = act_before if reader == "act" else dve_before


def plan():
    out, block, act, dve = {}, 0, 0, 0
    for name, tiles, per_tile, reader in PHASES:
        out[name] = Phase(block, tiles, per_tile, act, dve, reader)
        block += out[name].blocks
        act += tiles * (reader == "act")
        dve += tiles * (reader == "dve")
    return out, block


PLAN, N_BLOCKS = plan()

def constant_columns():
    r, c = np.arange(P)[:, None], np.arange(P)[None, :]
    rope = np.zeros((P, P), np.float32)
    half = ROPE_DIM // 2
    for head in (0, HD):
        for m in range(half):
            rope[head + m + half, head + m] = -1.0
            rope[head + m, head + m + half] = 1.0
    select = np.zeros((P, FOX_HEADS, P), np.float32)
    for h in range(FOX_HEADS):
        select[h, h] = 1.0
    inv_freq = np.zeros((P, 1), np.float32)
    freq = np.power(np.float32(ROPE_THETA), -np.arange(half, dtype=np.float32) * np.float32(2.0 / ROPE_DIM))
    for head in (0, HD):
        inv_freq[head:head + half, 0] = freq
        inv_freq[head + half:head + ROPE_DIM, 0] = freq
    window = np.repeat(np.array(POOL_WINDOWS, np.float32).reshape(2, 2).T, HD, axis=0)
    count = np.minimum(np.arange(PAD)[None, None, :] + 1.0, window[:, :, None])
    parts = {
        "ident": np.eye(P), "head_mean": (r // HD == c // HD) / HD, "rope": rope,
        "fox_mask": np.where(c <= r, 0.0, NEG),
        "band_mask": np.concatenate([np.where(c > r, 0.0, NEG), np.where(c <= r, 0.0, NEG)], 1),
        "past_add": np.where(r <= c, 0.0, NEG),
        "before_add": np.where(r < c, 0.0, NEG),
        "before_mul": r < c,
        "minus_later": -1.0 * (r >= c),
        "minus_one": -np.ones((P, P)), "mean": np.ones((P, P)) / D, "one": np.ones((P, P)),
        "select": select.reshape(P, -1), "inv_freq": inv_freq, "inv_window": 1.0 / window,
        "count_fix": (window[:, :, None] / count).reshape(P, -1),
    }
    at, cols = {}, []
    for name, a in parts.items():
        a = np.asarray(a, np.float32)
        at[name] = (sum(x.shape[1] for x in cols), a.shape[1])
        cols.append(a)
    return at, np.ascontiguousarray(np.concatenate(cols, 1))


CONST_AT, CONSTANTS = constant_columns()

PARAM_WIDTHS = [("norm_g", 8), ("b_f", 1), ("q_norm_g", 1), ("k_norm_g", 1), ("pool_scale", 2), ("b_gates", 2),
                ("head_g", 8), ("b_rope", 10), ("b_v", 2), ("sinks", Q_HEADS), ("b_o", 8),
                ("mix_g0", 8), ("mix_b0", 8), ("mlp_g0", 8), ("mlp_b0", 8), ("ple_b0", 8),
                ("mix_g1", 8), ("mix_b1", 8), ("mlp_g1", 8), ("mlp_b1", 8), ("ple_b1", 8), ("w_pool", 2 * P)]
PARAM_AT = {}
for _name, _width in PARAM_WIDTHS:
    PARAM_AT[_name] = (sum(w for _, w in PARAM_AT.values()), _width)
N_PARAMS = sum(w for _, w in PARAM_WIDTHS)

Q_ORDER = [(2 * g + half) * 4 + j for g in range(2) for j in range(4) for half in range(2)]


def grouped(eng, n, step, group=4):
    full = n // group
    for i in range(min(n, group)):
        step(i, i)
    if full > 2:
        with eng.Fori(1, full) as g:
            for j in range(group):
                step(g * group + j, j)
    elif full == 2:
        for j in range(group):
            step(group + j, j)
    if full:
        for j in range(n - full * group):
            step(full * group + j, j)


def early(i, n):
    return isinstance(i, int) and i < n


def build(nc, x, weights, constants, params, positions, ple_in, out, stop=None, probe=None):
    with ExitStack() as ctx:
        def sb(name, shape, dt=F32, where=ctx):
            return where.enter_context(nc.sbuf_tensor(name, shape, dt))

        def sem(name):
            return ctx.enter_context(nc.semaphore(name))

        X = sb("X", [P, KD, T])
        A_hi = sb("A_hi", [P, KD, T], F32R)
        A_lo = sb("A_lo", [P, KD, T], F32R)
        W_raw = sb("W_raw", [P, RAW_SLOTS, KD * P])
        W_hi = sb("W_hi", [P, W_SLOTS, KD * P], F32R)
        W_lo = sb("W_lo", [P, W_SLOTS, KD * P], F32R)
        CONST = sb("CONST", [P, CONSTANTS.shape[1]])
        PARAM = sb("PARAM", [P, N_PARAMS])
        SUM, SQSUM = sb("SUM", [P, T]), sb("SQSUM", [P, T])
        SQ = sb("SQ", [P, 2, T])
        MEAN, RSTD = sb("MEAN", [P, T]), sb("RSTD", [P, T])
        COS, SIN = sb("COS", [P, T]), sb("SIN", [P, T])
        MIX = sb("MIX", [P, 2, T])
        SMALL = sb("SMALL", [P, 64])
        GK = sb("GK", [P, 2])
        EPS_COL = sb("EPS_COL", [P, 2])
        HOLD, HOLD_ACT = sb("HOLD", [1, 1 + W_SLOTS]), sb("HOLD_ACT", [1, 9])
        IDENT_B, FOX_MASK_B = sb("IDENT_B", [P, P], BF16), sb("FOX_MASK_B", [P, P], BF16)
        BEFORE_B = sb("BEFORE_B", [P, P], BF16)
        BAND_MASK_B, ONE_B = sb("BAND_MASK_B", [P, 2 * P], BF16), sb("ONE_B", [3, P], BF16)

        with ExitStack() as part:
            POS_I = sb("POS_I", [1, T], I32, part)
            POS_F = sb("POS_F", [1, T], F32, part)
            ANG, TURN = sb("ANG", [P, T], F32, part), sb("TURN", [P, T], F32, part)
            ROT_TMP = sb("ROT_TMP", [P, T], F32, part)
        with ExitStack() as part:
            QK = sb("QK", [P, 8, T], F32, part)
            SBQK = sb("SBQK", [P, 4, T], F32, part)
            PX = sb("PX", [P, 2, PAD + T], F32, part)
            V1 = sb("V1", [P, NT, 6, P], F32, part)
            G1 = sb("G1", [P, 8, T], F32, part)
            with ExitStack() as sub:
                NEG_C = sb("NEG_C", [3, FOX_HEADS, T], BF16, sub)
                with ExitStack() as prelude:
                    FF = sb("FF", [FOX_HEADS, 3, T], F32, prelude)
                    FF_PART = sb("FF_PART", [FOX_HEADS, 3, T], BF16, prelude)
                with ExitStack() as prelude:
                    WIN = sb("WIN", [P, 2, PAD + T], F32, prelude)
                    POOLED = sb("POOLED", [P, 2, T], F32, prelude)
                STAGE_Q, STAGE_K = sb("STAGE_Q", [P, T], F32, sub), sb("STAGE_K", [P, T], F32, sub)
                PR, PT = sb("PR", [P, 2, T], F32, sub), sb("PT", [P, 2, T], F32, sub)
                O_T = sb("O_T", [P, NT, P], F32, sub)
            with ExitStack() as sub:
                ATT = sb("ATT", [P, 2, SB_COLS], F32, sub)
                SP_T = sb("SP_T", [P, 2, SB_COLS], F32, sub)
        with ExitStack() as part:
            MQK = sb("MQK", [P, 8, T], F32, part)
            V2 = sb("V2", [P, NT, M_HEADS, M_DV + 1], F32, part)
            O2 = sb("O2", [P, 8, T], F32, part)
            MCOL = sb("MCOL", [P, NT, 2, M_HEADS], F32, part)
            NEG_M = sb("NEG_M", [P, M_HEADS, T], F32, part)
            STATS = sb("STATS", [P, M_HEADS, NT, 6], F32, part)
            AGGR = sb("AGGR", [P, M_HEADS, NT, 2], F32, part)
            with ExitStack() as sub:
                MG = sb("MG", [36, 3, T], F32, sub)
                ROWS = sb("ROWS", [M_HEADS, 4, T], F32, sub)
            with ExitStack() as sub:
                MK = sb("MK", [P, T], F32, sub)
                DEC = sb("DEC", [P, NT, T], F32, sub)
                DIAG = sb("DIAG", [P, NT, P], F32, sub)
        with ExitStack() as part:
            QK3 = sb("QK3", [P, 10, T], F32, part)
            V3 = sb("V3", [P, NT, 2, P], F32, part)
            RAWQ, ROT = sb("RAWQ", [P, 2, T], F32, part), sb("ROT", [P, T], F32, part)
            STAGE_Q3 = sb("STAGE_Q3", [P, T], F32, part)
            PR3, PT3 = sb("PR3", [P, 2, T], F32, part), sb("PT3", [P, 2, T], F32, part)
            O_T3 = sb("O_T3", [P, NT, P], F32, part)
        with ExitStack() as part:
            H_hi = sb("H_hi", [P, HALF_FF, T], F32R, part)
            H_lo = sb("H_lo", [P, HALF_FF, T], F32R, part)
            RELU, SQR = sb("RELU", [P, 2, T], F32, part), sb("SQR", [P, 2, T], F32, part)
        with ExitStack() as part:
            GATE = sb("GATE", [P, KD, T], F32, part)
            P_hi, P_lo = sb("P_hi", [P, 2, T], F32R, part), sb("P_lo", [P, 2, T], F32R, part)

        PS = ctx.enter_context(nc.psum_tensor("PS", [P, 8, T], F32))

        def const(name, width=None, row=slice(None), skip=0):
            at, full = CONST_AT[name]
            return CONST[row, at + skip:at + skip + (width or full)]

        def param(name, i=0, rows=slice(None)):
            at = PARAM_AT[name][0]
            return PARAM[rows, at + i:at + i + 1]

        x_in, c_in, pos_in, ple_got, out_done = (sem(n) for n in ("x_in", "c_in", "pos_in", "ple_got", "out_done"))
        w_in = [sem(f"w_in{s}") for s in range(RAW_SLOTS)]
        w_hi, w_lo = sem("w_hi"), sem("w_lo")
        block_done = sem("block_done")
        sums_read = {"act": sem("sums_read_act"), "dve": sem("sums_read_dve")}
        by_act, by_dve = sums_read["act"], sums_read["dve"]
        a_hi, a_lo = sem("a_hi"), sem("a_lo")
        h_sq, h_hi, h_lo = sem("h_sq"), sem("h_hi"), sem("h_lo")
        p_hi, p_lo = sem("p_hi"), sem("p_lo")
        sq_ready, sum_added, sq_added = sem("sq_ready"), sem("sum_added"), sem("sq_added")
        stats_done, mean_ready = sem("stats_done"), sem("mean_ready")
        var_ready, sd_ready = sem("var_ready"), sem("sd_ready")
        diag_ready, rstd_ready = sem("diag_ready"), sem("rstd_ready")
        centred, normed, x_ready = sem("centred"), sem("normed"), sem("x_ready")
        act_own, dve_own = sem("act_own"), sem("dve_own")
        turned = sem("turned")
        v_ready = sem("v_ready")
        zeroed, hold_set = sem("zeroed"), sem("hold_set")
        mix_ready = sem("mix_ready")
        embedded = sem("embedded")
        proj_part = sem("proj_part")
        pos_float, pos_wide = sem("pos_float"), sem("pos_wide")
        angle_ready, angle_done = sem("angle_ready"), sem("angle_done")
        qk_sq, qk_ms, qk_sd, qk_normed = sem("qk_sq"), sem("qk_ms"), sem("qk_sd"), sem("qk_normed")
        fox_soft, fox_rows, fox_gates_in = sem("fox_soft"), sem("fox_rows"), sem("fox_gates_in")
        pooled, pool_done = sem("pooled"), sem("pool_done")
        sb_scored, sb_soft, sb_sp1, sb_sp, sb_summed, sb_att, sb_weighed = (
            sem("sb_" + n) for n in ("scored", "soft", "sp1", "sp", "summed", "att", "weighed"))
        m_tanh, m_capped, m_soft, m_log_f, m_shifted, m_rows, m_cols_turned, m_cols, m_spread, m_spread_read = (
            sem("m_" + n) for n in ("tanh", "capped", "soft", "log_f", "shifted", "rows", "cols_turned", "cols", "spread",
                                    "spread_read"))
        m_staged, m_scored, m_diag, m_dec, m_w, m_weighed, m_h, m_aggr, m_sd, m_normed, m_turned = (
            sem("m_" + n) for n in ("staged", "scored", "diag", "dec", "w", "weighed", "h", "aggr", "sd", "normed", "turned"))
        late_gates = sem("late_gates")
        rope_swapped, roped = sem("rope_swapped"), sem("roped")

        class Attention:

            def __init__(self, name):
                self.staged = sem(name + "_staged")
                self.scored = sem(name + "_scored")
                self.scores_read = sem(name + "_scores_read")
                self.maxed = sem(name + "_maxed")
                self.exped = sem(name + "_exped")
                self.turned = sem(name + "_turned")
                self.turned_read = sem(name + "_turned_read")
                self.weighed = sem(name + "_weighed")
                self.o_read = sem(name + "_o_read")
                self.pair_turned = sem(name + "_pair_turned")

        FOX, SWA = Attention("fox"), Attention("swa")

        def fox_keys(i):
            return 0, (i + 1) * P

        def swa_keys(i):
            return (0, P) if i == 0 else ((i - 1) * P, 2 * P)

        def sinks_at(p):
            at = PARAM_AT["sinks"][0]
            return slice(at + 2 * p, at + 2 * p + 2) if isinstance(p, int) else bass.ds(p * 2 + at, 2)

        def sink_at(p, h):
            at = PARAM_AT["sinks"][0]
            if isinstance(p, int):
                return slice(at + 2 * p + h, at + 2 * p + h + 1)
            return bass.ds(p * 2 + (at + h), 1)

        def sb_scores(h, j=None, skip=0):
            banks = PS[:, 3:6, :] if h % 2 == 0 else PS[:, 0:3, :]
            flat = banks.rearrange("p b t -> p (b t)")
            return flat[:, 0:SB_COLS] if j is None else flat[:, SB_AT[j] + skip:SB_AT[j] + T - j * P]

        def sb_cols(buffer, h, j=None):
            return buffer[:, h % 2, :] if j is None else buffer[:, h % 2, SB_AT[j]:SB_AT[j] + T - j * P]

        def mixed1(k):
            return QK[:, k, :] if not isinstance(k, int) or k < 4 else G1[:, k, :]

        H2F = MQK[:].rearrange("p a t -> p (a t)").rearrange("p (h i c) -> p h i c", h=M_HEADS, i=NT)

        class Own:

            def __init__(self, eng, s):
                self.eng, self.s, self.n = eng, s, 0
                self.loop, self.start, self.per = None, 0, 0

            def __call__(self, ins):
                ins.then_inc(self.s, 1)
                self.n += 1

            def wait(self):
                n = self.n
                if self.loop is not None:
                    n = self.start + (self.n - self.start) + self.loop * self.per
                self.eng.wait_ge(self.s, n)

            def enter(self, loop, per):
                self.loop, self.start, self.per = loop, self.n, per

            def leave(self, rounds):
                assert self.n - self.start == self.per, (self.n - self.start, self.per)
                self.n = self.start + rounds * self.per
                self.loop = None

        A_STAGE = {n: i for i, n in enumerate(["norm", "mixed1", "x1", "mixed2", "ln0", "ln1", "ple0", "mixed3",
                                               "ln2", "ln3"])}

        block = ctx.enter_context(nc.Block())

        @block.sync
        def _(sp):
            sp.dma_start(X[:], x).then_inc(x_in, 16)
            sp.dma_start(CONST[:], constants).then_inc(c_in, 16)
            sp.dma_start(PARAM[:], params).then_inc(c_in, 16)
            sp.dma_start(POS_I[:], positions).then_inc(pos_in, 16)

            def fetch(n, s):
                if not early(n, RAW_SLOTS):
                    sp.wait_ge(w_lo, n - RAW_SLOTS + 1)
                sp.dma_start(W_raw[:, s, :], weights[n]).then_inc(w_in[s], 16)

            grouped(sp, N_BLOCKS, fetch, RAW_SLOTS)

        @block.gpsimd
        def _(pool):
            def split(n, s, use):
                r = s % RAW_SLOTS
                pool.wait_ge(w_in[r], 16 * (use + 1))
                if not early(n, W_SLOTS):
                    pool.wait_ge(block_done, n - W_SLOTS + 1)
                pool.tensor_tensor(HOLD[:, 1 + s:2 + s], HOLD[:, 0:1], HOLD[:, 0:1], ALU.add)
                pool.tensor_scalar(W_hi[:, s, :], W_raw[:, r, :], 1.0, 1.0, ALU.mult, ALU.mult).then_inc(w_hi, 1)
                pool.wait_ge(w_hi, n + 1)
                pool.tensor_tensor(W_lo[:, s, :], W_raw[:, r, :], W_hi[:, s, :].bitcast(F32),
                                   ALU.subtract).then_inc(w_lo, 1)

            pool.memset(HOLD[:], 0.0).then_inc(hold_set, 1)
            pool.wait_ge(hold_set, 1)
            uses = W_SLOTS // RAW_SLOTS
            for n in range(W_SLOTS):
                split(n, n, n // RAW_SLOTS)
            with pool.Fori(1, N_BLOCKS // W_SLOTS) as g:
                for s in range(W_SLOTS):
                    split(g * W_SLOTS + s, s, g * uses + s // RAW_SLOTS)
            for n in range(N_BLOCKS // W_SLOTS * W_SLOTS, N_BLOCKS):
                split(n, n % W_SLOTS, n // RAW_SLOTS)

        @block.tensor
        def _(pe):
            def product(phase, hi, lo, ready, ready_at, tiles_k=KD, beside=None, woven=False):
                ph = PLAN[phase]
                per = max(1, int(ph.per_tile))
                pe.wait_ge(by_act, ph.act_before)
                if ph.dve_before:
                    pe.wait_ge(by_dve, ph.dve_before)

                def weave():
                    pe.wait_ge(w_lo, ph.first + WOVEN)
                    for k in range(KD):
                        pe.wait_ge(ready, ready_at + k + 1)
                        w = slice(k * P, k * P + P)
                        for i in range(WOVEN):
                            slot = (ph.first + i) % W_SLOTS
                            pe.matmul(PS[:, i, :], W_hi[:, slot, w], hi[:, k, :], start=k == 0, stop=False)
                            pe.matmul(PS[:, i, :], W_lo[:, slot, w], hi[:, k, :], start=False, stop=False)
                            done = pe.matmul(PS[:, i, :], W_hi[:, slot, w], lo[:, k, :], start=False, stop=k == KD - 1)
                            if k == KD - 1:
                                done.then_inc(block_done, 1)

                def tile(i, j):
                    if woven and early(i, WOVEN):
                        if i == 0:
                            weave()
                        elif beside:
                            beside(i - 1)
                        return
                    bank = j % ACC
                    if not early(i, ACC):
                        pe.wait_ge(sums_read[ph.reader], ph.before + i - ACC + 1)
                    for b in range(per):
                        slot = (ph.first + j * per + b) % W_SLOTS
                        pe.wait_ge(w_lo, i * per + (ph.first + b + 1))
                        for k in range(KD):
                            kk = b * KD + k
                            if early(i, 1):
                                pe.wait_ge(ready, ready_at + kk + 1)
                            w = slice(k * P, k * P + P)
                            first, last = kk == 0, kk == per * KD - 1
                            pe.matmul(PS[:, bank, :], W_hi[:, slot, w], hi[:, kk, :], start=first, stop=False)
                            pe.matmul(PS[:, bank, :], W_lo[:, slot, w], hi[:, kk, :], start=False, stop=False)
                            done = pe.matmul(PS[:, bank, :], W_hi[:, slot, w], lo[:, kk, :], start=False, stop=last)
                        done.then_inc(block_done, 1)
                    if beside and not early(i, 1):
                        beside(i - 1)

                grouped(pe, ph.tiles, tile, ACC)
                if beside:
                    beside(ph.tiles - 1)

            def beside_bank(i):
                return 4 + i % 2

            def turn_values(phase, at):
                ph = PLAN[phase]

                def turn(i):
                    pe.wait_ge(by_act, ph.before + i + 1)
                    if i >= 2:
                        pe.wait_ge(v_ready, at + i - 1)
                    for t in range(NT):
                        mm = pe.transpose(PS[:, beside_bank(i), t * P:t * P + P], SQ[:, i % 2, t * P:t * P + P],
                                          const("ident"))
                    mm.then_inc(turned, 1)
                return turn

            def angles():
                pe.wait_ge(c_in, 32)
                pe.wait_ge(pos_float, 1)
                pe.matmul(PS[:, 6, :], const("one", row=slice(0, 1)), POS_F[:], start=True, stop=True).then_inc(pos_wide, 1)

            def norm_columns(source, at):
                for t in range(NT):
                    mm = pe.matmul(PS[:, 5, at + t:at + t + 1], source[:, t * P:t * P + P], const("mean", 1), start=True,
                                   stop=True)
                return mm

            def spread_rstd(n):
                pe.wait_ge(diag_ready, NT * (n + 1))
                pe.matmul(PS[:, 6, :], const("one"), RSTD[:], start=True, stop=True).then_inc(rstd_ready, 1)

            def first_norm():
                pe.wait_ge(c_in, 32)
                pe.wait_ge(sq_added, KD)
                norm_columns(SQSUM, NT).then_inc(stats_done, 1)
                spread_rstd(0)

            def head_norm(i):
                pe.wait_ge(qk_sq, i + 1)
                if i >= 2:
                    pe.wait_ge(qk_sd, i - 1)
                pe.matmul(PS[:, beside_bank(i), :], const("head_mean"), SQ[:, i % 2, :], start=True,
                          stop=True).then_inc(qk_ms, 1)

            def spread_rows(rows, n, ready, ready_at, spread, used, banks):
                pe.wait_ge(ready, ready_at)
                for h in range(n):
                    if h >= len(banks):
                        pe.wait_ge(used, h - len(banks) + 1)
                    pe.matmul(PS[:, banks[h % len(banks)], :], const("select", P, slice(0, rows.shape[0]), h * P), rows,
                              start=True, stop=True).then_inc(spread, 1)

            def softmax_attention(S, keys, stage, values, mask, log_gates=None):
                PR_, PT_, O_, Q_, K_ = stage

                def turn_outputs(p):
                    pe.wait_ge(S.o_read, p * 8 + 8)
                    for t in range(NT):
                        mm = pe.transpose(PS[:, 2, t * P:t * P + P], O_[:, t, :], const("ident"))
                    mm.then_inc(S.pair_turned, 1)

                def pair(p, k_tile, stages, first=False, last=None):
                    def u(n):
                        return p * 8 + n

                    def scores(n):
                        h, i = n // NT, n % NT
                        first, width = keys(i)
                        bank = 3 + n % 3
                        if n >= 3:
                            pe.wait_ge(S.exped, u(n) - 2)
                        half = slice(h * HD, h * HD + HD)
                        pe.matmul(PS[:, bank, 0:width], Q_[half, i * P:i * P + P], k_tile[half, first:first + width],
                                  start=True, stop=False)
                        if log_gates is not None:
                            pe.matmul(PS[:, bank, 0:width], ONE_B[:], log_gates(p, h)[:, 0:width], start=False, stop=False)
                        mw = mask.shape[1] if width >= mask.shape[1] else width
                        mm = pe.matmul(PS[:, bank, width - mw:width], IDENT_B[:], mask[:, mask.shape[1] - mw:], start=False,
                                       stop=True)
                        mm.then_inc(S.scored, 1)

                    def transposes(n):
                        first, width = keys(n % NT)
                        pe.wait_ge(S.exped, u(n) + 1)
                        if not early(u(n), 2):
                            pe.wait_ge(S.turned_read, u(n) - 1)
                        for j in range(width // P):
                            mm = pe.transpose(PS[:, 6 + n % 2, j * P:j * P + P], PR_[:, n % 2, j * P:j * P + P],
                                              const("ident"))
                        mm.then_inc(S.turned, 1)

                    def weigh(n):
                        h, i = n // NT, n % NT
                        first, width = keys(i)
                        pe.wait_ge(S.turned_read, u(n) + 1)
                        if not early(u(n), 2):
                            pe.wait_ge(S.o_read, u(n) - 1)
                        for j in range(width // P):
                            mm = pe.matmul(PS[:, n % 2, 0:HD], PT_[:, n % 2, j * P:j * P + P],
                                           values(p, first // P + j, h), start=j == 0, stop=(j + 1) * P == width)
                        mm.then_inc(S.weighed, 1)

                    pe.wait_ge(S.staged, stages)
                    scores(0)
                    scores(1)
                    for n in range(8):
                        if n + 2 < 8:
                            scores(n + 2)
                        transposes(n)
                        if n:
                            weigh(n - 1)
                        if n == 1 and not first:
                            turn_outputs(p - 1)
                    if last:
                        last()
                    weigh(7)

                pair.turn_outputs = turn_outputs
                return pair

            def pool_product():
                for c in range(2):
                    pe.wait_ge(pooled, c + 1)
                    at = PARAM_AT["w_pool"][0] + c * P
                    pe.matmul(PS[:, 6 + c, :], PARAM[:, at:at + P], POOLED[:, c, :], start=True,
                              stop=True).then_inc(pool_done, 1)

            def stick_scores(h):
                c, half = h // 2, slice(h % 2 * HD, h % 2 * HD + HD)
                if h == 1:
                    pe.wait_ge(mix_ready, KD + FOX_HEADS // 2)
                elif h >= 2:
                    pe.wait_ge(sb_att, h - 1)
                for j in range(NT):
                    mm = pe.matmul(sb_scores(h, j), SBQK[half, 2 + c, j * P:j * P + P], SBQK[half, c, j * P:T],
                                   start=j != 3, stop=True, skip_group_check=True)
                mm.then_inc(sb_scored, 1)

            def stick_breaking():
                def sums(h, tiles=range(NT)):
                    pe.wait_ge(sb_sp, NT * (h + 1))
                    for j in tiles:
                        pe.matmul(sb_scores(h, j), const("minus_later"), sb_cols(SP_T, h, j), start=False, stop=True,
                                  skip_group_check=True)
                        for i in range(j + 1, NT):
                            pe.matmul(sb_scores(h, j, (i - j) * P), const("minus_one"), sb_cols(SP_T, h, i), start=False,
                                      stop=True, skip_group_check=True)
                        mm = pe.matmul(sb_scores(h, j)[:, 0:P], IDENT_B[:], BEFORE_B[:], start=False, stop=True,
                                       skip_group_check=True)
                    if tiles[-1] == NT - 1:
                        mm.then_inc(sb_summed, 1)

                def gate(i):
                    ph = PLAN["late1"]
                    slot = (ph.first + i) % W_SLOTS
                    pe.wait_ge(w_lo, ph.first + i + 1)
                    if i:
                        pe.wait_ge(by_act, ph.before + i)
                    for k in range(KD):
                        w = slice(k * P, k * P + P)
                        pe.matmul(PS[:, 7, :], W_hi[:, slot, w], A_hi[:, k, :], start=k == 0, stop=False)
                        pe.matmul(PS[:, 7, :], W_lo[:, slot, w], A_hi[:, k, :], start=False, stop=False)
                        done = pe.matmul(PS[:, 7, :], W_hi[:, slot, w], A_lo[:, k, :], start=False, stop=k == KD - 1)
                    done.then_inc(block_done, 1)

                def weigh(h):
                    c, half = h // 2, slice(h % 2 * HD, h % 2 * HD + HD)
                    pe.wait_ge(sb_att, h + 1)
                    for j in range(NT):
                        mm = pe.matmul(PS[half, 6 + c, j * P:T], V1[:, j, 4 + c, half], sb_cols(ATT, h, j),
                                       start=j == 0, stop=j == NT - 1, skip_group_check=True)
                    mm.then_inc(sb_weighed, 1)

                pair.turn_outputs(3)
                stick_scores(1)
                sums(0)
                sums(1, range(0, 1))
                weigh(0)
                stick_scores(2)
                sums(1, range(1, NT))
                gate(0)
                weigh(1)
                stick_scores(3)
                sums(2)
                gate(1)
                sums(3, range(0, 1))
                pe.wait_ge(by_act, PLAN["late1"].before + 2)
                weigh(2)
                sums(3, range(1, NT))
                weigh(3)

            def matrix_memory():
                pe.wait_ge(m_rows, 1)
                for t in range(NT):
                    for r in range(2):
                        mm = pe.transpose(PS[:, 6, (t * 2 + r) * M_HEADS:(t * 2 + r + 1) * M_HEADS],
                                          ROWS[:, r * 3, t * P:t * P + P], const("ident", M_HEADS, slice(0, M_HEADS)))
                mm.then_inc(m_cols_turned, 1)
                spread_rows(ROWS[:, 2, :], M_HEADS, m_rows, 1, m_spread, m_spread_read, (4, 5))

                def head(h, round_, first=False):
                    pe.wait_ge(m_staged, round_ + 1)
                    for j in range(NT):
                        if not first:
                            pe.wait_ge(m_w, round_ * NT - NT + j + 1)
                        pe.matmul(PS[:, j, 0:T - j * P], MK[:, j * P:j * P + P], MQK[:, 2 * h, j * P:T], start=True,
                                  stop=True).then_inc(m_scored, 1)
                    for i in range(NT):
                        pe.wait_ge(m_w, round_ * NT + NT)
                        if not first:
                            pe.wait_ge(m_h, round_ * NT - NT + i + 1)
                        for j in range(i + 1):
                            mm = pe.matmul(PS[:, 4 + i, 0:M_DV + 1], DEC[:, j, (i - j) * P:(i - j + 1) * P],
                                           V2[:, j, h, :], start=j == 0, stop=j == i)
                        mm.then_inc(m_weighed, 1)

                pe.wait_ge(m_spread_read, M_HEADS)
                head(0, 0, True)
                with pe.Fori(1, M_HEADS) as h:
                    head(h, h)
                pe.wait_ge(m_normed, M_HEADS * NT)
                for f in range(KD):
                    if f >= 2:
                        pe.wait_ge(mix_ready, 2 * KD + f - 1)
                    for t in range(NT):
                        h, c = f // 2, f % 2
                        mm = pe.transpose(PS[:, 4 + f % 2, t * P:t * P + P],
                                          H2F[:, h, t, c * P:c * P + P], const("ident"))
                    mm.then_inc(m_turned, 1)

            def layer_stats(n):
                pe.wait_ge(sum_added, KD * (n + 1))
                pe.matmul(PS[:, 4, :], const("mean"), SUM[:], start=True, stop=True).then_inc(mean_ready, 1)
                norm_columns(SUM, 0)
                pe.wait_ge(sq_added, KD * (n + 2))
                norm_columns(SQSUM, NT).then_inc(stats_done, 1)
                spread_rstd(n + 1)

            def from_a(phase, stage, beside=None, woven=False):
                product(phase, A_hi, A_lo, a_lo, KD * A_STAGE[stage], beside=beside, woven=woven)

            def mlp(l):
                for half, letter in enumerate("ab"):
                    from_a(f"up{l}{letter}", f"ln{2 * l}", woven=half == 0)
                    product(f"down{l}{letter}", H_hi, H_lo, h_lo, HALF_FF * (2 * l + half), HALF_FF)
                layer_stats(2 * l + 1)

            def embed(l):
                from_a(f"gate{l}", f"ln{2 * l + 1}", woven=True)
                ph = PLAN[f"proj{l}"]
                pe.wait_ge(by_act, ph.act_before)
                pe.wait_ge(p_lo, l + 1)
                for i in range(KD):
                    n, quarter = ph.first + i // 4, i % 4
                    if quarter == 0:
                        pe.wait_ge(w_lo, n + 1)
                    if i >= ACC:
                        pe.wait_ge(by_dve, ph.before + i - ACC + 1)
                    for k in range(2):
                        w = slice((quarter * 2 + k) * P, (quarter * 2 + k + 1) * P)
                        slot = n % W_SLOTS
                        pe.matmul(PS[:, i % ACC, :], W_hi[:, slot, w], P_hi[:, k, :], start=k == 0, stop=False)
                        pe.matmul(PS[:, i % ACC, :], W_lo[:, slot, w], P_hi[:, k, :], start=False, stop=False)
                        mm = pe.matmul(PS[:, i % ACC, :], W_hi[:, slot, w], P_lo[:, k, :], start=False, stop=k == 1)
                    if quarter == 3:
                        mm.then_inc(block_done, 1)
                    else:
                        mm.then_inc(proj_part, 1)

            def rope_swap(i):
                ph = PLAN["rope3"]
                pe.wait_ge(by_act, ph.before + i + 1)
                if i >= 2:
                    pe.wait_ge(roped, i - 1)
                pe.matmul(PS[:, beside_bank(i), :], const("rope"), RAWQ[:, i % 2, :], start=True,
                          stop=True).then_inc(rope_swapped, 1)

            angles()
            first_norm()
            from_a("gates1", "norm")
            from_a("qk1", "norm", head_norm)
            from_a("sbpool1", "norm")
            from_a("v1", "norm", turn_values("v1", 0))
            pool_product()
            from_a("silu1", "norm")
            pair = softmax_attention(FOX, fox_keys, (PR, PT, O_T, STAGE_Q, STAGE_K),
                                     lambda p, j, h: V1[:, j, p, h * HD:h * HD + HD], FOX_MASK_B,
                                     lambda p, h: NEG_C[:, p * 2 + h, :])
            pe.wait_ge(fox_gates_in, 48)
            pe.wait_ge(v_ready, 6)
            pe.wait_ge(by_act, PLAN["late1"].before)
            pair(0, STAGE_K, 2, first=True)
            with pe.Fori(1, 3) as p:
                pair(p, STAGE_K, p * 2 + 2)
            pair(3, STAGE_K, 8, last=lambda: stick_scores(0))
            stick_breaking()
            from_a("out1", "mixed1")
            from_a("gates2", "x1")
            from_a("qk2", "x1")
            from_a("v2", "x1", turn_values("v2", 6))
            from_a("o2", "x1")
            pe.wait_ge(v_ready, 14)
            pe.wait_ge(by_act, PLAN["out2"].act_before)
            matrix_memory()
            from_a("out2", "mixed2")
            layer_stats(0)
            mlp(0)
            embed(0)
            from_a("rope3", "ple0", rope_swap)
            pe.wait_ge(roped, 10)
            from_a("v3", "ple0", turn_values("v3", 14))
            pe.wait_ge(v_ready, 16)
            for g in range(2):
                pair = softmax_attention(SWA, swa_keys, (PR3, PT3, O_T3, STAGE_Q3, None),
                                         lambda p, j, h: V3[:, j, g, h * HD:h * HD + HD], BAND_MASK_B)
                pair(4 * g, QK3[:, g, :], 4 * g + 1, first=g == 0)
                with pe.Fori(4 * g + 1, 4 * g + 4) as p:
                    pair(p, QK3[:, g, :], p + 1)
            pair.turn_outputs(7)
            from_a("out3", "mixed3")
            layer_stats(2)
            mlp(1)
            embed(1)

        @block.scalar
        def _(act):
            own = Own(act, act_own)
            held = [0]

            def sums(phase, step):
                ph = PLAN[phase]

                def tile(i, j):
                    act.wait_ge(block_done, (i + 1) * int(ph.per_tile) + ph.first)
                    step(i, PS[:, j % ACC, :], ph.before + i)

                grouped(act, ph.tiles, tile, ACC)

            def split(source, k, stage, ready, at):
                act.wait_ge(ready, at)
                act.activation(A_hi[:, k, :], source, ACT.Copy).then_inc(a_hi, 1)

            def hold():
                at = held[0] = held[0] % 8 + 1
                act.activation(HOLD_ACT[:, at:at + 1], HOLD_ACT[:, 0:1], ACT.Copy)

            def log_one_plus_exp(dst, src):
                own(act.activation(dst, src, ACT.Abs))
                own.wait()
                own(act.activation(dst, dst, ACT.Exp, scale=-1.0))
                own.wait()
                return act.activation(dst, dst, ACT.Ln, bias=1.0)

            def angles():
                act.wait_ge(angle_ready, 2)
                act.activation(SIN[:], ANG[:], ACT.Sin)
                act.activation(COS[:], TURN[:], ACT.Sin).then_inc(angle_done, 1)

            def first_norm():
                act.wait_ge(x_in, 16)
                for k in range(KD):
                    if k >= 2:
                        act.wait_ge(sq_added, k - 1)
                    act.activation(SQ[:, k % 2, :], X[:, k, :], ACT.Square).then_inc(sq_ready, 1)
                act.wait_ge(stats_done, 1)
                act.wait_ge(zeroed, 1)
                act.activation(SMALL[:, 48:52], PS[:, 5, NT:2 * NT], ACT.Sqrt, bias=EPS_COL[:, 0:1]).then_inc(sd_ready, 1)
                for k in range(KD):
                    split(MIX[:, k % 2, :], k, 0, mix_ready, k + 1)

            def fox_gates(i, bank, at):
                act.activation(FF[:, 0, :], bank[0:FOX_HEADS], ACT.Identity, bias=param("b_f", 0, slice(0, FOX_HEADS))).then_inc(by_act, 1)
                act.wait_ge(by_act, at + 1)
                log_one_plus_exp(FF[:, 1, :], FF[:, 0, :]).then_inc(fox_soft, 1)

            def head_sd(i):
                act.wait_ge(qk_ms, i + 1)
                if i >= 2:
                    act.wait_ge(qk_normed, i - 1)
                act.activation(MIX[:, i % 2, :], PS[:, 4 + i % 2, :], ACT.Sqrt, bias=EPS_COL[:, 0:1]).then_inc(qk_sd, 1)

            def fox_qk(i, bank, at):
                act.activation(QK[:, i, :], bank, ACT.Copy).then_inc(by_act, 1)
                act.wait_ge(by_act, at + 1)
                if i >= 2:
                    act.wait_ge(qk_ms, i - 1)
                act.activation(SQ[:, i % 2, :], QK[:, i, :], ACT.Square).then_inc(qk_sq, 1)
                if i:
                    head_sd(i - 1)

            def read_spread(dst, n, spread, used, banks):
                for h in range(n):
                    act.wait_ge(spread, h + 1)
                    act.activation(dst[:, h, :], PS[:, banks[h % len(banks)], :], ACT.Copy).then_inc(used, 1)

            def sb_pool(i, bank, at):
                if i < 2:
                    act.activation(SBQK[:, i, :], bank, ACT.Copy, scale=QK_SCALE).then_inc(by_act, 1)
                elif i < 4:
                    act.activation(SBQK[:, i, :], bank, ACT.Copy).then_inc(by_act, 1)
                else:
                    act.activation(PX[:, i - 4, PAD:], bank, ACT.Copy).then_inc(by_act, 1)

            def values(at_v, bias=False):
                def step(i, bank, at):
                    if i >= 2:
                        act.wait_ge(turned, at_v + i - 1)
                    if bias:
                        act.activation(SQ[:, i % 2, :], bank, ACT.Identity, bias=param("b_v", i)).then_inc(by_act, 1)
                    else:
                        act.activation(SQ[:, i % 2, :], bank, ACT.Copy).then_inc(by_act, 1)
                return step

            def into(dst, func, bias=None):
                def step(i, bank, at):
                    b = {} if bias is None else {"bias": param(bias, i)}
                    act.activation(dst(i), bank, func, **b).then_inc(by_act, 1)
                return step

            def softmax_attention(S, keys, stage, mixed_at=None, sinks=None):
                PR_, PT_, Q_, K_ = stage

                def place(p, query, key=None, first=False):
                    if not first:
                        act.wait_ge(S.scored, p * 8)
                        hold()
                    act.activation(Q_[:], query, ACT.Copy).then_inc(S.staged, 1)
                    if key is not None:
                        act.activation(K_[:], key, ACT.Copy).then_inc(S.staged, 1)

                def mixed(p):
                    act.wait_ge(mix_ready, p + (mixed_at + 1))
                    hold()
                    act.activation(A_hi[:, p, :], MIX[:, 0, :], ACT.Copy).then_inc(a_hi, 1)

                def pair(p, place_next=None, first=False):
                    def u(n):
                        return p * 8 + n

                    def copy(n):
                        _, width = keys(n % NT)
                        act.wait_ge(S.turned, u(n) + 1)
                        if not early(u(n), 2):
                            act.wait_ge(S.weighed, u(n) - 1)
                        act.activation(PT_[:, n % 2, 0:width], PS[:, 6 + n % 2, 0:width], ACT.Copy).then_inc(S.turned_read, 1)

                    if sinks:
                        if not first:
                            act.wait_ge(S.o_read, u(0) - 2)
                            hold()
                        own(act.activation(SMALL[:, 40:42], sinks(p), ACT.Copy))
                        own.wait()
                    for n in range(8):
                        _, width = keys(n % NT)
                        act.wait_ge(S.maxed, u(n) + 1)
                        neg_max = SMALL[:, n % 4:n % 4 + 1]
                        if sinks:
                            act.activation(SMALL[:, 8 + n % 4:9 + n % 4], SMALL[:, 40 + n // NT:41 + n // NT], ACT.Exp,
                                           bias=neg_max)
                        act.activation(PR_[:, n % 2, 0:width], PS[:, 3 + n % 3, 0:width], ACT.Exp, bias=neg_max,
                                       accum_out=SMALL[:, 4 + n % 4:5 + n % 4]).then_inc(S.exped, 1)
                        if n:
                            copy(n - 1)
                        if n == 3 and not first and mixed_at is not None:
                            mixed(p - 1)
                        if n == 6 and place_next:
                            place_next(p + 1)
                    copy(7)

                pair.place, pair.mixed = place, mixed
                return pair

            def stick_breaking():
                def softplus(h):
                    z = sb_cols(ATT, h)
                    own(act.activation(z, z, ACT.Exp, scale=-1.0))
                    own.wait()
                    act.activation(z, z, ACT.Ln, bias=1.0).then_inc(sb_soft, 1)

                def magnitude(h):
                    act.wait_ge(sb_scored, h + 1)
                    if h >= 2:
                        act.wait_ge(sb_weighed, h - 1)
                    own(act.activation(sb_cols(ATT, h), sb_scores(h), ACT.Abs))
                    own.wait()

                def weights(h):
                    act.wait_ge(sb_summed, h + 1)
                    act.activation(sb_cols(ATT, h), sb_scores(h), ACT.Exp).then_inc(sb_att, 1)

                def read_gate(i):
                    ph = PLAN["late1"]
                    act.wait_ge(block_done, ph.first + i + 1)
                    act.activation(G1[:, 6 + i, :], PS[:, 7, :], ACT.Copy).then_inc(by_act, 1)

                for h in (0, 1):
                    magnitude(h)
                    softplus(h)
                weights(0)
                magnitude(2)
                weights(1)
                softplus(2)
                read_gate(0)
                magnitude(3)
                softplus(3)
                read_gate(1)
                weights(2)
                for k in range(6):
                    split(mixed1(k), k, 1, mix_ready, KD + k + 1)
                weights(3)
                act.wait_ge(by_act, PLAN["late1"].before + 2)
                act.activation(G1[:, 6:8, :], G1[:, 6:8, :], ACT.Silu).then_inc(late_gates, 1)
                for k in (6, 7):
                    split(mixed1(k), k, 1, mix_ready, KD + k + 1)

            def memory_gates(i, bank, at):
                act.activation(MG[:, 0, :], bank[0:36], ACT.Identity, bias=param("b_gates", 0, slice(0, 36))).then_inc(by_act, 1)
                act.wait_ge(by_act, at + 1)
                act.activation(MG[:, 1, :], MG[:, 0, :], ACT.Tanh, scale=1.0 / CAP).then_inc(m_tanh, 1)
                act.wait_ge(m_capped, 1)
                fg = slice(32, 32 + M_HEADS)
                log_one_plus_exp(MG[fg, 0, :], MG[fg, 2, :]).then_inc(m_soft, 1)
                act.wait_ge(m_log_f, 1)
                act.activation(ROWS[:, 3, :], MG[fg, 1, :], ACT.Copy).then_inc(m_shifted, 1)

            def matrix_memory():
                act.wait_ge(m_cols_turned, 1)
                cols = PS[:, 6, 0:NT * 2 * M_HEADS].rearrange("p (t r h) -> p t r h", t=NT, r=2)
                act.activation(MCOL[:, :, 0, :], cols[:, :, 0, :], ACT.Copy)
                act.activation(MCOL[:, :, 1, :], cols[:, :, 1, :], ACT.Exp, scale=-1.0).then_inc(m_cols, 1)
                act.wait_ge(m_cols, 1)
                read_spread(NEG_M, M_HEADS, m_spread, m_spread_read, (4, 5))

                def head(h, first=False):
                    if not first:
                        act.wait_ge(m_scored, h * NT)
                        hold()
                    act.activation(MK[:], MQK[:, 2 * h + 1, :], ACT.Copy).then_inc(m_staged, 1)
                    if not first:
                        act.wait_ge(m_weighed, h * NT)
                    for j in range(NT):
                        u = MCOL[:, j, 0, h:h + 1] if first else MCOL[:, j, 0, bass.ds(h, 1)]
                        act.wait_ge(m_diag, h * NT + j + 1)
                        hold()
                        act.activation(DEC[:, j, 0:P], DIAG[:, j, :], ACT.Exp, bias=u).then_inc(m_dec, 1)
                        if j + 1 < NT:
                            act.activation(DEC[:, j, P:T - j * P], NEG_M[:, h, (j + 1) * P:T], ACT.Exp,
                                           bias=u).then_inc(m_dec, 1)

                head(0, True)
                with act.Fori(1, M_HEADS) as h:
                    head(h)
                act.wait_ge(m_aggr, 1)
                act.activation(SMALL[:, 16:32].rearrange("p (h i) -> p h i", h=M_HEADS), AGGR[:, :, :, 1], ACT.Sqrt,
                               bias=EPS_COL[:, 1:2]).then_inc(m_sd, 1)
                for f in range(KD):
                    split(MIX[:, f % 2, :], f, 3, mix_ready, 16 + f + 1)

            def squares(phase, n):
                ph = PLAN[phase]
                act.activation(HOLD_ACT[:, 1:2], HOLD_ACT[:, 0:1], ACT.Sqrt)
                for i in range(KD):
                    act.wait_ge(by_dve, ph.before + i + 1)
                    if i >= 2:
                        act.wait_ge(sq_added, KD * (n + 1) + i - 1)
                    act.activation(SQ[:, i % 2, :], X[:, i, :], ACT.Square).then_inc(sq_ready, 1)

            def layer_norm(n, g, b, stage):
                act.wait_ge(var_ready, n + 1)
                act.activation(SMALL[:, 48:52], SMALL[:, 56:60], ACT.Sqrt, bias=EPS_COL[:, 1:2]).then_inc(sd_ready, 1)
                for k in range(KD):
                    act.wait_ge(normed, KD * n + k + 1)
                    act.activation(X[:, k, :], X[:, k, :], ACT.Identity, scale=param(g, k), bias=param(b, k)).then_inc(x_ready, 1)
                    split(X[:, k, :], k, stage, x_ready, KD * n + k + 1)

            def mlp(l):
                for half, letter in enumerate("ab"):
                    base = HALF_FF * (2 * l + half)

                    def hidden(i, bank, at):
                        slot = (i if isinstance(i, int) else at_j[0]) % 2
                        if not early(i, 2):
                            act.wait_ge(h_sq, i + (base - 1))
                        act.activation(RELU[:, slot, :], bank, ACT.Relu).then_inc(by_act, 1)
                        act.wait_ge(h_sq, i + (base + 1))
                        hold()
                        act.activation(H_hi[:, i, :], SQR[:, slot, :], ACT.Copy).then_inc(h_hi, 1)

                    ph = PLAN[f"up{l}{letter}"]
                    at_j = [0]

                    def tile(i, j):
                        at_j[0] = j
                        act.wait_ge(block_done, i + (ph.first + 1))
                        hidden(i, PS[:, j, :], None)

                    grouped(act, ph.tiles, tile, ACC)
                squares(f"down{l}b", 2 * l + 1)

            def embed(l):
                act.wait_ge(sq_added, KD * (2 * l + 3))
                act.dma_start(SQ[:], ple_in[l]).then_inc(ple_got, 16)
                layer_norm(2 * l + 1, f"mlp_g{l}", f"mlp_b{l}", f"ln{2 * l + 1}")
                act.wait_ge(ple_got, 16 * (l + 1))
                act.activation(P_hi[:], SQ[:], ACT.Copy).then_inc(p_hi, 1)
                sums(f"gate{l}", into(lambda i: GATE[:, i, :], ACT.Sigmoid, f"ple_b{l}"))
                for i in range(KD):
                    if l == 0:
                        split(X[:, i, :], i, "ple0", embedded, i + 1)
                    else:
                        act.wait_ge(embedded, KD + i + 1)
                        act.dma_start(out[i], X[:, i, :]).then_inc(out_done, 16)

            def rope(i, bank, at):
                if i >= 2:
                    act.wait_ge(roped, i - 1)
                act.activation(RAWQ[:, i % 2, :], bank, ACT.Identity, bias=param("b_rope", i)).then_inc(by_act, 1)

            angles()
            first_norm()
            sums("gates1", fox_gates)
            sums("qk1", fox_qk)
            head_sd(7)
            act.wait_ge(fox_rows, 3)
            for part in range(3):
                act.dma_start(NEG_C[part:part + 1, :, :], FF_PART[:, part, :]).then_inc(fox_gates_in, 16)
            sums("sbpool1", sb_pool)
            sums("v1", values(0))
            sums("silu1", into(lambda i: G1[:, i, :], ACT.Silu))
            pair = softmax_attention(FOX, fox_keys, (PR, PT, STAGE_Q, STAGE_K))
            act.wait_ge(qk_normed, 8)
            act.wait_ge(fox_gates_in, 48)
            act.wait_ge(pool_done, 2)
            place = lambda p: pair.place(p, QK[:, p, :], QK[:, p + 4, :])
            pair.place(0, QK[:, 0, :], QK[:, 4, :], first=True)
            pair(0, place, first=True)
            with act.Fori(1, 3) as p:
                pair(p, place)
            pair(3)
            stick_breaking()
            act.wait_ge(block_done, PLAN["out1"].last)
            for k in range(KD):
                split(X[:, k, :], k, 2, by_dve, PLAN["out1"].before + k + 1)
            sums("gates2", memory_gates)
            sums("qk2", into(lambda i: MQK[:, 2 * i if i < M_HEADS else 2 * (i - M_HEADS) + 1, :], ACT.Copy))
            sums("v2", values(6))
            sums("o2", into(lambda i: O2[:, i, :], ACT.Sigmoid))
            matrix_memory()
            squares("out2", 0)
            layer_norm(0, "mix_g0", "mix_b0", "ln0")
            mlp(0)
            embed(0)
            sums("rope3", rope)
            sums("v3", values(14, True))
            act.wait_ge(roped, 10)
            pair = softmax_attention(SWA, swa_keys, (PR3, PT3, STAGE_Q3, None), 24, lambda p: PARAM[:, sinks_at(p)])
            place = lambda p: pair.place(p, QK3[:, p + 2, :])
            pair.place(0, QK3[:, 2, :], first=True)
            pair(0, place, first=True)
            with act.Fori(1, 7) as p:
                own.enter(p - 1, 1)
                pair(p, place)
                own.leave(6)
            pair(7)
            pair.mixed(7)
            squares("out3", 2)
            layer_norm(2, "mix_g1", "mix_b1", "ln2")
            mlp(1)
            embed(1)
            act.wait_ge(out_done, 16 * KD)

        @block.vector
        def _(dve):
            own = Own(dve, dve_own)

            def low_part(k, stage_at, source):
                dve.wait_ge(a_hi, k + (stage_at + 1))
                dve.tensor_tensor(A_lo[:, k, :], source, A_hi[:, k, :].bitcast(F32), ALU.subtract).then_inc(a_lo, 1)

            def prepare():
                dve.memset(MEAN[:], 1.0)
                dve.memset(SQSUM[:], 0.0)
                dve.memset(PX[:, :, 0:PAD], 0.0)
                dve.memset(HOLD_ACT[:], 0.0)
                dve.memset(EPS_COL[:, 1:2], LN_EPS)
                dve.memset(EPS_COL[:, 0:1], EPS).then_inc(zeroed, 1)
                dve.wait_ge(zeroed, 1)

            def angles():
                two_pi, magic = 2 * np.pi, 1.5 * 2.0 ** 23
                c1 = 6.28125
                c2 = float(np.float32(round((two_pi - c1) * 2 ** 24) / 2 ** 24))
                c2 = float(np.floor((two_pi - c1) * 2 ** 21) / 2 ** 21)
                c3 = float(two_pi - c1 - c2)
                dve.wait_ge(pos_in, 16)
                dve.tensor_copy(POS_F[:], POS_I[:]).then_inc(pos_float, 1)
                dve.wait_ge(pos_wide, 1)
                own(dve.tensor_scalar(ANG[:], PS[:, 6, :], const("inv_freq"), None, ALU.mult))
                own.wait()
                own(dve.tensor_scalar(TURN[:], ANG[:], 1.0 / two_pi, magic, ALU.mult, ALU.add))
                own.wait()
                own(dve.tensor_scalar(TURN[:], TURN[:], magic, None, ALU.subtract))
                own.wait()
                for c in (c1, c2, c3):
                    own(dve.scalar_tensor_tensor(out=ANG[:], in0=TURN[:], scalar=-c, in1=ANG[:], op0=ALU.mult, op1=ALU.add))
                    own.wait()
                top = float(np.nextafter(np.float32(np.pi), np.float32(0)))
                own(dve.tensor_scalar(ANG[:], ANG[:], top, -top, ALU.min, ALU.max))
                own.wait()
                own(dve.tensor_scalar(ROT_TMP[:], ANG[:], float(np.pi / 2), -two_pi, ALU.is_gt, ALU.mult))
                own.wait()
                dve.scalar_tensor_tensor(out=TURN[:], in0=ANG[:], scalar=float(np.pi / 2), in1=ROT_TMP[:], op0=ALU.add,
                                         op1=ALU.add).then_inc(angle_ready, 1)
                dve.wait_ge(angle_ready, 1)
                dve.tensor_scalar(TURN[:], TURN[:], top, -top, ALU.min, ALU.max).then_inc(angle_ready, 1)

            def add_square(i, n_before):
                dve.wait_ge(sq_ready, n_before + i + 1)
                if i:
                    dve.wait_ge(sq_added, n_before + i)
                dve.tensor_tensor(SQSUM[:], SQSUM[:], SQ[:, i % 2, :], ALU.add).then_inc(sq_added, 1)

            def mix_slot(k, stage_at):
                if k >= 2:
                    dve.wait_ge(a_lo, stage_at + k - 1)

            def diagonals(n):
                rstd = SMALL[:, 48:52]
                dve.wait_ge(sd_ready, n + 1)
                own(dve.reciprocal(rstd, rstd))
                own.wait()
                for t in range(NT):
                    dve.tensor_scalar(RSTD[:, t * P:t * P + P], const("ident"), SMALL[:, 48 + t:49 + t], None,
                                      ALU.mult).then_inc(diag_ready, 1)

            def first_norm():
                for k in range(KD):
                    add_square(k, 0)
                diagonals(0)
                dve.wait_ge(rstd_ready, 1)
                for k in range(KD):
                    mix_slot(k, 0)
                    dve.scalar_tensor_tensor(out=MIX[:, k % 2, :], in0=X[:, k, :], scalar=param("norm_g", k), in1=PS[:, 6, :],
                                             op0=ALU.mult, op1=ALU.mult).then_inc(mix_ready, 1)
                    if k:
                        low_part(k - 1, 0, MIX[:, (k - 1) % 2, :])
                low_part(KD - 1, 0, MIX[:, (KD - 1) % 2, :])

            def running_sum(out, rows_in):
                n = out.shape[0]
                return dve.tensor_tensor_scan(out, MEAN[0:n, :], rows_in, 0.0, ALU.mult, ALU.add)

            def fox_gates():
                dve.wait_ge(fox_soft, 1)
                own(dve.scalar_tensor_tensor(out=FF[:, 2, :], in0=FF[:, 0, :], scalar=0.0, in1=FF[:, 1, :], op0=ALU.min,
                                             op1=ALU.subtract))
                own.wait()
                own(running_sum(FF[:, 1, :], FF[:, 2, :]))
                own.wait()
                own(dve.tensor_scalar(FF[:, 0, :], FF[:, 1, :], -1.0, None, ALU.mult))
                own.wait()
                for part in range(3):
                    dve.tensor_copy(FF_PART[:, part, :], FF[:, 0, :]).then_inc(fox_rows, 1)
                    if part < 2:
                        dve.wait_ge(fox_rows, part + 1)
                        own(dve.tensor_tensor(FF[:, 0, :], FF[:, 0, :], FF_PART[:, part, :], ALU.subtract))
                        own.wait()

            def fox_qk():
                for i in range(8):
                    dve.wait_ge(qk_sd, i + 1)
                    own(dve.reciprocal(MIX[:, i % 2, :], MIX[:, i % 2, :]))
                    own.wait()
                    g = GK[:, 0:1] if i < 4 else param("k_norm_g")
                    dve.scalar_tensor_tensor(out=QK[:, i, :], in0=QK[:, i, :], scalar=g, in1=MIX[:, i % 2, :],
                                             op0=ALU.mult, op1=ALU.mult).then_inc(qk_normed, 1)

            def store_values(at_v, n, dst):
                for i in range(n):
                    dve.wait_ge(turned, at_v + i + 1)
                    dve.tensor_copy(dst(i), PS[:, 4 + i % 2, :].rearrange("p (t f) -> p t f", t=NT)).then_inc(v_ready, 1)

            def softmax_attention(S, keys, O_, a_at, sinks, gate):

                def pair(p, first_pair=False):
                    def u(n):
                        return p * 8 + n

                    def finish(n):
                        h, i = n // NT, n % NT
                        dve.wait_ge(S.weighed, u(n) + 1)
                        total = SMALL[:, 4 + n % 4:5 + n % 4]
                        if sinks:
                            own(dve.tensor_tensor(total, total, SMALL[:, 8 + n % 4:9 + n % 4], ALU.add))
                            own.wait()
                        own(dve.reciprocal(SMALL[:, 14 + n % 2:15 + n % 2], total))
                        own.wait()
                        dve.tensor_scalar(O_[:, i, h * HD:h * HD + HD], PS[:, n % 2, 0:HD], SMALL[:, 14 + n % 2:15 + n % 2],
                                          None, ALU.mult).then_inc(S.o_read, 1)

                    for n in range(8):
                        first, width = keys(n % NT)
                        dve.wait_ge(S.scored, u(n) + 1)
                        dve.tensor_reduce(SMALL[:, 12 + n % 2:13 + n % 2], PS[:, 3 + n % 3, 0:width],
                                          mybir.AxisListType.X, ALU.max).then_inc(S.scores_read, 1)
                        dve.wait_ge(S.scores_read, u(n) + 1)
                        if sinks:
                            dve.tensor_scalar(SMALL[:, n % 4:n % 4 + 1], SMALL[:, 12 + n % 2:13 + n % 2],
                                              sinks(p, n // NT), -1.0, ALU.max, ALU.mult).then_inc(S.maxed, 1)
                        else:
                            dve.tensor_scalar(SMALL[:, n % 4:n % 4 + 1], SMALL[:, 12 + n % 2:13 + n % 2],
                                              -1.0, None, ALU.mult).then_inc(S.maxed, 1)
                        if n == 2 and not first_pair:
                            mix(p - 1)
                        if n == 4 and not first_pair and not gate:
                            low_part(p - 1, a_at, MIX[:, 0, :])
                        if n >= 3:
                            finish(n - 3)
                    for n in (5, 6, 7):
                        finish(n)

                def mix(p):
                    if not gate:
                        dve.wait_ge(a_lo, p + a_at)
                    dve.wait_ge(S.pair_turned, p + 1)
                    if gate:
                        dve.tensor_tensor(mixed1(p), PS[:, 2, :], gate(p), ALU.mult).then_inc(mix_ready, 1)
                    else:
                        dve.tensor_copy(MIX[:, 0, :], PS[:, 2, :]).then_inc(mix_ready, 1)

                def mixed(p):
                    mix(p)
                    low_part(p, a_at, MIX[:, 0, :])

                pair.mix, pair.mixed = mix, mixed
                return pair

            def pool():
                dve.wait_ge(fox_gates_in, 48)
                dve.wait_ge(by_act, PLAN["v1"].act_before)
                own(dve.memset(WIN[:, :, 0:PAD], 0.0))
                for c in range(2):
                    src, dst = PX[:, c, :], 0
                    steps = POOL_WINDOWS[2 * c + 1].bit_length() - 1
                    for s in range(steps):
                        rows = slice(HD, P) if s == steps - 1 else slice(0, P)
                        own.wait()
                        own(dve.tensor_tensor(WIN[rows, dst, PAD:], src[rows, PAD:], src[rows, PAD - 2 ** s:PAD + T - 2 ** s],
                                              ALU.add))
                        src, dst = WIN[:, dst, :], 1 - dst
                    own.wait()
                    wide, narrow = 1 - dst, dst
                    own(dve.tensor_scalar(POOLED[0:HD, c, :], WIN[0:HD, narrow, PAD:],
                                          const("inv_window", 1, slice(0, HD), c), None, ALU.mult))
                    own(dve.tensor_scalar(POOLED[HD:P, c, :], WIN[HD:P, wide, PAD:],
                                          const("inv_window", 1, slice(HD, P), c), None, ALU.mult))
                    own.wait()
                    own(dve.tensor_tensor(POOLED[:, c, 0:PAD], POOLED[:, c, 0:PAD], const("count_fix", PAD, skip=c * PAD),
                                          ALU.mult))
                    own.wait()
                    dve.tensor_tensor(POOLED[:, c, :], POOLED[:, c, :], PX[:, c, PAD:], ALU.subtract).then_inc(pooled, 1)

            def pool_outputs():
                for c in range(2):
                    dve.wait_ge(pool_done, c + 1)
                    own(dve.tensor_scalar(PX[:, c, PAD:], PS[:, 6 + c, :], param("pool_scale", c), None, ALU.mult))

            def stick_breaking():
                def softplus(h):
                    dve.wait_ge(sb_soft, h + 1)
                    if h >= 2:
                        dve.wait_ge(sb_summed, h - 1)
                    dve.scalar_tensor_tensor(out=sb_cols(SP_T, h), in0=sb_scores(h), scalar=0.0, in1=sb_cols(ATT, h),
                                             op0=ALU.max, op1=ALU.add).then_inc(sb_sp1, 1)
                    dve.wait_ge(sb_sp1, h + 1)
                    for j in range(NT):
                        diagonal = sb_cols(SP_T, h, j)[:, 0:P]
                        dve.tensor_tensor(diagonal, diagonal, const("before_mul"), ALU.mult).then_inc(sb_sp, 1)

                def low(k):
                    low_part(k, KD, mixed1(k))

                def mix(c):
                    dve.wait_ge(sb_weighed, 2 * c + 2)
                    dve.wait_ge(late_gates, 1)
                    dve.tensor_tensor(mixed1(6 + c), PS[:, 6 + c, :], G1[:, 6 + c, :], ALU.mult).then_inc(mix_ready, 1)

                softplus(0)
                softplus(1)
                for c in range(2):
                    dve.tensor_tensor(mixed1(4 + c), PX[:, c, PAD:], G1[:, 4 + c, :], ALU.mult).then_inc(mix_ready, 1)
                softplus(2)
                softplus(3)
                for k in range(6):
                    low(k)
                for c in range(2):
                    mix(c)
                    if c:
                        low(6)
                low(7)

            def residual(phase, n=None, scale=None, bias=None):
                ph = PLAN[phase]
                if n is not None:
                    own(dve.memset(SUM[:], 0.0))
                    own(dve.memset(SQSUM[:], 0.0))
                    own.wait()
                for i in range(KD):
                    if bias:
                        own(dve.tensor_scalar(X[:, i, :], X[:, i, :], scale, param(bias, i), ALU.mult, ALU.add))
                        own.wait()
                    dve.wait_ge(block_done, ph.first + (i + 1) * ph.per_tile)
                    if scale and not bias:
                        dve.scalar_tensor_tensor(out=X[:, i, :], in0=X[:, i, :], scalar=scale, in1=PS[:, i % ACC, :],
                                                 op0=ALU.mult, op1=ALU.add).then_inc(by_dve, 1)
                    else:
                        dve.tensor_tensor(X[:, i, :], X[:, i, :], PS[:, i % ACC, :], ALU.add).then_inc(by_dve, 1)
                    if n is not None:
                        dve.wait_ge(by_dve, ph.before + i + 1)
                        if i:
                            dve.wait_ge(sum_added, KD * n + i)
                        dve.tensor_tensor(SUM[:], SUM[:], X[:, i, :], ALU.add).then_inc(sum_added, 1)
                        if i:
                            add_square(i - 1, KD * (n + 1))
                if n is not None:
                    add_square(KD - 1, KD * (n + 1))

            def layer_norm(n, stage_at):
                mean, square, var = SMALL[:, 48:52], SMALL[:, 52:56], SMALL[:, 56:60]

                def centre(k):
                    dve.tensor_tensor(X[:, k, :], X[:, k, :], PS[:, 4, :], ALU.subtract).then_inc(centred, 1)

                dve.wait_ge(stats_done, n + 2)
                own(dve.tensor_copy(mean, PS[:, 5, 0:NT]))
                own.wait()
                own(dve.tensor_tensor(square, mean, mean, ALU.mult))
                own.wait()
                own(dve.tensor_tensor(var, PS[:, 5, NT:2 * NT], square, ALU.subtract))
                own.wait()
                dve.tensor_scalar(var, var, 0.0, None, ALU.max).then_inc(var_ready, 1)
                dve.wait_ge(mean_ready, n + 1)
                centre(0)
                diagonals(n + 1)
                centre(1)
                dve.wait_ge(rstd_ready, n + 2)
                for k in range(KD):
                    dve.wait_ge(centred, KD * n + k + 1)
                    dve.tensor_tensor(X[:, k, :], X[:, k, :], PS[:, 6, :], ALU.mult).then_inc(normed, 1)
                    if k + 2 < KD:
                        centre(k + 2)
                    if k:
                        low_part(k - 1, stage_at, X[:, k - 1, :])
                low_part(KD - 1, stage_at, X[:, KD - 1, :])

            def mlp(l):
                for half, letter in enumerate("ab"):
                    base, ph = HALF_FF * (2 * l + half), PLAN[f"up{l}{letter}"]

                    def tile(i, j):
                        slot = j % 2
                        dve.wait_ge(by_act, i + (ph.before + 1))
                        if not early(i, 2):
                            dve.wait_ge(h_lo, i + (base - 1))
                        dve.tensor_tensor(SQR[:, slot, :], RELU[:, slot, :], RELU[:, slot, :], ALU.mult).then_inc(h_sq, 1)
                        dve.wait_ge(h_hi, i + (base + 1))
                        dve.tensor_tensor(H_lo[:, i, :], SQR[:, slot, :], H_hi[:, i, :].bitcast(F32),
                                          ALU.subtract).then_inc(h_lo, 1)

                    grouped(dve, ph.tiles, tile, ACC)
                    if half == 0:
                        residual(f"down{l}a", None, ALPHA)
                    else:
                        residual(f"down{l}b", 2 * l + 1)

            def embed(l):
                dve.wait_ge(p_hi, l + 1)
                dve.tensor_tensor(P_lo[:], SQ[:], P_hi[:].bitcast(F32), ALU.subtract).then_inc(p_lo, 1)
                ph = PLAN[f"proj{l}"]
                for i in range(KD):
                    if i % 4 == 3:
                        dve.wait_ge(block_done, ph.first + i // 4 + 1)
                    else:
                        dve.wait_ge(proj_part, 6 * l + i // 4 * 3 + i % 4 + 1)
                    dve.tensor_tensor(GATE[:, i, :], GATE[:, i, :], PS[:, i % ACC, :], ALU.mult).then_inc(by_dve, 1)
                    dve.wait_ge(by_dve, ph.before + i + 1)
                    dve.tensor_tensor(X[:, i, :], X[:, i, :], GATE[:, i, :], ALU.add).then_inc(embedded, 1)
                    if l == 0 and i:
                        low_part(i - 1, KD * A_STAGE["ple0"], X[:, i - 1, :])
                if l == 0:
                    low_part(KD - 1, KD * A_STAGE["ple0"], X[:, KD - 1, :])

            def memory_gates():
                fg = slice(32, 32 + M_HEADS)
                dve.wait_ge(m_tanh, 1)
                dve.tensor_scalar(MG[:, 2, :], MG[:, 1, :], CAP, None, ALU.mult).then_inc(m_capped, 1)
                dve.wait_ge(m_soft, 1)
                dve.scalar_tensor_tensor(out=MG[fg, 1, :], in0=MG[fg, 2, :], scalar=0.0, in1=MG[fg, 0, :], op0=ALU.min,
                                         op1=ALU.subtract).then_inc(m_log_f, 1)
                dve.wait_ge(m_shifted, 1)
                own(running_sum(ROWS[:, 1, :], ROWS[:, 3, :]))
                own.wait()
                own(dve.tensor_tensor(ROWS[:, 0, :], MG[0:M_HEADS, 2, :], ROWS[:, 1, :], ALU.subtract))
                own.wait()
                own(dve.tensor_tensor_scan(ROWS[:, 2, :], ROWS[:, 0, :], ROWS[:, 0, :], 0.0, ALU.max, ALU.max))
                own.wait()
                own(dve.tensor_tensor(ROWS[:, 3, :], ROWS[:, 1, :], ROWS[:, 2, :], ALU.add))
                own(dve.memset(V2[:, :, :, M_DV:M_DV + 1], 1.0))
                dve.tensor_scalar(ROWS[:, 2, :], ROWS[:, 2, :], -1.0, None, ALU.mult).then_inc(m_rows, 1)

            def matrix_memory():
                dve.wait_ge(m_cols, 1)
                dve.wait_ge(m_spread_read, M_HEADS)

                def head(h, first=False):
                    for j in range(NT):
                        dve.tensor_tensor(DIAG[:, j, :], NEG_M[:, h, j * P:j * P + P], const("past_add"),
                                          ALU.add).then_inc(m_diag, 1)
                    for j in range(NT):
                        dve.wait_ge(m_scored, h * NT + j + 1)
                        dve.wait_ge(m_dec, h * (2 * NT - 1) + min(2 * j + 2, 2 * NT - 1))
                        dve.scalar_tensor_tensor(out=DEC[:, j, 0:T - j * P], in0=PS[:, j, 0:T - j * P],
                                                 scalar=float(M_DK ** -0.5), in1=DEC[:, j, 0:T - j * P], op0=ALU.mult,
                                                 op1=ALU.mult).then_inc(m_w, 1)
                    for i in range(NT):
                        e = MCOL[:, i, 1, h:h + 1] if first else MCOL[:, i, 1, bass.ds(h, 1)]
                        den, mag = SMALL[:, 32 + i:33 + i], SMALL[:, 36 + i:37 + i]
                        dve.wait_ge(m_weighed, h * NT + i + 1)
                        own(dve.tensor_copy(den, PS[:, 4 + i, M_DV:M_DV + 1]))
                        own.wait()
                        own(dve.scalar_tensor_tensor(out=mag, in0=den, scalar=-1.0, in1=den, op0=ALU.mult, op1=ALU.max))
                        own.wait()
                        own(dve.tensor_tensor(mag, mag, e, ALU.max))
                        own.wait()
                        own(dve.reciprocal(mag, mag))
                        own.wait()
                        row = H2F[:, h, i, :]
                        dve.tensor_scalar(row, PS[:, 4 + i, 0:M_DV], mag, None, ALU.mult).then_inc(m_h, 1)
                        dve.wait_ge(m_h, h * NT + i + 1)
                        own(dve.bn_stats(STATS[:, h, i, :], row))

                head(0, True)
                with dve.Fori(1, M_HEADS) as h:
                    own.enter(h - 1, 5 * NT)
                    head(h)
                    own.leave(M_HEADS - 1)
                own.wait()
                for h in range(M_HEADS):
                    for i in range(NT):
                        ins = dve.bn_aggr(AGGR[:, h, i, :], STATS[:, h, i, :])
                ins.then_inc(m_aggr, 1)
                dve.wait_ge(m_sd, 1)
                own(dve.reciprocal(SMALL[:, 16:32], SMALL[:, 16:32]))
                own.wait()
                for h in range(M_HEADS):
                    for i in range(NT):
                        r = 16 + h * NT + i
                        dve.tensor_scalar(H2F[:, h, i, :], H2F[:, h, i, :], AGGR[:, h, i, 0:1], SMALL[:, r:r + 1],
                                          ALU.subtract, ALU.mult).then_inc(m_normed, 1)
                for f in range(KD):
                    dve.wait_ge(m_turned, f + 1)
                    mix_slot(f, 24)
                    dve.scalar_tensor_tensor(out=MIX[:, f % 2, :], in0=PS[:, 4 + f % 2, :], scalar=param("head_g", f),
                                             in1=O2[:, f, :], op0=ALU.mult, op1=ALU.mult).then_inc(mix_ready, 1)
                    if f:
                        low_part(f - 1, 24, MIX[:, (f - 1) % 2, :])
                low_part(KD - 1, 24, MIX[:, (KD - 1) % 2, :])

            def rope():
                ph = PLAN["rope3"]
                for i in range(10):
                    s = 1.0 if i < 2 else QK_SCALE
                    dve.wait_ge(rope_swapped, i + 1)
                    own(dve.scalar_tensor_tensor(out=QK3[:, i, :], in0=RAWQ[:, i % 2, :], scalar=s, in1=COS[:],
                                                 op0=ALU.mult, op1=ALU.mult))
                    if i:
                        dve.wait_ge(roped, i)
                    own(dve.scalar_tensor_tensor(out=ROT[:], in0=PS[:, 4 + i % 2, :], scalar=s, in1=SIN[:],
                                                 op0=ALU.mult, op1=ALU.mult))
                    own.wait()
                    dve.tensor_tensor(QK3[:, i, :], QK3[:, i, :], ROT[:], ALU.add).then_inc(roped, 1)

            prepare()
            dve.wait_ge(c_in, 32)
            dve.tensor_copy(IDENT_B[:], const("ident"))
            dve.tensor_copy(FOX_MASK_B[:], const("fox_mask"))
            dve.tensor_copy(BEFORE_B[:], const("before_add"))
            dve.tensor_copy(BAND_MASK_B[:], const("band_mask"))
            dve.tensor_copy(ONE_B[:], const("one", P, slice(0, 3)))
            own(dve.tensor_scalar(GK[:, 0:1], param("q_norm_g"), QK_SCALE, None, ALU.mult))
            angles()
            first_norm()
            fox_gates()
            fox_qk()
            pool()
            store_values(0, 6, lambda i: V1[:, :, i, :])
            pool_outputs()
            pair = softmax_attention(FOX, fox_keys, O_T, 8, None, lambda p: G1[:, p, :])
            dve.wait_ge(by_act, PLAN["late1"].before)
            pair(0, True)
            with dve.Fori(1, 4) as p:
                own.enter(p - 1, 8)
                pair(p)
                own.leave(3)
            own.wait()
            pair.mix(3)
            stick_breaking()
            residual("out1")
            for k in range(KD):
                low_part(k, KD * A_STAGE["x1"], X[:, k, :])
            memory_gates()
            store_values(6, 8, lambda i: V2[:, :, i // 2, i % 2 * P:i % 2 * P + P])
            matrix_memory()
            residual("out2", 0, ALPHA)
            layer_norm(0, KD * A_STAGE["ln0"])
            mlp(0)
            layer_norm(1, KD * A_STAGE["ln1"])
            embed(0)
            dve.wait_ge(angle_done, 1)
            rope()
            store_values(14, 2, lambda i: V3[:, :, i, :])

            pair = softmax_attention(SWA, swa_keys, O_T3, KD * A_STAGE["mixed3"], lambda p, h: PARAM[:, sink_at(p, h)],
                                     None)
            pair(0, True)
            with dve.Fori(1, 8) as p:
                own.enter(p - 1, 16)
                pair(p)
                own.leave(7)
            pair.mixed(7)
            residual("out3", 2, ALPHA, "b_o")
            layer_norm(2, KD * A_STAGE["ln2"])
            mlp(1)
            layer_norm(3, KD * A_STAGE["ln3"])
            embed(1)


def _blocks(w):
    k, m = w.shape
    if m % P:
        w = np.concatenate([w, np.zeros((k, P - m % P), w.dtype)], 1)
        m = w.shape[1]
    return w.reshape(k // D, KD, P, m // P, P).transpose(3, 0, 2, 1, 4).reshape(-1, P, D)


def _columns(v):
    return np.asarray(v).reshape(-1, P).T


def lay_out(a):
    a = {k: np.asarray(v) for k, v in a.items()}
    wi = a["w_in"][0]
    edges = np.cumsum([0, 512, 512, 512, 512, 8, 256, 256, 256, 256, 256, 256])
    fq, fk, fv, fg, ff, px, pg, sq, sk, sv, sg = (wi[:, s:e] for s, e in zip(edges[:-1], edges[1:]))
    wm = a["a_w_in_2"][0]
    gates2 = np.zeros((D, P), wm.dtype)
    gates2[:, 0:4] = wm[:, 3072:3076]
    gates2[:, 32:36] = wm[:, 3076:3080]
    q_cols = np.concatenate([np.arange(h * HD, h * HD + HD) for h in Q_ORDER])
    stream = [_blocks(w) for w in (ff, fq, fk, sq, sk, px, fv, sv, fg, pg, sg, a["w_out"][0], gates2,
                                   wm[:, 0:3072], a["a_w_out_2"][0])]

    def mlp(l):
        up, down = a["mlp_w_up_2"][l], a["mlp_w_down_2"][l]
        half = D_FF // 2
        for s in (0, half):
            yield _blocks(up[:, s:s + half])
            yield _blocks(down[s:s + half])
        yield _blocks(a["ple_w_gate_2"][l])
        w = a["ple_w_proj_2"][l].reshape(2, P, 2, 4, P)
        yield w.transpose(2, 1, 3, 0, 4).reshape(2, P, D)

    stream += list(mlp(0))
    stream += [_blocks(w) for w in (a["kv_w_2"][:, 0:256], a["b_w_q_2"][0][:, q_cols], a["kv_w_2"][:, 256:512],
                                    a["b_w_o_2"][0][q_cols])]
    stream += list(mlp(1))

    def col(v, at=0):
        c = np.zeros((P, 1), np.float32)
        c[at:at + v.size, 0] = v
        return c

    b_gates = col(a["a_b_igate_2"][0])
    b_gates[32:36, 0] = a["a_b_fgate_2"][0]
    pool = np.zeros((P, 2, P), np.float32)
    for g in range(POOL_GROUPS):
        r = slice(g % 2 * HD, g % 2 * HD + HD)
        pool[r, g // 2, r] = a["w_pool"][0, g]
    sinks = np.broadcast_to(a["b_sinks_2"][0][np.array(Q_ORDER)][None, :], (P, Q_HEADS))
    parts = {
        "norm_g": _columns(a["norm_g"]), "b_f": col(a["b_f"][0]),
        "q_norm_g": np.concatenate([a["q_norm_g"][0]] * 2)[:, None],
        "k_norm_g": np.concatenate([a["k_norm_g"][0]] * 2)[:, None],
        "pool_scale": _columns(a["pool_scale"]), "b_gates": np.concatenate([b_gates, b_gates], 1),
        "head_g": _columns(a["a_head_norm_g_2"]),
        "b_rope": _columns(np.concatenate([a["kv_b_2"][0:256], a["b_b_q_2"][0][q_cols]])),
        "b_v": _columns(a["kv_b_2"][256:512]), "sinks": sinks, "b_o": _columns(a["b_b_o_2"]),
        "w_pool": pool.reshape(P, -1),
    }
    for l in range(2):
        parts[f"mix_g{l}"] = _columns(a["mix_ln_g_2"][l])
        parts[f"mix_b{l}"] = _columns(a["mix_ln_b_2"][l])
        parts[f"mlp_g{l}"] = _columns(a["mlp_ln_g_2"][l])
        parts[f"mlp_b{l}"] = _columns(a["mlp_ln_b_2"][l])
        parts[f"ple_b{l}"] = _columns(a["ple_b_gate_2"][l])
    return {
        "x": np.ascontiguousarray(a["x"][0].T.reshape(KD, P, T).transpose(1, 0, 2)),
        "weights": np.concatenate(stream, 0),
        "constants": CONSTANTS,
        "params": np.ascontiguousarray(np.concatenate([parts[n] for n, _ in PARAM_WIDTHS], 1)),
        "positions": np.ascontiguousarray(a["positions_2"]),
        "ple_in": np.ascontiguousarray(a["p_2"][:, 0].transpose(0, 2, 1).reshape(2, 2, P, T).transpose(0, 2, 1, 3)),
    }


def kernel(**inputs):
    import concourse.bacc as bacc
    from concourse.bass_utils import run_bass_kernel_spmd

    nc = bacc.Bacc("TRN2", target_bir_lowering=False, num_devices=1)
    arrays, aps = {}, []
    for name, a in lay_out(inputs).items():
        arrays[f"in_{name}"] = a
        aps.append(nc.dram_tensor(f"in_{name}", a.shape, mybir.dt.from_np(a.dtype), kind="ExternalInput").ap())
    out = nc.dram_tensor("out", (KD, P, T), F32, kind="ExternalOutput").ap()
    build(nc, *aps, out)
    got = run_bass_kernel_spmd(nc, [arrays], core_ids=[0]).results[0]["out"]
    return np.ascontiguousarray(np.asarray(got).reshape(D, T).T)[None]
```

```python
from contextlib import ExitStack

import numpy as np

import concourse.bass as bass
from concourse import mybir

F32 = mybir.dt.float32
F32R = mybir.dt.float32r
I32 = mybir.dt.int32
BF16 = mybir.dt.bfloat16
ACT = mybir.ActivationFunctionType
ALU = mybir.AluOpType

P = 128
T = 512
NT = T // P
D = 1024
KD = D // P
D_FF = 4 * D
HALF_FF = D_FF // 2 // P
HD = 64
FOX_HEADS, SB_HEADS, POOL_GROUPS = 8, 4, 4
M_HEADS, M_DK, M_DV = 4, 128, 256
Q_HEADS = 16
POOL_WINDOWS = (2, 4, 8, 16)
PAD = POOL_WINDOWS[-1]
ROPE_DIM, ROPE_THETA = 16, 500000.0
ALPHA = float((2 * 2) ** 0.25)
EPS, LN_EPS, CAP = 1e-6, 1e-5, 15.0
QK_SCALE = HD ** -0.5
NEG = -1e30
RAW_SLOTS, W_SLOTS = 2, 4
X_PARTS = 4
WOVEN = 3
ACC = 4

PACKED_AT = {0: 0, 1: T, 3: T + 3 * P, 2: 2 * T}
PACKED = 2 * T + 2 * P

_MLP = [("up{0}a", 16, 1, "act"), ("down{0}a", 8, 2, "dve"), ("up{0}b", 16, 1, "act"), ("down{0}b", 8, 2, "dve"),
        ("proj{0}", 8, 0.25, "act"), ("gate{0}", 8, 1, "act")]
PHASES = [("qk1", 8, 1, "act"), ("gates1", 1, 1, "act"), ("sbpool1", 6, 1, "act"), ("v1", 6, 1, "act"),
          ("silu1", 6, 1, "act"), ("late1", 2, 1, "act"), ("out1", 8, 1, "dve"),
          ("gates2", 1, 1, "act"), ("qk2", 8, 1, "act"), ("v2", 8, 1, "act"), ("o2", 8, 1, "act"),
          ("out2", 8, 1, "dve")]
PHASES += [(n.format(0), t, b, e) for n, t, b, e in _MLP]
PHASES += [("rope3", 10, 1, "act"), ("v3", 2, 1, "act"), ("out3", 8, 1, "dve")]
PHASES += [(n.format(1), t, b, e) for n, t, b, e in _MLP]


class Phase:

    def __init__(self, first, tiles, per_tile, act_before, dve_before, reader):
        self.first, self.tiles, self.per_tile, self.reader = first, tiles, per_tile, reader
        self.blocks = int(tiles * per_tile)
        self.last = first + self.blocks
        self.act_before, self.dve_before = act_before, dve_before
        self.before = act_before if reader == "act" else dve_before


def plan():
    out, block, act, dve = {}, 0, 0, 0
    for name, tiles, per_tile, reader in PHASES:
        out[name] = Phase(block, tiles, per_tile, act, dve, reader)
        block += out[name].blocks
        act += tiles * (reader == "act")
        dve += tiles * (reader == "dve")
    return out, block


PLAN, N_BLOCKS = plan()

def constant_columns():
    r, c = np.arange(P)[:, None], np.arange(P)[None, :]
    rope = np.zeros((P, P), np.float32)
    half = ROPE_DIM // 2
    for head in (0, HD):
        for m in range(half):
            rope[head + m + half, head + m] = -1.0
            rope[head + m, head + m + half] = 1.0
    select = np.zeros((P, M_HEADS, P), np.float32)
    for h in range(M_HEADS):
        select[h, h] = 1.0
    inv_freq = np.zeros((P, 1), np.float32)
    freq = np.power(np.float32(ROPE_THETA), -np.arange(half, dtype=np.float32) * np.float32(2.0 / ROPE_DIM))
    for head in (0, HD):
        inv_freq[head:head + half, 0] = freq
        inv_freq[head + half:head + ROPE_DIM, 0] = freq
    window = np.repeat(np.array(POOL_WINDOWS, np.float32).reshape(2, 2).T, HD, axis=0)
    count = np.minimum(np.arange(PAD)[None, None, :] + 1.0, window[:, :, None])
    parts = {
        "ident": np.eye(P), "mean": np.ones((P, P)) / D, "one": np.ones((P, P)),
        "head_mean": (r // HD == c // HD) / HD, "rope": rope,
        "fox_mask": np.where(c <= r, 0.0, NEG),
        "band_mask": np.concatenate([np.where(c > r, 0.0, NEG), np.where(c <= r, 0.0, NEG)], 1),
        "past_add": np.where(r <= c, 0.0, NEG),
        "before_add": np.where(r < c, 0.0, NEG),
        "before_mul": r < c,
        "minus_later": -1.0 * (r >= c),
        "minus_one": -np.ones((P, P)),
        "select": select.reshape(P, -1), "inv_freq": inv_freq, "inv_window": 1.0 / window,
        "count_fix": (window[:, :, None] / count).reshape(P, -1),
    }
    at, cols = {}, []
    for name, a in parts.items():
        a = np.asarray(a, np.float32)
        at[name] = (sum(x.shape[1] for x in cols), a.shape[1])
        cols.append(a)
    return at, np.ascontiguousarray(np.concatenate(cols, 1))


CONST_AT, CONSTANTS = constant_columns()
FIRST_CONSTANTS = 3 * P

PARAM_WIDTHS = [("norm_g", 8), ("b_f", 1), ("q_norm_g", 1), ("k_norm_g", 1), ("pool_scale", 2), ("b_gates", 2),
                ("head_g", 8), ("b_rope", 10), ("b_v", 2), ("sinks", Q_HEADS), ("b_o", 8),
                ("mix_g0", 8), ("mix_b0", 8), ("mlp_g0", 8), ("mlp_b0", 8), ("ple_b0", 8),
                ("mix_g1", 8), ("mix_b1", 8), ("mlp_g1", 8), ("mlp_b1", 8), ("ple_b1", 8), ("w_pool", 2 * P)]
PARAM_AT = {}
for _name, _width in PARAM_WIDTHS:
    PARAM_AT[_name] = (sum(w for _, w in PARAM_AT.values()), _width)
N_PARAMS = sum(w for _, w in PARAM_WIDTHS)

Q_ORDER = [(2 * g + half) * 4 + j for g in range(2) for j in range(4) for half in range(2)]


def grouped(eng, n, step, group=4):
    full = n // group
    for i in range(min(n, group)):
        step(i, i)
    if full > 2:
        with eng.Fori(1, full) as g:
            for j in range(group):
                step(g * group + j, j)
    elif full == 2:
        for j in range(group):
            step(group + j, j)
    if full:
        for j in range(n - full * group):
            step(full * group + j, j)


def early(i, n):
    return isinstance(i, int) and i < n


def build(nc, x, weights, constants, params, positions, ple_in, out):
    with ExitStack() as ctx:
        def sb(name, shape, dt=F32, where=ctx):
            return where.enter_context(nc.sbuf_tensor(name, shape, dt))

        def sem(name):
            return ctx.enter_context(nc.semaphore(name))

        X = sb("X", [P, KD, T])
        A_hi = sb("A_hi", [P, KD, T], F32R)
        A_lo = sb("A_lo", [P, KD, T], F32R)
        W_raw = sb("W_raw", [P, RAW_SLOTS, KD * P])
        W_hi = sb("W_hi", [P, W_SLOTS, KD * P], F32R)
        W_lo = sb("W_lo", [P, W_SLOTS, KD * P], F32R)
        CONST = sb("CONST", [P, CONSTANTS.shape[1]])
        PARAM = sb("PARAM", [P, N_PARAMS])
        SUM, SQSUM = sb("SUM", [P, T]), sb("SQSUM", [P, T])
        SQ = sb("SQ", [P, 2, T])
        MEAN, RSTD = sb("MEAN", [P, T]), sb("RSTD", [P, T])
        COS, SIN = sb("COS", [P, T]), sb("SIN", [P, T])
        MIX = sb("MIX", [P, 2, T])
        SMALL = sb("SMALL", [P, 64])
        GK = sb("GK", [P, 1])
        EPS_COL = sb("EPS_COL", [P, 2])
        HOLD, HOLD_ACT = sb("HOLD", [1, 1 + W_SLOTS]), sb("HOLD_ACT", [1, 20])
        IDENT_B, FOX_MASK_B = sb("IDENT_B", [P, P], BF16), sb("FOX_MASK_B", [P, P], BF16)
        BEFORE_B, PAST_B = sb("BEFORE_B", [P, P], BF16), sb("PAST_B", [P, P], BF16)
        BAND_MASK_B, ONE_B = sb("BAND_MASK_B", [P, 2 * P], BF16), sb("ONE_B", [3, P], BF16)

        with ExitStack() as part:
            QK = sb("QK", [P, 8, T], F32, part)
            SBQ, SBK = sb("SBQ", [P, SB_HEADS, T], F32, part), sb("SBK", [P, 2, T], F32, part)
            PX = sb("PX", [P, 2, PAD + T], F32, part)
            V1 = sb("V1", [P, NT, 6, P], F32, part)
            with ExitStack() as sub:
                POS_I = sb("POS_I", [1, T], I32, sub)
                POS_F = sb("POS_F", [1, T], F32, sub)
                ANG, TURN = sb("ANG", [P, T], F32, sub), sb("TURN", [P, T], F32, sub)
                ROT_TMP = sb("ROT_TMP", [P, T], F32, sub)
            G1 = sb("G1", [P, 8, T], F32, part)
            with ExitStack() as sub:
                NEG_C = sb("NEG_C", [3, FOX_HEADS, T], BF16, sub)
                with ExitStack() as prelude:
                    FF = sb("FF", [FOX_HEADS, 3, T], F32, prelude)
                    FF_PART = sb("FF_PART", [FOX_HEADS, 3, T], BF16, prelude)
                with ExitStack() as prelude:
                    WIN = sb("WIN", [P, 2, PAD + T], F32, prelude)
                    POOLED = sb("POOLED", [P, 2, T], F32, prelude)
                STAGE_Q = sb("STAGE_Q", [P, 2, T], F32, sub)
                PR, PT = sb("PR", [P, 2, T], F32, sub), sb("PT", [P, 2, T], F32, sub)
                O_T = sb("O_T", [P, NT, P], F32, sub)
            with ExitStack() as sub:
                ATT = sb("ATT", [P, 2, PACKED], F32, sub)
                SP_T = sb("SP_T", [P, 2, PACKED], F32, sub)
        with ExitStack() as part:
            MQK = sb("MQK", [P, 8, T], F32, part)
            V2 = sb("V2", [P, NT, M_HEADS, M_DV + 1], F32, part)
            O2 = sb("O2", [P, 8, T], F32, part)
            MCOL = sb("MCOL", [P, NT, 2, M_HEADS], F32, part)
            DEC = sb("DEC", [P, M_HEADS, PACKED], F32, part)
            STATS = sb("STATS", [P, M_HEADS, NT, 6], F32, part)
            AGGR = sb("AGGR", [P, M_HEADS, NT, 2], F32, part)
            with ExitStack() as sub:
                MG = sb("MG", [36, 3, T], F32, sub)
                ROWS = sb("ROWS", [M_HEADS, 4, T], F32, sub)
        with ExitStack() as part:
            QK3 = sb("QK3", [P, 10, T], F32, part)
            V3 = sb("V3", [P, NT, 2, P], F32, part)
            RAWQ, ROT = sb("RAWQ", [P, 2, T], F32, part), sb("ROT", [P, T], F32, part)
            STAGE_Q3 = sb("STAGE_Q3", [P, 2, T], F32, part)
            PR3, PT3 = sb("PR3", [P, 2, T], F32, part), sb("PT3", [P, 2, T], F32, part)
            O_T3 = sb("O_T3", [P, NT, P], F32, part)
        with ExitStack() as part:
            H_hi = sb("H_hi", [P, HALF_FF, T], F32R, part)
            H_lo = sb("H_lo", [P, HALF_FF, T], F32R, part)
            RELU = sb("RELU", [P, 2, T], F32, part)
            with ExitStack() as sub:
                SQR = sb("SQR", [P, 2, T], F32, sub)
            P_hi = sb("P_hi", [P, 2, T], F32R, part)
            P_lo = sb("P_lo", [P, 2, T], F32R, part)
        with ExitStack() as part:
            GATE, PROJ = sb("GATE", [P, KD, T], F32, part), sb("PROJ", [P, KD, T], F32, part)

        PS = ctx.enter_context(nc.psum_tensor("PS", [P, 8, T], F32))

        def const(name, width=None, row=slice(None), skip=0):
            at, full = CONST_AT[name]
            return CONST[row, at + skip:at + skip + (width or full)]

        def param(name, i=0, rows=slice(None)):
            at = PARAM_AT[name][0]
            return PARAM[rows, at + i:at + i + 1]

        x_in = [sem(f"x_in{part}") for part in range(X_PARTS)]
        c_in, c_rest, p_in, pos_in, ple_got, out_done = (sem(n) for n in (
            "c_in", "c_rest", "p_in", "pos_in", "ple_got", "out_done"))
        w_in = [sem(f"w_in{s}") for s in range(RAW_SLOTS)]
        w_hi, w_lo = sem("w_hi"), sem("w_lo")
        block_done = sem("block_done")
        sums_read = {"act": sem("sums_read_act"), "dve": sem("sums_read_dve")}
        by_act, by_dve = sums_read["act"], sums_read["dve"]
        a_hi, a_lo = sem("a_hi"), sem("a_lo")
        h_sq, h_hi, h_lo = sem("h_sq"), sem("h_hi"), sem("h_lo")
        p_hi, p_lo = sem("p_hi"), sem("p_lo")
        sq_ready, sum_added, sq_added = sem("sq_ready"), sem("sum_added"), sem("sq_added")
        stats_done, mean_ready = sem("stats_done"), sem("mean_ready")
        var_ready, sd_ready = sem("var_ready"), sem("sd_ready")
        diag_ready, rstd_ready = sem("diag_ready"), sem("rstd_ready")
        centred, normed, x_ready = sem("centred"), sem("normed"), sem("x_ready")
        act_own, dve_own = sem("act_own"), sem("dve_own")
        turned = sem("turned")
        v_ready = sem("v_ready")
        zeroed, hold_set = sem("zeroed"), sem("hold_set")
        stage_zeroed = sem("stage_zeroed")
        mix_ready = sem("mix_ready")
        gated = sem("gated")
        embedded = sem("embedded")
        proj_part = sem("proj_part")
        pos_float, pos_wide = sem("pos_float"), sem("pos_wide")
        angle_ready, angle_done = sem("angle_ready"), sem("angle_done")
        qk_sq, qk_ms, qk_sd, qk_normed = sem("qk_sq"), sem("qk_ms"), sem("qk_sd"), sem("qk_normed")
        fox_soft, fox_rows, fox_gates_in = sem("fox_soft"), sem("fox_rows"), sem("fox_gates_in")
        pooled, pool_done = sem("pooled"), sem("pool_done")
        sb_scored, sb_soft, sb_sp1, sb_sp, sb_summed, sb_att, sb_weighed = (
            sem("sb_" + n) for n in ("scored", "soft", "sp1", "sp", "summed", "att", "weighed"))
        m_tanh, m_capped, m_soft, m_log_f, m_shifted, m_rows, m_cols_turned, m_cols = (
            sem("m_" + n) for n in ("tanh", "capped", "soft", "log_f", "shifted", "rows", "cols_turned", "cols"))
        m_spread, m_dec, m_scored, m_w, m_weighed, m_den_read, m_var, m_sd, m_normed, m_turned = (
            sem("m_" + n) for n in ("spread", "dec", "scored", "w", "weighed", "den_read", "var", "sd", "normed", "turned"))
        late_gates = sem("late_gates")
        rope_swapped, roped = sem("rope_swapped"), sem("roped")

        class Attention:

            def __init__(self, name):
                self.staged = sem(name + "_staged")
                self.scored = sem(name + "_scored")
                self.scores_read = sem(name + "_scores_read")
                self.maxed = sem(name + "_maxed")
                self.sink_in = sem(name + "_sink_in")
                self.sinked = sem(name + "_sinked")
                self.exped = sem(name + "_exped")
                self.turned = sem(name + "_turned")
                self.turned_read = sem(name + "_turned_read")
                self.weighed = sem(name + "_weighed")
                self.o_read = sem(name + "_o_read")
                self.pair_turned = sem(name + "_pair_turned")

        FOX, SWA = Attention("fox"), Attention("swa")

        def fox_keys(i):
            return 0, (i + 1) * P

        def swa_keys(i):
            return (0, P) if i == 0 else ((i - 1) * P, 2 * P)

        def sink_at(p, h):
            at = PARAM_AT["sinks"][0]
            if isinstance(p, int):
                return slice(at + 2 * p + h, at + 2 * p + h + 1)
            return bass.ds(p * 2 + (at + h), 1)

        def packed_scores(h, j=None, skip=0):
            banks = PS[:, 3:6, :] if h % 2 == 0 else PS[:, 0:3, :]
            flat = banks.rearrange("p b t -> p (b t)")
            return flat[:, 0:PACKED] if j is None else flat[:, PACKED_AT[j] + skip:PACKED_AT[j] + T - j * P]

        def packed(buffer, slot, j=None, skip=0, width=None):
            if j is None:
                return buffer[:, slot, :]
            at = PACKED_AT[j] + skip
            return buffer[:, slot, at:at + (width or T - j * P - skip)]

        def spread_bank(h):
            return 4 + 2 * (h % 2)

        def memory_out(h, i):
            return PS[:, 4 + 2 * (h % 2) + i // 2, i % 2 * M_DV:i % 2 * M_DV + M_DV]

        TURNED_BANK = [0, 1, 2, 4, 5, 3, 6, 7]

        def mixed1(k):
            return QK[:, k, :] if not isinstance(k, int) or k < 4 else G1[:, k, :]

        H2F = MQK[:].rearrange("p a t -> p (a t)").rearrange("p (h i c) -> p h i c", h=M_HEADS, i=NT)

        class Own:

            def __init__(self, eng, s):
                self.eng, self.s, self.n = eng, s, 0
                self.loop, self.start, self.per = None, 0, 0

            def __call__(self, ins):
                ins.then_inc(self.s, 1)
                self.n += 1

            def wait(self):
                n = self.n
                if self.loop is not None:
                    n = self.start + (self.n - self.start) + self.loop * self.per
                self.eng.wait_ge(self.s, n)

            def enter(self, loop, per):
                self.loop, self.start, self.per = loop, self.n, per

            def leave(self, rounds):
                assert self.n - self.start == self.per, (self.n - self.start, self.per)
                self.n = self.start + rounds * self.per
                self.loop = None

        A_STAGE = {n: i for i, n in enumerate(["norm", "mixed1", "x1", "mixed2", "ln0", "ln1", "ple0", "mixed3",
                                               "ln2", "ln3"])}

        block = ctx.enter_context(nc.Block())

        @block.sync
        def _(sp):
            for part in range(X_PARTS):
                tiles = slice(part * KD // X_PARTS, (part + 1) * KD // X_PARTS)
                sp.dma_start(X[:, tiles, :], x[:, tiles, :]).then_inc(x_in[part], 16)
                if part == 0:
                    sp.dma_start(PARAM[:], params).then_inc(p_in, 16)
            sp.dma_start(CONST[:, 0:FIRST_CONSTANTS], constants[:, 0:FIRST_CONSTANTS]).then_inc(c_in, 16)

            def fetch(n, s):
                if not early(n, RAW_SLOTS):
                    sp.wait_ge(w_lo, n - RAW_SLOTS + 1)
                sp.dma_start(W_raw[:, s, :], weights[n]).then_inc(w_in[s], 16)
                if early(n, RAW_SLOTS) and n == RAW_SLOTS - 1:
                    sp.dma_start(CONST[:, FIRST_CONSTANTS:], constants[:, FIRST_CONSTANTS:]).then_inc(c_rest, 16)
                    sp.dma_start(POS_I[:], positions).then_inc(pos_in, 16)

            grouped(sp, N_BLOCKS, fetch, RAW_SLOTS)

        @block.gpsimd
        def _(pool):
            def split(n, s, use):
                r = s % RAW_SLOTS
                pool.wait_ge(w_in[r], 16 * (use + 1))
                if not early(n, W_SLOTS):
                    pool.wait_ge(block_done, n - W_SLOTS + 1)
                pool.tensor_tensor(HOLD[:, 1 + s:2 + s], HOLD[:, 0:1], HOLD[:, 0:1], ALU.add)
                pool.tensor_scalar(W_hi[:, s, :], W_raw[:, r, :], 1.0, 1.0, ALU.mult, ALU.mult).then_inc(w_hi, 1)
                pool.wait_ge(w_hi, n + 1)
                pool.tensor_tensor(W_lo[:, s, :], W_raw[:, r, :], W_hi[:, s, :].bitcast(F32),
                                   ALU.subtract).then_inc(w_lo, 1)

            pool.memset(HOLD[:], 0.0).then_inc(hold_set, 1)
            pool.wait_ge(hold_set, 1)
            uses = W_SLOTS // RAW_SLOTS
            for n in range(W_SLOTS):
                split(n, n, n // RAW_SLOTS)
            with pool.Fori(1, N_BLOCKS // W_SLOTS) as g:
                for s in range(W_SLOTS):
                    split(g * W_SLOTS + s, s, g * uses + s // RAW_SLOTS)
            for n in range(N_BLOCKS // W_SLOTS * W_SLOTS, N_BLOCKS):
                split(n, n % W_SLOTS, n // RAW_SLOTS)

        @block.tensor
        def _(pe):
            def product(phase, hi, lo, ready, ready_at, beside=None, woven=False,
                        between=None):
                ph = PLAN[phase]
                per = max(1, int(ph.per_tile))
                pe.wait_ge(by_act, ph.act_before)
                if ph.dve_before:
                    pe.wait_ge(by_dve, ph.dve_before)

                def weave():
                    for k in range(KD):
                        pe.wait_ge(ready, ready_at + k + 1)
                        w = slice(k * P, k * P + P)
                        for i in range(WOVEN):
                            slot = (ph.first + i) % W_SLOTS
                            if k == 0:
                                pe.wait_ge(w_lo, ph.first + i + 1)
                            pe.matmul(PS[:, i, :], W_hi[:, slot, w], hi[:, k, :], start=k == 0, stop=False)
                            pe.matmul(PS[:, i, :], W_lo[:, slot, w], hi[:, k, :], start=False, stop=False)
                            done = pe.matmul(PS[:, i, :], W_hi[:, slot, w], lo[:, k, :], start=False, stop=k == KD - 1)
                            if k == KD - 1:
                                done.then_inc(block_done, 1)
                        if between and k == 0:
                            between()

                def tile(i, j):
                    if woven and early(i, WOVEN):
                        if i == 0:
                            weave()
                        elif beside:
                            beside(i - 1)
                        return
                    bank = j % ACC
                    if not early(i, ACC):
                        pe.wait_ge(sums_read[ph.reader], ph.before + i - ACC + 1)
                    for b in range(per):
                        slot = (ph.first + j * per + b) % W_SLOTS
                        pe.wait_ge(w_lo, i * per + (ph.first + b + 1))
                        for k in range(KD):
                            kk = b * KD + k
                            if early(i, 1):
                                pe.wait_ge(ready, ready_at + kk + 1)
                            w = slice(k * P, k * P + P)
                            first, last = kk == 0, kk == per * KD - 1
                            pe.matmul(PS[:, bank, :], W_hi[:, slot, w], hi[:, kk, :], start=first, stop=False)
                            pe.matmul(PS[:, bank, :], W_lo[:, slot, w], hi[:, kk, :], start=False, stop=False)
                            done = pe.matmul(PS[:, bank, :], W_hi[:, slot, w], lo[:, kk, :], start=False, stop=last)
                        done.then_inc(block_done, 1)
                    if beside and not early(i, 1):
                        beside(i - 1)

                grouped(pe, ph.tiles, tile, ACC)
                if beside:
                    beside(ph.tiles - 1)

            def beside_bank(i):
                return 4 + i % 2

            def turn_values(phase, at):
                ph = PLAN[phase]

                def turn(i):
                    pe.wait_ge(by_act, ph.before + i + 1)
                    if i >= 2:
                        pe.wait_ge(v_ready, at + i - 1)
                    for t in range(NT):
                        mm = pe.transpose(PS[:, beside_bank(i), t * P:t * P + P], SQ[:, i % 2, t * P:t * P + P],
                                          const("ident"))
                    mm.then_inc(turned, 1)
                return turn

            def angles():
                pe.wait_ge(pos_float, 1)
                pe.matmul(PS[:, 6, :], const("one", row=slice(0, 1)), POS_F[:], start=True, stop=True).then_inc(pos_wide, 1)

            def norm_columns(source, at):
                for t in range(NT):
                    mm = pe.matmul(PS[:, 5, at + t:at + t + 1], source[:, t * P:t * P + P], const("mean", 1), start=True,
                                   stop=True)
                return mm

            def spread_rstd(n):
                pe.wait_ge(diag_ready, NT * (n + 1))
                pe.matmul(PS[:, 6, :], const("one"), RSTD[:], start=True, stop=True).then_inc(rstd_ready, 1)

            def first_norm():
                pe.wait_ge(c_in, 16)
                pe.wait_ge(sq_added, KD)
                norm_columns(SQSUM, NT).then_inc(stats_done, 1)
                spread_rstd(0)

            def head_norm(i):
                if i == 0:
                    pe.wait_ge(c_rest, 16)
                pe.wait_ge(qk_sq, i + 1)
                if i >= 2:
                    pe.wait_ge(qk_sd, i - 1)
                pe.matmul(PS[:, beside_bank(i), :], const("head_mean"), SQ[:, i % 2, :], start=True,
                          stop=True).then_inc(qk_ms, 1)

            def softmax_attention(S, keys, stage, values, mask, log_gates=None):
                PR_, PT_, O_, Q_ = stage

                def turn_outputs(p):
                    pe.wait_ge(S.o_read, p * 2 + 2)
                    for t in range(NT):
                        mm = pe.transpose(PS[:, 2, t * P:t * P + P], O_[:, t, :], const("ident"))
                    mm.then_inc(S.pair_turned, 1)

                def pair(p, k_tile, next_k=None, first=False, last=None):
                    def u(n):
                        return p * 8 + n

                    def scores(pair_, n, k_tile):
                        h, i = n // NT, n % NT
                        first, width = keys(i)
                        bank = 3 + n % 3
                        if i == 0:
                            pe.wait_ge(S.staged, pair_ * 2 + (h + 1))
                        if n >= 3:
                            pe.wait_ge(S.exped, u(n) - 2)
                        pe.matmul(PS[:, bank, 0:width], Q_[:, h, i * P:i * P + P], k_tile[:, first:first + width],
                                  start=True, stop=False)
                        if log_gates is not None:
                            pe.matmul(PS[:, bank, 0:width], ONE_B[:], log_gates(pair_, h)[:, 0:width], start=False,
                                      stop=False)
                        mw = mask.shape[1] if width >= mask.shape[1] else width
                        mm = pe.matmul(PS[:, bank, width - mw:width], IDENT_B[:], mask[:, mask.shape[1] - mw:], start=False,
                                       stop=True)
                        mm.then_inc(S.scored, 1)

                    def transposes(n):
                        first, width = keys(n % NT)
                        pe.wait_ge(S.exped, u(n) + 1)
                        if not early(u(n), 2):
                            pe.wait_ge(S.turned_read, u(n) - 1)
                        for j in range(width // P):
                            mm = pe.transpose(PS[:, 6 + n % 2, j * P:j * P + P], PR_[:, n % 2, j * P:j * P + P],
                                              const("ident"))
                        mm.then_inc(S.turned, 1)

                    def weigh(n):
                        h, i = n // NT, n % NT
                        keys_from, width = keys(i)
                        pe.wait_ge(S.turned_read, u(n) + 1)
                        if i == 0 and not first:
                            pe.wait_ge(S.o_read, p * 2 + (h - 1))
                        for j in range(width // P):
                            mm = pe.matmul(PS[:, h, i * P:i * P + P], PT_[:, n % 2, j * P:j * P + P],
                                           values(p, keys_from // P + j), start=j == 0, stop=(j + 1) * P == width)
                        mm.then_inc(S.weighed, 1)

                    if first:
                        scores(p, 0, k_tile)
                        scores(p, 1, k_tile)
                    for n in range(8):
                        if n + 2 < 8:
                            scores(p, n + 2, k_tile)
                        transposes(n)
                        if n:
                            weigh(n - 1)
                        if n == 3 and not first:
                            turn_outputs(p - 1)
                        if n + 2 >= 8 and next_k is not None:
                            scores(p + 1, n - 6, next_k)
                    if last:
                        last()
                    weigh(7)

                pair.turn_outputs = turn_outputs
                return pair

            def pool_product():
                for c in range(2):
                    pe.wait_ge(pooled, c + 1)
                    at = PARAM_AT["w_pool"][0] + c * P
                    pe.matmul(PS[:, 6 + c, :], PARAM[:, at:at + P], POOLED[:, c, :], start=True,
                              stop=True).then_inc(pool_done, 1)

            def stick_scores(h):
                if h == 1:
                    pe.wait_ge(mix_ready, KD + FOX_HEADS // 2)
                elif h >= 2:
                    pe.wait_ge(sb_att, h - 1)
                for j in range(NT):
                    mm = pe.matmul(packed_scores(h, j), SBK[:, h // 2, j * P:j * P + P], SBQ[:, h, j * P:T],
                                   start=j != 3, stop=True, skip_group_check=True)
                mm.then_inc(sb_scored, 1)

            def stick_breaking():
                def sums(h, tiles=range(NT)):
                    pe.wait_ge(sb_sp, NT * (h + 1))
                    for j in tiles:
                        pe.matmul(packed_scores(h, j), const("minus_later"), packed(SP_T, h % 2, j), start=False, stop=True,
                                  skip_group_check=True)
                        for i in range(j + 1, NT):
                            pe.matmul(packed_scores(h, j, (i - j) * P), const("minus_one"), packed(SP_T, h % 2, i), start=False,
                                      stop=True, skip_group_check=True)
                        mm = pe.matmul(packed_scores(h, j)[:, 0:P], IDENT_B[:], BEFORE_B[:], start=False, stop=True,
                                       skip_group_check=True)
                    if tiles[-1] == NT - 1:
                        mm.then_inc(sb_summed, 1)

                def gate(i):
                    ph = PLAN["late1"]
                    slot = (ph.first + i) % W_SLOTS
                    pe.wait_ge(w_lo, ph.first + i + 1)
                    if i:
                        pe.wait_ge(by_act, ph.before + i)
                    for k in range(KD):
                        w = slice(k * P, k * P + P)
                        pe.matmul(PS[:, 7, :], W_hi[:, slot, w], A_hi[:, k, :], start=k == 0, stop=False)
                        pe.matmul(PS[:, 7, :], W_lo[:, slot, w], A_hi[:, k, :], start=False, stop=False)
                        done = pe.matmul(PS[:, 7, :], W_hi[:, slot, w], A_lo[:, k, :], start=False, stop=k == KD - 1)
                    done.then_inc(block_done, 1)

                def weigh(h):
                    c, half = h // 2, slice(h % 2 * HD, h % 2 * HD + HD)
                    pe.wait_ge(sb_att, h + 1)
                    for j in range(NT):
                        mm = pe.matmul(PS[half, 6 + c, j * P:T], V1[:, j, 4 + c, half], packed(ATT, h % 2, j),
                                       start=j == 0, stop=j == NT - 1, skip_group_check=True)
                    mm.then_inc(sb_weighed, 1)

                pair.turn_outputs(3)
                stick_scores(1)
                sums(0)
                sums(1, range(0, 1))
                weigh(0)
                stick_scores(2)
                sums(1, range(1, NT))
                gate(0)
                weigh(1)
                stick_scores(3)
                sums(2)
                gate(1)
                sums(3, range(0, 1))
                pe.wait_ge(by_act, PLAN["late1"].before + 2)
                weigh(2)
                sums(3, range(1, NT))
                weigh(3)

            def memory_columns():
                pe.wait_ge(v_ready, 14)
                pe.wait_ge(m_rows, 1)
                for t in range(NT):
                    for r in range(2):
                        mm = pe.transpose(PS[:, 6, (t * 2 + r) * M_HEADS:(t * 2 + r + 1) * M_HEADS],
                                          ROWS[:, r * 3, t * P:t * P + P], const("ident", M_HEADS, slice(0, M_HEADS)))
                mm.then_inc(m_cols_turned, 1)

            def spread_maxima(h):
                if h == 1:
                    pe.wait_ge(m_cols, 1)
                if h >= 2:
                    pe.wait_ge(m_dec, h - 1)
                plain = spread_bank(h)
                for bank in (plain, plain + 1):
                    mm = pe.matmul(PS[:, bank, :], const("select", P, slice(0, M_HEADS), h * P), ROWS[:, 2, :],
                                   start=True, stop=True)
                for t in range(NT):
                    mm = pe.matmul(PS[:, plain + 1, t * P:t * P + P], IDENT_B[:], PAST_B[:], start=False,
                                   stop=True, skip_group_check=True)
                mm.then_inc(m_spread, 1)

            def matrix_memory():
                def scores(h):
                    if h:
                        pe.wait_ge(m_w, h)
                    for j in range(NT):
                        mm = pe.matmul(packed_scores(1, j), MQK[:, 2 * h + 1, j * P:j * P + P], MQK[:, 2 * h, j * P:T],
                                       start=j != 3, stop=True, skip_group_check=True)
                    mm.then_inc(m_scored, 1)

                def weigh(h):
                    pe.wait_ge(m_w, h + 1)
                    if h:
                        pe.wait_ge(m_den_read, h)
                    if h >= 2:
                        pe.wait_ge(m_normed, NT * (h - 1))
                    for i in range(NT):
                        for j in range(i + 1):
                            weights = packed(DEC, h, j, (i - j) * P, P)
                            pe.matmul(memory_out(h, i), weights, V2[:, j, h, 0:M_DV], start=j == 0, stop=j == i)
                            mm = pe.matmul(PS[:, 3, i:i + 1], weights, V2[:, j, h, M_DV:M_DV + 1], start=j == 0,
                                           stop=j == i)
                    mm.then_inc(m_weighed, 1)

                scores(0)
                for h in range(M_HEADS):
                    if h + 1 < M_HEADS:
                        scores(h + 1)
                    weigh(h)
                for f in range(NT):
                    turn_memory(f)

            def turn_memory(f):
                h, c = f // 2, f % 2
                pe.wait_ge(m_normed, NT * (3 if f in (3, 4) else h + 1))
                if f == 5:
                    pe.wait_ge(m_den_read, M_HEADS)
                for t in range(NT):
                    mm = pe.transpose(PS[:, TURNED_BANK[f], t * P:t * P + P], H2F[:, h, t, c * P:c * P + P],
                                      const("ident"))
                mm.then_inc(m_turned, 1)

            def layer_stats(n, behind_sums=lambda: None, behind_rstd=lambda: None):
                pe.wait_ge(sum_added, KD * (n + 1))
                pe.matmul(PS[:, 4, :], const("mean"), SUM[:], start=True, stop=True).then_inc(mean_ready, 1)
                norm_columns(SUM, 0)
                pe.wait_ge(sq_added, KD * (n + 2))
                norm_columns(SQSUM, NT).then_inc(stats_done, 1)
                behind_sums()
                spread_rstd(n + 1)
                behind_rstd()

            def from_a(phase, stage, beside=None, woven=False, between=None):
                product(phase, A_hi, A_lo, a_lo, KD * A_STAGE[stage], beside=beside, woven=woven,
                        between=between)

            def project(l, i):
                ph = PLAN[f"proj{l}"]
                n, quarter = ph.first + i // 4, i % 4
                if i == 0:
                    pe.wait_ge(p_lo, l + 1)
                if quarter == 0:
                    pe.wait_ge(w_lo, n + 1)
                if i >= ACC:
                    pe.wait_ge(by_act, ph.before + i - ACC + 1)
                for k in range(2):
                    w = slice((quarter * 2 + k) * P, (quarter * 2 + k + 1) * P)
                    slot = n % W_SLOTS
                    pe.matmul(PS[:, i % ACC, :], W_hi[:, slot, w], P_hi[:, k, :], start=k == 0, stop=False)
                    pe.matmul(PS[:, i % ACC, :], W_lo[:, slot, w], P_hi[:, k, :], start=False, stop=False)
                    mm = pe.matmul(PS[:, i % ACC, :], W_hi[:, slot, w], P_lo[:, k, :], start=False, stop=k == 1)
                mm.then_inc(block_done if quarter == 3 else proj_part, 1)

            def mlp(l):
                for half, letter in enumerate("ab"):
                    from_a(f"up{l}{letter}", f"ln{2 * l}", woven=half == 0)
                    product(f"down{l}{letter}", H_hi, H_lo, h_lo, HALF_FF * (2 * l + half))
                layer_stats(2 * l + 1, lambda: [project(l, i) for i in (0, 1)],
                            lambda: [project(l, i) for i in range(2, KD)])

            def embed(l):
                from_a(f"gate{l}", f"ln{2 * l + 1}", woven=True)

            def rope_swap(i):
                ph = PLAN["rope3"]
                pe.wait_ge(by_act, ph.before + i + 1)
                if i >= 2:
                    pe.wait_ge(roped, i - 1)
                pe.matmul(PS[:, beside_bank(i), :], const("rope"), RAWQ[:, i % 2, :], start=True,
                          stop=True).then_inc(rope_swapped, 1)

            first_norm()
            from_a("qk1", "norm", head_norm, woven=True)
            from_a("gates1", "norm")
            angles()
            from_a("sbpool1", "norm")
            from_a("v1", "norm", turn_values("v1", 0))
            pool_product()
            from_a("silu1", "norm")
            pair = softmax_attention(FOX, fox_keys, (PR, PT, O_T, STAGE_Q),
                                     lambda p, j: V1[:, j, p, :], FOX_MASK_B,
                                     lambda p, h: NEG_C[:, p * 2 + h, :])
            pe.wait_ge(fox_gates_in, 48)
            pe.wait_ge(v_ready, 6)
            pe.wait_ge(by_act, PLAN["late1"].before)
            k = lambda p: QK[:, p + 4, :]
            pair(0, k(0), k(1), first=True)
            with pe.Fori(1, 3) as p:
                pair(p, k(p), k(p + 1))
            pair(3, k(3), last=lambda: stick_scores(0))
            stick_breaking()
            from_a("out1", "mixed1")
            from_a("gates2", "x1")
            from_a("qk2", "x1")
            from_a("v2", "x1", turn_values("v2", 6))
            memory_columns()
            spread_maxima(0)
            spread_maxima(1)
            from_a("o2", "x1", lambda i: [spread_maxima(h) for h in (2, 3)] if i == 0 else None)
            pe.wait_ge(by_act, PLAN["out2"].act_before)
            matrix_memory()
            pe.wait_ge(mix_ready, 2 * KD + WOVEN)
            from_a("out2", "mixed2", woven=True, between=lambda: [turn_memory(f) for f in range(NT, KD)])
            layer_stats(0)
            mlp(0)
            embed(0)
            from_a("rope3", "ple0", rope_swap, woven=True)
            turn_v3 = turn_values("v3", 14)

            def turn_behind_rope(i):
                pe.wait_ge(roped, 10)
                turn_v3(i)

            from_a("v3", "ple0", turn_behind_rope)
            pe.wait_ge(v_ready, 16)
            for g in range(2):
                pair = softmax_attention(SWA, swa_keys, (PR3, PT3, O_T3, STAGE_Q3),
                                         lambda p, j: V3[:, j, g, :], BAND_MASK_B)
                k = QK3[:, g, :]
                if g == 0:
                    pair(0, k, k, first=True)
                with pe.Fori(4 * g + (g == 0), 4 * g + 3) as p:
                    pair(p, k, k)
                pair(4 * g + 3, k, QK3[:, 1, :] if g == 0 else None)
            pair.turn_outputs(7)
            from_a("out3", "mixed3")
            layer_stats(2)
            mlp(1)
            embed(1)

        @block.scalar
        def _(act):
            own = Own(act, act_own)
            held, tables = [0], [8]

            def sums(phase, step):
                ph = PLAN[phase]

                def tile(i, j):
                    act.wait_ge(block_done, (i + 1) * int(ph.per_tile) + ph.first)
                    step(i, PS[:, j % ACC, :], ph.before + i)

                grouped(act, ph.tiles, tile, ACC)

            def split(source, k, stage, ready, at):
                act.wait_ge(ready, at)
                act.activation(A_hi[:, k, :], source, ACT.Copy).then_inc(a_hi, 1)

            def hold():
                at = held[0] = held[0] % 8 + 1
                act.activation(HOLD_ACT[:, at:at + 1], HOLD_ACT[:, 0:1], ACT.Copy)

            def load_table(func):
                at = tables[0] = tables[0] + 1
                act.activation(HOLD_ACT[:, at:at + 1], HOLD_ACT[:, 0:1], func)

            def log_one_plus_exp(dst, src):
                own(act.activation(dst, src, ACT.Abs))
                own.wait()
                own(act.activation(dst, dst, ACT.Exp, scale=-1.0))
                own.wait()
                return act.activation(dst, dst, ACT.Ln, bias=1.0)

            def angles():
                act.wait_ge(angle_ready, 2)
                act.activation(SIN[:], ANG[:], ACT.Sin).then_inc(angle_done, 1)
                act.activation(COS[:], TURN[:], ACT.Sin).then_inc(angle_done, 1)
                act.wait_ge(angle_done, 2)

            def first_norm():
                act.wait_ge(zeroed, 1)
                load_table(ACT.Sqrt)
                for k in range(KD):
                    if k % (KD // X_PARTS) == 0:
                        act.wait_ge(x_in[k // (KD // X_PARTS)], 16)
                    if k >= 2:
                        act.wait_ge(sq_added, k - 1)
                    act.activation(SQ[:, k % 2, :], X[:, k, :], ACT.Square).then_inc(sq_ready, 1)
                act.wait_ge(stats_done, 1)
                act.activation(SMALL[:, 48:52], PS[:, 5, NT:2 * NT], ACT.Sqrt, bias=EPS_COL[:, 0:1]).then_inc(sd_ready, 1)
                for k in range(KD):
                    split(MIX[:, k % 2, :], k, 0, mix_ready, k + 1)

            def fox_gates(i, bank, at):
                act.activation(FF[:, 0, :], bank[0:FOX_HEADS], ACT.Identity, bias=param("b_f", 0, slice(0, FOX_HEADS))).then_inc(by_act, 1)
                act.wait_ge(by_act, at + 1)
                log_one_plus_exp(FF[:, 1, :], FF[:, 0, :]).then_inc(fox_soft, 1)

            def head_sd(i):
                act.wait_ge(qk_ms, i + 1)
                if i >= 2:
                    act.wait_ge(qk_normed, i - 1)
                act.activation(MIX[:, i % 2, :], PS[:, 4 + i % 2, :], ACT.Sqrt, bias=EPS_COL[:, 0:1]).then_inc(qk_sd, 1)

            def fox_qk(i, bank, at):
                act.activation(QK[:, i, :], bank, ACT.Copy).then_inc(by_act, 1)
                act.wait_ge(by_act, at + 1)
                if i >= 2:
                    act.wait_ge(qk_ms, i - 1)
                act.activation(SQ[:, i % 2, :], QK[:, i, :], ACT.Square).then_inc(qk_sq, 1)
                if i:
                    head_sd(i - 1)

            def sb_pool(i, bank, at):
                if i < 2:
                    act.activation(SBQ[0:HD, 2 * i, :], bank[0:HD], ACT.Copy, scale=QK_SCALE)
                    act.activation(SBQ[HD:P, 2 * i + 1, :], bank[HD:P], ACT.Copy, scale=QK_SCALE).then_inc(by_act, 1)
                elif i < 4:
                    act.activation(SBK[:, i - 2, :], bank, ACT.Copy).then_inc(by_act, 1)
                else:
                    act.activation(PX[:, i - 4, PAD:], bank, ACT.Copy).then_inc(by_act, 1)

            def values(at_v, bias=False):
                def step(i, bank, at):
                    if i >= 2:
                        act.wait_ge(turned, at_v + i - 1)
                    if bias:
                        act.activation(SQ[:, i % 2, :], bank, ACT.Identity, bias=param("b_v", i)).then_inc(by_act, 1)
                    else:
                        act.activation(SQ[:, i % 2, :], bank, ACT.Copy).then_inc(by_act, 1)
                return step

            def into(dst, func, bias=None):
                def step(i, bank, at):
                    b = {} if bias is None else {"bias": param(bias, i)}
                    act.activation(dst(i), bank, func, **b).then_inc(by_act, 1)
                return step

            def softmax_attention(S, keys, stage, mixed_at=None, sinks=False):
                PR_, PT_, Q_ = stage

                def place(p, h, query, first=False):
                    if not first:
                        act.wait_ge(S.scored, p * 8 + (4 * h - 4))
                        hold()
                    half = slice(h * HD, h * HD + HD)
                    act.activation(Q_[half, h, :], query[half], ACT.Copy).then_inc(S.staged, 1)

                def mixed(p):
                    act.wait_ge(mix_ready, p + (mixed_at + 1))
                    hold()
                    act.activation(A_hi[:, p, :], MIX[:, 0, :], ACT.Copy).then_inc(a_hi, 1)

                def pair(p, queries, first=False, last=False):
                    def u(n):
                        return p * 8 + n

                    def copy(n):
                        _, width = keys(n % NT)
                        act.wait_ge(S.turned, u(n) + 1)
                        if not early(u(n), 2):
                            act.wait_ge(S.weighed, u(n) - 1)
                        act.activation(PT_[:, n % 2, 0:width], PS[:, 6 + n % 2, 0:width], ACT.Copy).then_inc(S.turned_read, 1)

                    def sink(h):
                        act.wait_ge(S.sink_in, p * 2 + (h + 1))
                        e = SMALL[:, 8 + 4 * h:12 + 4 * h]
                        act.activation(e, e, ACT.Exp).then_inc(S.sinked, 1)

                    for n in range(8):
                        _, width = keys(n % NT)
                        act.wait_ge(S.maxed, u(n) + 1)
                        act.activation(PR_[:, n % 2, 0:width], PS[:, 3 + n % 3, 0:width], ACT.Exp, bias=SMALL[:, n:n + 1],
                                       accum_out=SMALL[:, 16 + n:17 + n]).then_inc(S.exped, 1)
                        if n:
                            copy(n - 1)
                        if n == 4 and sinks:
                            sink(0)
                        if n == 5 and not first and mixed_at is not None:
                            mixed(p - 1)
                        if n == 1 and not first:
                            place(p, 1, queries(p))
                        if n == 3 and not last:
                            place(p + 1, 0, queries(p + 1))
                    copy(7)
                    if sinks:
                        sink(1)

                pair.place, pair.mixed = place, mixed
                return pair

            def stick_breaking():
                def softplus(h):
                    z = packed(ATT, h % 2)
                    own(act.activation(z, z, ACT.Exp, scale=-1.0))
                    own.wait()
                    act.activation(z, z, ACT.Ln, bias=1.0).then_inc(sb_soft, 1)

                def magnitude(h):
                    act.wait_ge(sb_scored, h + 1)
                    if h >= 2:
                        act.wait_ge(sb_weighed, h - 1)
                    own(act.activation(packed(ATT, h % 2), packed_scores(h), ACT.Abs))
                    own.wait()

                def weights(h):
                    act.wait_ge(sb_summed, h + 1)
                    act.activation(packed(ATT, h % 2), packed_scores(h), ACT.Exp).then_inc(sb_att, 1)

                def read_gate(i):
                    ph = PLAN["late1"]
                    act.wait_ge(block_done, ph.first + i + 1)
                    act.activation(G1[:, 6 + i, :], PS[:, 7, :], ACT.Copy).then_inc(by_act, 1)

                for h in (0, 1):
                    magnitude(h)
                    softplus(h)
                weights(0)
                magnitude(2)
                weights(1)
                softplus(2)
                read_gate(0)
                magnitude(3)
                softplus(3)
                read_gate(1)
                weights(2)
                for k in range(6):
                    split(mixed1(k), k, 1, mix_ready, KD + k + 1)
                weights(3)
                act.wait_ge(by_act, PLAN["late1"].before + 2)
                act.activation(G1[:, 6:8, :], G1[:, 6:8, :], ACT.Silu).then_inc(late_gates, 1)
                for k in (6, 7):
                    split(mixed1(k), k, 1, mix_ready, KD + k + 1)

            def memory_gates(i, bank, at):
                act.activation(MG[:, 0, :], bank[0:36], ACT.Identity, bias=param("b_gates", 0, slice(0, 36))).then_inc(by_act, 1)
                act.wait_ge(by_act, at + 1)
                act.activation(MG[:, 1, :], MG[:, 0, :], ACT.Tanh, scale=1.0 / CAP).then_inc(m_tanh, 1)
                act.wait_ge(m_capped, 1)
                fg = slice(32, 32 + M_HEADS)
                log_one_plus_exp(MG[fg, 0, :], MG[fg, 2, :]).then_inc(m_soft, 1)
                act.wait_ge(m_log_f, 1)
                act.activation(ROWS[:, 3, :], MG[fg, 1, :], ACT.Copy).then_inc(m_shifted, 1)

            def memory_columns():
                act.wait_ge(m_cols_turned, 1)
                cols = PS[:, 6, 0:NT * 2 * M_HEADS].rearrange("p (t r h) -> p t r h", t=NT, r=2)
                act.activation(MCOL[:, :, 0, :], cols[:, :, 0, :], ACT.Copy)
                act.activation(MCOL[:, :, 1, :], cols[:, :, 1, :], ACT.Exp, scale=-1.0).then_inc(m_cols, 1)
                act.wait_ge(m_cols, 1)

            def decays():
                for h in range(M_HEADS):
                    act.wait_ge(m_spread, h + 1)
                    plain = spread_bank(h)
                    for j in range(NT):
                        u = MCOL[:, j, 0, h:h + 1]
                        if j + 1 < NT:
                            act.activation(packed(DEC, h, j, P), PS[:, plain, (j + 1) * P:T], ACT.Exp, bias=u)
                        last = act.activation(packed(DEC, h, j, 0, P), PS[:, plain + 1, j * P:j * P + P], ACT.Exp, bias=u)
                    last.then_inc(m_dec, 1)

            def matrix_memory():
                load_table(ACT.Sqrt)
                for h in range(M_HEADS):
                    act.wait_ge(m_var, h + 1)
                    act.activation(SMALL[:, 12 + 4 * h:16 + 4 * h], SMALL[:, 12 + 4 * h:16 + 4 * h], ACT.Sqrt,
                                   bias=EPS_COL[:, 1:2]).then_inc(m_sd, 1)
                for f in range(KD):
                    split(MIX[:, f % 2, :], f, 3, mix_ready, 16 + f + 1)

            def squares(phase, n):
                ph = PLAN[phase]
                load_table(ACT.Sqrt)
                for i in range(KD):
                    act.wait_ge(by_dve, ph.before + i + 1)
                    if i >= 2:
                        act.wait_ge(sq_added, KD * (n + 1) + i - 1)
                    act.activation(SQ[:, i % 2, :], X[:, i, :], ACT.Square).then_inc(sq_ready, 1)

            def layer_norm(n, g, b, stage, between=lambda k: None):
                act.wait_ge(var_ready, n + 1)
                act.activation(SMALL[:, 48:52], SMALL[:, 56:60], ACT.Sqrt, bias=EPS_COL[:, 1:2]).then_inc(sd_ready, 1)
                between(0)
                for k in range(KD):
                    act.wait_ge(normed, KD * n + k + 1)
                    act.activation(X[:, k, :], X[:, k, :], ACT.Identity, scale=param(g, k), bias=param(b, k)).then_inc(x_ready, 1)
                    split(X[:, k, :], k, stage, x_ready, KD * n + k + 1)
                    between(k + 1)

            def mlp(l):
                for half, letter in enumerate("ab"):
                    base = HALF_FF * (2 * l + half)

                    def hidden(i, bank, at):
                        slot = (i if isinstance(i, int) else at_j[0]) % 2
                        if not early(i, 2):
                            act.wait_ge(h_sq, i + (base - 1))
                        act.activation(RELU[:, slot, :], bank, ACT.Relu).then_inc(by_act, 1)
                        act.wait_ge(h_sq, i + (base + 1))
                        hold()
                        act.activation(H_hi[:, i, :], SQR[:, slot, :], ACT.Copy).then_inc(h_hi, 1)

                    ph = PLAN[f"up{l}{letter}"]
                    at_j = [0]

                    def tile(i, j):
                        at_j[0] = j
                        act.wait_ge(block_done, i + (ph.first + 1))
                        hidden(i, PS[:, j, :], None)

                    grouped(act, ph.tiles, tile, ACC)
                act.wait_ge(h_sq, HALF_FF * (2 * l + 2))
                act.dma_start(RELU[:], ple_in[l]).then_inc(ple_got, 16)
                act.wait_ge(h_lo, HALF_FF * (2 * l + 2))
                act.wait_ge(ple_got, 16 * (l + 1))
                act.activation(P_hi[:], RELU[:], ACT.Copy).then_inc(p_hi, 1)
                squares(f"down{l}b", 2 * l + 1)

            def embed(l):
                ph = PLAN[f"proj{l}"]

                def projected(i):
                    if i % 4 == 3:
                        act.wait_ge(block_done, ph.first + i // 4 + 1)
                    else:
                        act.wait_ge(proj_part, 6 * l + i // 4 * 3 + i % 4 + 1)
                    act.activation(PROJ[:, i, :], PS[:, i % ACC, :], ACT.Copy).then_inc(by_act, 1)

                layer_norm(2 * l + 1, f"mlp_g{l}", f"mlp_b{l}", f"ln{2 * l + 1}",
                           lambda k: [projected(i) for i in range(2 * k, min(2 * k + 2, KD))])
                sums(f"gate{l}", into(lambda i: GATE[:, i, :], ACT.Sigmoid, f"ple_b{l}"))
                for i in range(KD):
                    if l == 0:
                        split(X[:, i, :], i, "ple0", embedded, i + 1)
                    else:
                        act.wait_ge(embedded, KD + i + 1)
                        act.dma_start(out[i], X[:, i, :]).then_inc(out_done, 16)

            def rope(i, bank, at):
                if i >= 2:
                    act.wait_ge(roped, i - 1)
                act.activation(RAWQ[:, i % 2, :], bank, ACT.Identity, bias=param("b_rope", i)).then_inc(by_act, 1)

            first_norm()
            sums("qk1", fox_qk)
            head_sd(7)
            sums("gates1", fox_gates)
            act.wait_ge(fox_rows, 3)
            for part in range(3):
                act.dma_start(NEG_C[part:part + 1, :, :], FF_PART[:, part, :]).then_inc(fox_gates_in, 16)
            sums("sbpool1", sb_pool)
            sums("v1", values(0))
            angles()
            sums("silu1", into(lambda i: G1[:, i, :], ACT.Silu))
            pair = softmax_attention(FOX, fox_keys, (PR, PT, STAGE_Q))
            act.wait_ge(qk_normed, 8)
            act.wait_ge(fox_gates_in, 48)
            act.wait_ge(pool_done, 2)
            act.wait_ge(stage_zeroed, 1)
            queries = lambda p: QK[:, p, :]
            for h in range(2):
                pair.place(0, h, queries(0), first=True)
            load_table(ACT.Exp)
            pair(0, queries, first=True)
            with act.Fori(1, 3) as p:
                pair(p, queries)
            pair(3, queries, last=True)
            stick_breaking()
            act.wait_ge(block_done, PLAN["out1"].last)
            for k in range(KD):
                split(X[:, k, :], k, 2, by_dve, PLAN["out1"].before + k + 1)
            sums("gates2", memory_gates)
            sums("qk2", into(lambda i: MQK[:, 2 * i if i < M_HEADS else 2 * (i - M_HEADS) + 1, :], ACT.Copy))
            sums("v2", values(6))
            memory_columns()
            decays()
            sums("o2", into(lambda i: O2[:, i, :], ACT.Sigmoid))
            matrix_memory()
            squares("out2", 0)
            layer_norm(0, "mix_g0", "mix_b0", "ln0")
            mlp(0)
            embed(0)
            sums("rope3", rope)
            act.wait_ge(roped, 10)
            pair = softmax_attention(SWA, swa_keys, (PR3, PT3, STAGE_Q3), 24, True)
            act.wait_ge(stage_zeroed, 2)
            queries = lambda p: QK3[:, p + 2, :]
            for h in range(2):
                pair.place(0, h, queries(0), first=True)
            load_table(ACT.Exp)
            sums("v3", values(14, True))
            pair(0, queries, first=True)
            with act.Fori(1, 7) as p:
                pair(p, queries)
            pair(7, queries, last=True)
            pair.mixed(7)
            squares("out3", 2)
            layer_norm(2, "mix_g1", "mix_b1", "ln2")
            mlp(1)
            embed(1)
            act.wait_ge(out_done, 16 * KD)

        @block.vector
        def _(dve):
            own = Own(dve, dve_own)

            def low_part(k, stage_at, source):
                dve.wait_ge(a_hi, k + (stage_at + 1))
                dve.tensor_tensor(A_lo[:, k, :], source, A_hi[:, k, :].bitcast(F32), ALU.subtract).then_inc(a_lo, 1)

            def prepare():
                dve.memset(MEAN[:], 1.0)
                dve.memset(SQSUM[:], 0.0)
                dve.memset(PX[:, :, 0:PAD], 0.0)
                dve.memset(SBQ[:], 0.0)
                dve.memset(HOLD_ACT[:], 0.0)
                dve.memset(EPS_COL[:, 1:2], LN_EPS)
                dve.memset(EPS_COL[:, 0:1], EPS).then_inc(zeroed, 1)
                dve.wait_ge(zeroed, 1)

            def angles():
                two_pi, magic = 2 * np.pi, 1.5 * 2.0 ** 23
                c1 = 6.28125
                c2 = float(np.floor((two_pi - c1) * 2 ** 21) / 2 ** 21)
                c3 = float(two_pi - c1 - c2)
                dve.wait_ge(pos_wide, 1)
                own(dve.tensor_scalar(ANG[:], PS[:, 6, :], const("inv_freq"), None, ALU.mult))
                own.wait()
                own(dve.tensor_scalar(TURN[:], ANG[:], 1.0 / two_pi, magic, ALU.mult, ALU.add))
                own.wait()
                own(dve.tensor_scalar(TURN[:], TURN[:], magic, None, ALU.subtract))
                own.wait()
                for c in (c1, c2, c3):
                    own(dve.scalar_tensor_tensor(out=ANG[:], in0=TURN[:], scalar=-c, in1=ANG[:], op0=ALU.mult, op1=ALU.add))
                    own.wait()
                top = float(np.nextafter(np.float32(np.pi), np.float32(0)))
                own(dve.tensor_scalar(ANG[:], ANG[:], top, -top, ALU.min, ALU.max))
                own.wait()
                own(dve.tensor_scalar(ROT_TMP[:], ANG[:], float(np.pi / 2), -two_pi, ALU.is_gt, ALU.mult))
                own.wait()
                dve.scalar_tensor_tensor(out=TURN[:], in0=ANG[:], scalar=float(np.pi / 2), in1=ROT_TMP[:], op0=ALU.add,
                                         op1=ALU.add).then_inc(angle_ready, 1)
                dve.wait_ge(angle_ready, 1)
                dve.tensor_scalar(TURN[:], TURN[:], top, -top, ALU.min, ALU.max).then_inc(angle_ready, 1)

            def add_square(i, n_before):
                dve.wait_ge(sq_ready, n_before + i + 1)
                if i:
                    dve.wait_ge(sq_added, n_before + i)
                dve.tensor_tensor(SQSUM[:], SQSUM[:], SQ[:, i % 2, :], ALU.add).then_inc(sq_added, 1)

            def mix_slot(k, stage_at):
                if k >= 2:
                    dve.wait_ge(a_lo, stage_at + k - 1)

            def diagonals(n):
                rstd = SMALL[:, 48:52]
                dve.wait_ge(sd_ready, n + 1)
                own(dve.reciprocal(rstd, rstd))
                own.wait()
                for t in range(NT):
                    dve.tensor_scalar(RSTD[:, t * P:t * P + P], const("ident"), SMALL[:, 48 + t:49 + t], None,
                                      ALU.mult).then_inc(diag_ready, 1)

            def first_norm():
                for k in range(KD):
                    add_square(k, 0)
                dve.wait_ge(p_in, 16)
                own(dve.tensor_scalar(GK[:, 0:1], param("q_norm_g"), QK_SCALE, None, ALU.mult))
                dve.wait_ge(c_in, 16)
                diagonals(0)
                dve.wait_ge(rstd_ready, 1)
                for k in range(KD):
                    mix_slot(k, 0)
                    dve.scalar_tensor_tensor(out=MIX[:, k % 2, :], in0=X[:, k, :], scalar=param("norm_g", k), in1=PS[:, 6, :],
                                             op0=ALU.mult, op1=ALU.mult).then_inc(mix_ready, 1)
                    if k:
                        low_part(k - 1, 0, MIX[:, (k - 1) % 2, :])
                low_part(KD - 1, 0, MIX[:, (KD - 1) % 2, :])

            def running_sum(out, rows_in):
                n = out.shape[0]
                return dve.tensor_tensor_scan(out, MEAN[0:n, :], rows_in, 0.0, ALU.mult, ALU.add)

            def fox_gates():
                dve.wait_ge(fox_soft, 1)
                own(dve.scalar_tensor_tensor(out=FF[:, 2, :], in0=FF[:, 0, :], scalar=0.0, in1=FF[:, 1, :], op0=ALU.min,
                                             op1=ALU.subtract))
                own.wait()
                own(running_sum(FF[:, 1, :], FF[:, 2, :]))
                own.wait()
                own(dve.tensor_scalar(FF[:, 0, :], FF[:, 1, :], -1.0, None, ALU.mult))
                own.wait()
                for part in range(3):
                    dve.tensor_copy(FF_PART[:, part, :], FF[:, 0, :]).then_inc(fox_rows, 1)
                    if part < 2:
                        dve.wait_ge(fox_rows, part + 1)
                        own(dve.tensor_tensor(FF[:, 0, :], FF[:, 0, :], FF_PART[:, part, :], ALU.subtract))
                        own.wait()

            def fox_qk():
                for i in range(8):
                    dve.wait_ge(qk_sd, i + 1)
                    own(dve.reciprocal(MIX[:, i % 2, :], MIX[:, i % 2, :]))
                    own.wait()
                    g = GK[:, 0:1] if i < 4 else param("k_norm_g")
                    dve.scalar_tensor_tensor(out=QK[:, i, :], in0=QK[:, i, :], scalar=g, in1=MIX[:, i % 2, :],
                                             op0=ALU.mult, op1=ALU.mult).then_inc(qk_normed, 1)

            def store_values(at_v, n, dst):
                for i in range(n):
                    dve.wait_ge(turned, at_v + i + 1)
                    dve.tensor_copy(dst(i), PS[:, 4 + i % 2, :].rearrange("p (t f) -> p t f", t=NT)).then_inc(v_ready, 1)

            def softmax_attention(S, keys, O_, a_at, sinks, gate):

                def outputs(p, h):
                    total, e = SMALL[:, 16 + 4 * h:20 + 4 * h], SMALL[:, 8 + 4 * h:12 + 4 * h]
                    dve.wait_ge(S.weighed, p * 8 + (4 * h + 4))
                    if sinks:
                        dve.wait_ge(S.sinked, p * 2 + (h + 1))
                        own(dve.tensor_tensor(total, total, e, ALU.add))
                        own.wait()
                    own(dve.reciprocal(total, total))
                    own.wait()
                    half = slice(h * HD, h * HD + HD)
                    dve.tensor_tensor(O_[:, :, half], PS[:, h, :].rearrange("p (i c) -> p i c", i=NT)[:, :, half],
                                      total.unsqueeze(2).broadcast_to([P, NT, HD]), ALU.mult).then_inc(S.o_read, 1)

                def pair(p, first_pair=False):
                    def u(n):
                        return p * 8 + n

                    for n in range(8):
                        _, width = keys(n % NT)
                        h = n // NT
                        raw, neg_max = SMALL[:, 32 + n % 2:33 + n % 2], SMALL[:, n:n + 1]
                        dve.wait_ge(S.scored, u(n) + 1)
                        dve.tensor_reduce(raw, PS[:, 3 + n % 3, 0:width], mybir.AxisListType.X,
                                          ALU.max).then_inc(S.scores_read, 1)
                        dve.wait_ge(S.scores_read, u(n) + 1)
                        if sinks:
                            dve.tensor_scalar(neg_max, raw, sinks(p, h), -1.0, ALU.max, ALU.mult).then_inc(S.maxed, 1)
                        else:
                            dve.tensor_scalar(neg_max, raw, -1.0, None, ALU.mult).then_inc(S.maxed, 1)
                        if sinks and n % NT == NT - 1:
                            dve.wait_ge(S.maxed, u(n) + 1)
                            dve.tensor_scalar(SMALL[:, 8 + 4 * h:12 + 4 * h], SMALL[:, 4 * h:4 * h + 4], sinks(p, h), None,
                                              ALU.add).then_inc(S.sink_in, 1)
                        if n == 2 and not first_pair:
                            outputs(p - 1, 1)
                        if n == 4 and not first_pair:
                            mix(p - 1)
                        if n == 5:
                            outputs(p, 0)
                        if n == 7 and not first_pair and not gate:
                            low_part(p - 1, a_at, MIX[:, 0, :])

                def mix(p):
                    if not gate:
                        dve.wait_ge(a_lo, p + a_at)
                    dve.wait_ge(S.pair_turned, p + 1)
                    if gate:
                        dve.tensor_tensor(mixed1(p), PS[:, 2, :], gate(p), ALU.mult).then_inc(mix_ready, 1)
                    else:
                        dve.tensor_copy(MIX[:, 0, :], PS[:, 2, :]).then_inc(mix_ready, 1)

                def mixed(p):
                    mix(p)
                    low_part(p, a_at, MIX[:, 0, :])

                pair.outputs, pair.mix, pair.mixed = outputs, mix, mixed
                return pair

            def pool():
                dve.wait_ge(fox_gates_in, 48)
                dve.wait_ge(by_act, PLAN["v1"].act_before)
                own(dve.memset(WIN[:, :, 0:PAD], 0.0))
                for c in range(2):
                    src, dst = PX[:, c, :], 0
                    steps = POOL_WINDOWS[2 * c + 1].bit_length() - 1
                    for s in range(steps):
                        rows = slice(HD, P) if s == steps - 1 else slice(0, P)
                        own.wait()
                        own(dve.tensor_tensor(WIN[rows, dst, PAD:], src[rows, PAD:], src[rows, PAD - 2 ** s:PAD + T - 2 ** s],
                                              ALU.add))
                        src, dst = WIN[:, dst, :], 1 - dst
                    own.wait()
                    wide, narrow = 1 - dst, dst
                    own(dve.tensor_scalar(POOLED[0:HD, c, :], WIN[0:HD, narrow, PAD:],
                                          const("inv_window", 1, slice(0, HD), c), None, ALU.mult))
                    own(dve.tensor_scalar(POOLED[HD:P, c, :], WIN[HD:P, wide, PAD:],
                                          const("inv_window", 1, slice(HD, P), c), None, ALU.mult))
                    own.wait()
                    own(dve.tensor_tensor(POOLED[:, c, 0:PAD], POOLED[:, c, 0:PAD], const("count_fix", PAD, skip=c * PAD),
                                          ALU.mult))
                    own.wait()
                    dve.tensor_tensor(POOLED[:, c, :], POOLED[:, c, :], PX[:, c, PAD:], ALU.subtract).then_inc(pooled, 1)

            def pool_outputs():
                for c in range(2):
                    dve.wait_ge(pool_done, c + 1)
                    own(dve.tensor_scalar(PX[:, c, PAD:], PS[:, 6 + c, :], param("pool_scale", c), None, ALU.mult))

            def stick_breaking():
                def softplus(h):
                    dve.wait_ge(sb_soft, h + 1)
                    if h >= 2:
                        dve.wait_ge(sb_summed, h - 1)
                    dve.scalar_tensor_tensor(out=packed(SP_T, h % 2), in0=packed_scores(h), scalar=0.0, in1=packed(ATT, h % 2),
                                             op0=ALU.max, op1=ALU.add).then_inc(sb_sp1, 1)
                    dve.wait_ge(sb_sp1, h + 1)
                    for j in range(NT):
                        diagonal = packed(SP_T, h % 2, j)[:, 0:P]
                        dve.tensor_tensor(diagonal, diagonal, const("before_mul"), ALU.mult).then_inc(sb_sp, 1)

                def low(k):
                    low_part(k, KD, mixed1(k))

                def mix(c):
                    dve.wait_ge(sb_weighed, 2 * c + 2)
                    dve.wait_ge(late_gates, 1)
                    dve.tensor_tensor(mixed1(6 + c), PS[:, 6 + c, :], G1[:, 6 + c, :], ALU.mult).then_inc(mix_ready, 1)

                softplus(0)
                softplus(1)
                for c in range(2):
                    dve.tensor_tensor(mixed1(4 + c), PX[:, c, PAD:], G1[:, 4 + c, :], ALU.mult).then_inc(mix_ready, 1)
                softplus(2)
                softplus(3)
                for k in range(6):
                    low(k)
                for c in range(2):
                    mix(c)
                    if c:
                        low(6)
                low(7)

            def residual(phase, n=None, scale=None, bias=None):
                ph = PLAN[phase]
                if n is not None:
                    own(dve.memset(SUM[:], 0.0))
                    own(dve.memset(SQSUM[:], 0.0))
                    own.wait()
                for i in range(KD):
                    if bias:
                        own(dve.tensor_scalar(X[:, i, :], X[:, i, :], scale, param(bias, i), ALU.mult, ALU.add))
                        own.wait()
                    dve.wait_ge(block_done, ph.first + (i + 1) * ph.per_tile)
                    if scale and not bias:
                        dve.scalar_tensor_tensor(out=X[:, i, :], in0=X[:, i, :], scalar=scale, in1=PS[:, i % ACC, :],
                                                 op0=ALU.mult, op1=ALU.add).then_inc(by_dve, 1)
                    else:
                        dve.tensor_tensor(X[:, i, :], X[:, i, :], PS[:, i % ACC, :], ALU.add).then_inc(by_dve, 1)
                    if n is not None:
                        dve.wait_ge(by_dve, ph.before + i + 1)
                        if i:
                            dve.wait_ge(sum_added, KD * n + i)
                        dve.tensor_tensor(SUM[:], SUM[:], X[:, i, :], ALU.add).then_inc(sum_added, 1)
                        if i:
                            add_square(i - 1, KD * (n + 1))
                if n is not None:
                    add_square(KD - 1, KD * (n + 1))

            def layer_norm(n, stage_at):
                mean, square, var = SMALL[:, 48:52], SMALL[:, 52:56], SMALL[:, 56:60]

                def centre(k):
                    dve.tensor_tensor(X[:, k, :], X[:, k, :], PS[:, 4, :], ALU.subtract).then_inc(centred, 1)

                dve.wait_ge(stats_done, n + 2)
                own(dve.tensor_copy(mean, PS[:, 5, 0:NT]))
                own.wait()
                own(dve.tensor_tensor(square, mean, mean, ALU.mult))
                own.wait()
                own(dve.tensor_tensor(var, PS[:, 5, NT:2 * NT], square, ALU.subtract))
                own.wait()
                dve.tensor_scalar(var, var, 0.0, None, ALU.max).then_inc(var_ready, 1)
                dve.wait_ge(mean_ready, n + 1)
                centre(0)
                diagonals(n + 1)
                centre(1)
                dve.wait_ge(rstd_ready, n + 2)
                for k in range(KD):
                    dve.wait_ge(centred, KD * n + k + 1)
                    dve.tensor_tensor(X[:, k, :], X[:, k, :], PS[:, 6, :], ALU.mult).then_inc(normed, 1)
                    if k + 2 < KD:
                        centre(k + 2)
                    if k:
                        low_part(k - 1, stage_at, X[:, k - 1, :])
                low_part(KD - 1, stage_at, X[:, KD - 1, :])

            def mlp(l):
                for half, letter in enumerate("ab"):
                    base, ph = HALF_FF * (2 * l + half), PLAN[f"up{l}{letter}"]

                    def tile(i, j):
                        slot = j % 2
                        dve.wait_ge(by_act, i + (ph.before + 1))
                        if not early(i, 2):
                            dve.wait_ge(h_lo, i + (base - 1))
                        dve.tensor_tensor(SQR[:, slot, :], RELU[:, slot, :], RELU[:, slot, :], ALU.mult).then_inc(h_sq, 1)
                        dve.wait_ge(h_hi, i + (base + 1))
                        dve.tensor_tensor(H_lo[:, i, :], SQR[:, slot, :], H_hi[:, i, :].bitcast(F32),
                                          ALU.subtract).then_inc(h_lo, 1)

                    grouped(dve, ph.tiles, tile, ACC)
                    if half == 1:
                        dve.wait_ge(p_hi, l + 1)
                        dve.tensor_tensor(P_lo[:], RELU[:], P_hi[:].bitcast(F32), ALU.subtract).then_inc(p_lo, 1)
                    if half == 0:
                        residual(f"down{l}a", None, ALPHA)
                    else:
                        residual(f"down{l}b", 2 * l + 1)

            def embed(l):
                ph = PLAN[f"gate{l}"]
                for i in range(KD):
                    dve.wait_ge(by_act, ph.before + i + 1)
                    dve.tensor_tensor(GATE[:, i, :], GATE[:, i, :], PROJ[:, i, :], ALU.mult).then_inc(gated, 1)
                    dve.wait_ge(gated, KD * l + i + 1)
                    dve.tensor_tensor(X[:, i, :], X[:, i, :], GATE[:, i, :], ALU.add).then_inc(embedded, 1)
                    if l == 0 and i:
                        low_part(i - 1, KD * A_STAGE["ple0"], X[:, i - 1, :])
                if l == 0:
                    low_part(KD - 1, KD * A_STAGE["ple0"], X[:, KD - 1, :])

            def memory_gates():
                fg = slice(32, 32 + M_HEADS)
                dve.wait_ge(m_tanh, 1)
                dve.tensor_scalar(MG[:, 2, :], MG[:, 1, :], CAP, None, ALU.mult).then_inc(m_capped, 1)
                dve.wait_ge(m_soft, 1)
                dve.scalar_tensor_tensor(out=MG[fg, 1, :], in0=MG[fg, 2, :], scalar=0.0, in1=MG[fg, 0, :], op0=ALU.min,
                                         op1=ALU.subtract).then_inc(m_log_f, 1)
                dve.wait_ge(m_shifted, 1)
                own(running_sum(ROWS[:, 1, :], ROWS[:, 3, :]))
                own.wait()
                own(dve.tensor_tensor(ROWS[:, 0, :], MG[0:M_HEADS, 2, :], ROWS[:, 1, :], ALU.subtract))
                own.wait()
                own(dve.tensor_tensor_scan(ROWS[:, 2, :], ROWS[:, 0, :], ROWS[:, 0, :], 0.0, ALU.max, ALU.max))
                own.wait()
                own(dve.tensor_tensor(ROWS[:, 3, :], ROWS[:, 1, :], ROWS[:, 2, :], ALU.add))
                own(dve.memset(V2[:, :, :, M_DV:M_DV + 1], 1.0))
                dve.tensor_scalar(ROWS[:, 2, :], ROWS[:, 2, :], -1.0, None, ALU.mult).then_inc(m_rows, 1)

            def matrix_memory():
                def weights(h):
                    dve.wait_ge(m_scored, h + 1)
                    dve.wait_ge(m_dec, h + 1)
                    dve.scalar_tensor_tensor(out=packed(DEC, h), in0=packed_scores(1), scalar=float(M_DK ** -0.5),
                                             in1=packed(DEC, h), op0=ALU.mult, op1=ALU.mult).then_inc(m_w, 1)

                def small(name, h, i=None):
                    at = {"sd": 12, "r": 28}[name] + NT * h
                    return SMALL[:, at:at + NT] if i is None else SMALL[:, at + i:at + i + 1]

                den = SMALL[:, 44:48]

                def statistics(h):
                    r, var = small("r", h), small("sd", h)
                    dve.wait_ge(m_weighed, h + 1)
                    dve.tensor_copy(den, PS[:, 3, 0:NT]).then_inc(m_den_read, 1)
                    for i in range(NT):
                        own(dve.bn_stats(STATS[:, h, i, :], memory_out(h, i)))
                    dve.wait_ge(m_den_read, h + 1)
                    own(dve.scalar_tensor_tensor(out=r, in0=den, scalar=-1.0, in1=den, op0=ALU.mult, op1=ALU.max))
                    own.wait()
                    own(dve.tensor_tensor(r, r, MCOL[:, :, 1, h], ALU.max))
                    for i in range(NT):
                        own(dve.bn_aggr(AGGR[:, h, i, :], STATS[:, h, i, :]))
                    own.wait()
                    own(dve.reciprocal(r, r))
                    own.wait()
                    own(dve.tensor_tensor(var, AGGR[:, h, :, 1], r, ALU.mult))
                    own.wait()
                    dve.tensor_tensor(var, var, r, ALU.mult).then_inc(m_var, 1)

                def normed(h):
                    s = small("sd", h)
                    dve.wait_ge(m_sd, h + 1)
                    own(dve.reciprocal(s, s))
                    own.wait()
                    own(dve.tensor_tensor(s, s, small("r", h), ALU.mult))
                    own.wait()
                    for i in range(NT):
                        dve.tensor_scalar(H2F[:, h, i, :], memory_out(h, i), AGGR[:, h, i, 0:1], small("sd", h, i),
                                          ALU.subtract, ALU.mult).then_inc(m_normed, 1)

                def mix(f):
                    dve.wait_ge(m_turned, f + 1)
                    mix_slot(f, 24)
                    dve.scalar_tensor_tensor(out=MIX[:, f % 2, :], in0=PS[:, TURNED_BANK[f], :], scalar=param("head_g", f),
                                             in1=O2[:, f, :], op0=ALU.mult, op1=ALU.mult).then_inc(mix_ready, 1)

                weights(0)
                for h in range(1, M_HEADS):
                    weights(h)
                    statistics(h - 1)
                    normed(h - 1)
                statistics(M_HEADS - 1)
                mix(0)
                mix(1)
                low_part(0, 24, MIX[:, 0, :])
                mix(2)
                normed(M_HEADS - 1)
                low_part(1, 24, MIX[:, 1, :])
                for f in range(3, KD):
                    mix(f)
                    low_part(f - 1, 24, MIX[:, (f - 1) % 2, :])
                low_part(KD - 1, 24, MIX[:, (KD - 1) % 2, :])

            def rope():
                ph = PLAN["rope3"]
                for i in range(10):
                    s = 1.0 if i < 2 else QK_SCALE
                    dve.wait_ge(rope_swapped, i + 1)
                    own(dve.scalar_tensor_tensor(out=QK3[:, i, :], in0=RAWQ[:, i % 2, :], scalar=s, in1=COS[:],
                                                 op0=ALU.mult, op1=ALU.mult))
                    if i:
                        dve.wait_ge(roped, i)
                    own(dve.scalar_tensor_tensor(out=ROT[:], in0=PS[:, 4 + i % 2, :], scalar=s, in1=SIN[:],
                                                 op0=ALU.mult, op1=ALU.mult))
                    own.wait()
                    dve.tensor_tensor(QK3[:, i, :], QK3[:, i, :], ROT[:], ALU.add).then_inc(roped, 1)

            prepare()
            first_norm()
            dve.wait_ge(c_rest, 16)
            dve.wait_ge(pos_in, 16)
            dve.tensor_copy(POS_F[:], POS_I[:]).then_inc(pos_float, 1)
            dve.tensor_copy(IDENT_B[:], const("ident"))
            dve.tensor_copy(FOX_MASK_B[:], const("fox_mask"))
            dve.tensor_copy(BEFORE_B[:], const("before_add"))
            dve.tensor_copy(PAST_B[:], const("past_add"))
            dve.tensor_copy(BAND_MASK_B[:], const("band_mask"))
            dve.tensor_copy(ONE_B[:], const("one", P, slice(0, 3)))
            fox_qk()
            fox_gates()
            angles()
            pool()
            store_values(0, 6, lambda i: V1[:, :, i, :])
            pool_outputs()
            own.wait()
            dve.memset(STAGE_Q[:], 0.0).then_inc(stage_zeroed, 1)
            pair = softmax_attention(FOX, fox_keys, O_T, 8, None, lambda p: G1[:, p, :])
            dve.wait_ge(by_act, PLAN["late1"].before)
            pair(0, True)
            with dve.Fori(1, 4) as p:
                own.enter(p - 1, 2)
                pair(p)
                own.leave(3)
            pair.outputs(3, 1)
            own.wait()
            pair.mix(3)
            stick_breaking()
            residual("out1")
            for k in range(KD):
                low_part(k, KD * A_STAGE["x1"], X[:, k, :])
            memory_gates()
            store_values(6, 8, lambda i: V2[:, :, i // 2, i % 2 * P:i % 2 * P + P])
            matrix_memory()
            residual("out2", 0, ALPHA)
            layer_norm(0, KD * A_STAGE["ln0"])
            mlp(0)
            layer_norm(1, KD * A_STAGE["ln1"])
            embed(0)
            dve.wait_ge(angle_done, 2)
            dve.memset(STAGE_Q3[:], 0.0).then_inc(stage_zeroed, 1)
            rope()
            store_values(14, 2, lambda i: V3[:, :, i, :])

            pair = softmax_attention(SWA, swa_keys, O_T3, KD * A_STAGE["mixed3"], lambda p, h: PARAM[:, sink_at(p, h)],
                                     None)
            pair(0, True)
            with dve.Fori(1, 8) as p:
                own.enter(p - 1, 4)
                pair(p)
                own.leave(7)
            pair.outputs(7, 1)
            pair.mixed(7)
            residual("out3", 2, ALPHA, "b_o")
            layer_norm(2, KD * A_STAGE["ln2"])
            mlp(1)
            layer_norm(3, KD * A_STAGE["ln3"])
            embed(1)


def _blocks(w):
    k, m = w.shape
    if m % P:
        w = np.concatenate([w, np.zeros((k, P - m % P), w.dtype)], 1)
        m = w.shape[1]
    return w.reshape(k // D, KD, P, m // P, P).transpose(3, 0, 2, 1, 4).reshape(-1, P, D)


def _columns(v):
    return np.asarray(v).reshape(-1, P).T


def lay_out(a):
    a = {k: np.asarray(v) for k, v in a.items()}
    wi = a["w_in"][0]
    edges = np.cumsum([0, 512, 512, 512, 512, 8, 256, 256, 256, 256, 256, 256])
    fq, fk, fv, fg, ff, px, pg, sq, sk, sv, sg = (wi[:, s:e] for s, e in zip(edges[:-1], edges[1:]))
    wm = a["a_w_in_2"][0]
    gates2 = np.zeros((D, P), wm.dtype)
    gates2[:, 0:4] = wm[:, 3072:3076]
    gates2[:, 32:36] = wm[:, 3076:3080]
    q_cols = np.concatenate([np.arange(h * HD, h * HD + HD) for h in Q_ORDER])
    stream = [_blocks(w) for w in (fq, fk, ff, sq, sk, px, fv, sv, fg, pg, sg, a["w_out"][0], gates2,
                                   wm[:, 0:3072], a["a_w_out_2"][0])]

    def mlp(l):
        up, down = a["mlp_w_up_2"][l], a["mlp_w_down_2"][l]
        half = D_FF // 2
        for s in (0, half):
            yield _blocks(up[:, s:s + half])
            yield _blocks(down[s:s + half])
        w = a["ple_w_proj_2"][l].reshape(2, P, 2, 4, P)
        yield w.transpose(2, 1, 3, 0, 4).reshape(2, P, D)
        yield _blocks(a["ple_w_gate_2"][l])

    stream += list(mlp(0))
    stream += [_blocks(w) for w in (a["kv_w_2"][:, 0:256], a["b_w_q_2"][0][:, q_cols], a["kv_w_2"][:, 256:512],
                                    a["b_w_o_2"][0][q_cols])]
    stream += list(mlp(1))

    def col(v, at=0):
        c = np.zeros((P, 1), np.float32)
        c[at:at + v.size, 0] = v
        return c

    b_gates = col(a["a_b_igate_2"][0])
    b_gates[32:36, 0] = a["a_b_fgate_2"][0]
    pool = np.zeros((P, 2, P), np.float32)
    for g in range(POOL_GROUPS):
        r = slice(g % 2 * HD, g % 2 * HD + HD)
        pool[r, g // 2, r] = a["w_pool"][0, g]
    sinks = np.broadcast_to(a["b_sinks_2"][0][np.array(Q_ORDER)][None, :], (P, Q_HEADS))
    parts = {
        "norm_g": _columns(a["norm_g"]), "b_f": col(a["b_f"][0]),
        "q_norm_g": np.concatenate([a["q_norm_g"][0]] * 2)[:, None],
        "k_norm_g": np.concatenate([a["k_norm_g"][0]] * 2)[:, None],
        "pool_scale": _columns(a["pool_scale"]), "b_gates": np.concatenate([b_gates, b_gates], 1),
        "head_g": _columns(a["a_head_norm_g_2"]),
        "b_rope": _columns(np.concatenate([a["kv_b_2"][0:256], a["b_b_q_2"][0][q_cols]])),
        "b_v": _columns(a["kv_b_2"][256:512]), "sinks": sinks, "b_o": _columns(a["b_b_o_2"]),
        "w_pool": pool.reshape(P, -1),
    }
    for l in range(2):
        parts[f"mix_g{l}"] = _columns(a["mix_ln_g_2"][l])
        parts[f"mix_b{l}"] = _columns(a["mix_ln_b_2"][l])
        parts[f"mlp_g{l}"] = _columns(a["mlp_ln_g_2"][l])
        parts[f"mlp_b{l}"] = _columns(a["mlp_ln_b_2"][l])
        parts[f"ple_b{l}"] = _columns(a["ple_b_gate_2"][l])
    return {
        "x": np.ascontiguousarray(a["x"][0].T.reshape(KD, P, T).transpose(1, 0, 2)),
        "weights": np.concatenate(stream, 0),
        "constants": CONSTANTS,
        "params": np.ascontiguousarray(np.concatenate([parts[n] for n, _ in PARAM_WIDTHS], 1)),
        "positions": np.ascontiguousarray(a["positions_2"]),
        "ple_in": np.ascontiguousarray(a["p_2"][:, 0].transpose(0, 2, 1).reshape(2, 2, P, T).transpose(0, 2, 1, 3)),
    }


def kernel(**inputs):
    import concourse.bacc as bacc
    from concourse.bass_utils import run_bass_kernel_spmd

    nc = bacc.Bacc("TRN2", target_bir_lowering=False, num_devices=1)
    arrays, aps = {}, []
    for name, a in lay_out(inputs).items():
        arrays[f"in_{name}"] = a
        aps.append(nc.dram_tensor(f"in_{name}", a.shape, mybir.dt.from_np(a.dtype), kind="ExternalInput").ap())
    out = nc.dram_tensor("out", (KD, P, T), F32, kind="ExternalOutput").ap()
    build(nc, *aps, out)
    got = run_bass_kernel_spmd(nc, [arrays], core_ids=[0]).results[0]["out"]
    return np.ascontiguousarray(np.asarray(got).reshape(D, T).T)[None]
```
